# Optimizing a Trainium2 kernel written in Bass

```python
import jax
import jax.numpy as jnp
from jax import lax
import numpy as np
import math

D_MODEL = 1024
BATCH = 1
SEQ = 256
DEPTH = 2

HEAD_DIM = 64
ROT_DIM = HEAD_DIM // 4
ROPE_THETA = 500000.0
NORM_EPS = 1e-6
MIX_WIDTH = D_MODEL

S5_WIDTH = MIX_WIDTH // 2
S5_GROUP = 16
S5_GROUPS = S5_WIDTH // S5_GROUP
S5_STATE = 64
MOBA_WIDTH = MIX_WIDTH - S5_WIDTH
MOBA_HEADS = MOBA_WIDTH // HEAD_DIM
MOBA_BLOCK = 256
MOBA_TOPK = 3
MOBA_QCHUNK = 32
EVEN_SPLITS = (S5_WIDTH, MOBA_WIDTH, MOBA_WIDTH, MOBA_WIDTH)
EVEN_PROJ = sum(EVEN_SPLITS)

RWKV_WIDTH = MIX_WIDTH // 2
RWKV_HEADS = RWKV_WIDTH // HEAD_DIM
RWKV_W_LORA = 64
RWKV_A_LORA = 64
RWKV_G_LORA = 128
RWKV_GN_EPS = 64e-5
RWKV_SPLITS = (RWKV_WIDTH, RWKV_WIDTH, RWKV_WIDTH, RWKV_W_LORA, RWKV_A_LORA, RWKV_G_LORA)
RWKV_PROJ = sum(RWKV_SPLITS)
DSA_WIDTH = MIX_WIDTH - RWKV_WIDTH
DSA_HEADS = DSA_WIDTH // HEAD_DIM
DSA_IDX_HEADS = 4
DSA_IDX_DIM = HEAD_DIM
DSA_TOPK = 256
DSA_QBLOCK = 128
DSA_SPLITS = (DSA_WIDTH, HEAD_DIM, HEAD_DIM, DSA_IDX_HEADS * DSA_IDX_DIM, DSA_IDX_DIM, DSA_IDX_HEADS)
ODD_PROJ = RWKV_PROJ + sum(DSA_SPLITS)

FFN_DENSE = 2816
N_EXPERTS = 8
TOP_K = 2
FFN_EXPERT = 3584
MOE_BLOCK = 256

N_EVEN = (DEPTH + 1) // 2
N_ODD = DEPTH // 2

kernel_name = 'hybrid_s5_moba_rwkv7_dsa_moe'

def split_cols(t, sizes):
    return jnp.split(t, [int(c) for c in np.cumsum(sizes)[:-1]], axis=-1)

def rms_norm(x, g):
    xf = x.astype(jnp.float32)
    y = xf * lax.rsqrt(jnp.mean(xf * xf, axis=-1, keepdims=True) + NORM_EPS)
    return (y * g.astype(jnp.float32)).astype(x.dtype)

def partial_rope(x, pos):
    half = ROT_DIM // 2
    inv_freq = ROPE_THETA ** (-jnp.arange(half, dtype=jnp.float32) / half)
    ang = pos.astype(jnp.float32)[:, None] * inv_freq[None, :]
    cos = jnp.cos(ang)[None, :, None, :]
    sin = jnp.sin(ang)[None, :, None, :]
    x1 = x[..., :half].astype(jnp.float32)
    x2 = x[..., half:ROT_DIM].astype(jnp.float32)
    rot = jnp.concatenate([x1 * cos - x2 * sin, x2 * cos + x1 * sin], axis=-1).astype(x.dtype)
    return jnp.concatenate([rot, x[..., ROT_DIM:]], axis=-1)

def swiglu(x, w_gate, w_up, w_down):
    return (jax.nn.silu(x @ w_gate) * (x @ w_up)) @ w_down

def s5_mixer(u, a_re, a_im, log_dt, b_re, b_im, c_re, c_im, d, glu_w, glu_b):
    f32 = jnp.float32
    Bsz, S, _ = u.shape
    uf = u.astype(f32)
    ug = uf.reshape(Bsz, S, S5_GROUPS, S5_GROUP)
    ar, ai = a_re.astype(f32), a_im.astype(f32)
    dt = jnp.exp(log_dt.astype(f32))[:, None]
    mag = jnp.exp(dt * ar)
    abar_re = mag * jnp.cos(dt * ai)
    abar_im = mag * jnp.sin(dt * ai)
    den = ar * ar + ai * ai
    xr, xi = abar_re - 1.0, abar_im
    f_re = (xr * ar + xi * ai) / den
    f_im = (xi * ar - xr * ai) / den
    br, bi = b_re.astype(f32), b_im.astype(f32)
    bbar_re = f_re[..., None] * br - f_im[..., None] * bi
    bbar_im = f_re[..., None] * bi + f_im[..., None] * br
    bu_re = jnp.einsum('gpc,bsgc->bsgp', bbar_re, ug)
    bu_im = jnp.einsum('gpc,bsgc->bsgp', bbar_im, ug)
    a_re_t = jnp.broadcast_to(abar_re, bu_re.shape)
    a_im_t = jnp.broadcast_to(abar_im, bu_re.shape)

    def combine(e1, e2):
        a1r, a1i, b1r, b1i = e1
        a2r, a2i, b2r, b2i = e2
        return (a1r * a2r - a1i * a2i, a1r * a2i + a1i * a2r,
                a2r * b1r - a2i * b1i + b2r, a2r * b1i + a2i * b1r + b2i)

    _, _, st_re, st_im = lax.associative_scan(combine, (a_re_t, a_im_t, bu_re, bu_im), axis=1)
    y = (jnp.einsum('gcp,bsgp->bsgc', c_re.astype(f32), st_re)
         - jnp.einsum('gcp,bsgp->bsgc', c_im.astype(f32), st_im))
    y = y.reshape(Bsz, S, S5_WIDTH) + d.astype(f32) * uf
    y = jax.nn.gelu(y)
    y = y * jax.nn.sigmoid(y @ glu_w.astype(f32) + glu_b.astype(f32))
    return y.astype(u.dtype)

def moba_attention(q, k, v):
    f32 = jnp.float32
    Bsz, S, H, hd = q.shape
    nb = -(-S // MOBA_BLOCK)
    pad = nb * MOBA_BLOCK - S
    kp = jnp.pad(k, ((0, 0), (0, pad), (0, 0), (0, 0)))
    vp = jnp.pad(v, ((0, 0), (0, pad), (0, 0), (0, 0)))
    kb = kp.reshape(Bsz, nb, MOBA_BLOCK, H, hd).transpose(0, 3, 1, 2, 4)
    vb = vp.reshape(Bsz, nb, MOBA_BLOCK, H, hd).transpose(0, 3, 1, 2, 4)
    qh = q.transpose(0, 2, 1, 3)
    pos = jnp.arange(S, dtype=jnp.int32)
    qblk = pos // MOBA_BLOCK
    own = jnp.broadcast_to(qblk[None, None, :, None], (Bsz, H, S, 1))
    n_sel = min(MOBA_TOPK, nb - 1)
    if n_sel > 0:
        k_mean = jnp.mean(kb.astype(f32), axis=3)
        gate = jnp.einsum('bhsd,bhnd->bhsn', qh.astype(f32), k_mean)
        past = jnp.arange(nb)[None, :] < qblk[:, None]
        gate = jnp.where(past[None, None], gate, -jnp.inf)
        _, top_idx = lax.top_k(gate, n_sel)
        idx = jnp.concatenate([top_idx.astype(jnp.int32), own], axis=-1)
        valid = jnp.concatenate([jnp.arange(n_sel)[None, :] < qblk[:, None],
                                 jnp.ones((S, 1), bool)], axis=-1)
    else:
        idx = own
        valid = jnp.ones((S, 1), bool)
    n_j = idx.shape[-1]
    nc = S // MOBA_QCHUNK
    scale = hd ** -0.5

    def to_chunks(t):
        return jnp.moveaxis(t.reshape(Bsz, H, nc, MOBA_QCHUNK, *t.shape[3:]), 2, 0)

    gather = jax.vmap(jax.vmap(lambda blocks, i: blocks[i]))

    def chunk_attn(args):
        qc, ic, vc, pc = args
        kg = gather(kb, ic)
        vg = gather(vb, ic)
        s = jnp.einsum('bhqd,bhqjkd->bhqjk', qc, kg, preferred_element_type=f32) * scale
        kpos = ic[..., None] * MOBA_BLOCK + jnp.arange(MOBA_BLOCK)
        mask = (kpos <= pc[None, None, :, None, None]) & vc[None, None, :, :, None]
        s = jnp.where(mask, s, -jnp.inf)
        p = jax.nn.softmax(s.reshape(Bsz, H, MOBA_QCHUNK, n_j * MOBA_BLOCK), axis=-1)
        p = p.reshape(s.shape)
        return jnp.einsum('bhqjk,bhqjkd->bhqd', p, vg.astype(f32)).astype(q.dtype)

    out = lax.map(chunk_attn, (to_chunks(qh), to_chunks(idx),
                               valid.reshape(nc, MOBA_QCHUNK, n_j), pos.reshape(nc, MOBA_QCHUNK)))
    out = jnp.moveaxis(out, 0, 2).reshape(Bsz, H, S, hd)
    return out.transpose(0, 2, 1, 3)

def rwkv7_time_mix(p, mu, w0, w_up, a0, a_up, g_up, k_k, k_a, r_k, ln_w, ln_b):
    f32 = jnp.float32
    out_dtype = p.dtype
    Bsz, S, _ = p.shape
    p = p.astype(f32)
    prev = jnp.pad(p, ((0, 0), (1, 0), (0, 0)))[:, :S]
    p = p + (prev - p) * mu.astype(f32)
    r, k, v, wd, ad, gd = split_cols(p, RWKV_SPLITS)
    w_log = -jax.nn.softplus(-(w0.astype(f32) + jnp.tanh(wd) @ w_up.astype(f32))) - 0.5
    decay = jnp.exp(-jnp.exp(w_log))
    a = jax.nn.sigmoid(a0.astype(f32) + ad @ a_up.astype(f32))
    g = jax.nn.sigmoid(gd) @ g_up.astype(f32)

    def heads(t):
        return t.reshape(Bsz, S, RWKV_HEADS, HEAD_DIM)

    kk = heads(k * k_k.astype(f32))
    kk = kk / jnp.maximum(jnp.sqrt(jnp.sum(kk * kk, axis=-1, keepdims=True)), 1e-12)
    k = k * (1.0 + (a - 1.0) * k_a.astype(f32))
    r, decay, k, v, a = heads(r), heads(decay), heads(k), heads(v), heads(a)
    xs = (jnp.moveaxis(r, 1, 0), jnp.moveaxis(decay, 1, 0), jnp.moveaxis(k, 1, 0),
          jnp.moveaxis(v, 1, 0), jnp.moveaxis(-kk, 1, 0), jnp.moveaxis(kk * a, 1, 0))

    def step(state, inp):
        r_t, w_t, k_t, v_t, a_t, b_t = inp
        sa = jnp.einsum('bhvk,bhk->bhv', state, a_t)
        state = (state * w_t[:, :, None, :] + sa[..., None] * b_t[:, :, None, :]
                 + v_t[..., None] * k_t[:, :, None, :])
        return state, jnp.einsum('bhvk,bhk->bhv', state, r_t)

    state0 = jnp.zeros((Bsz, RWKV_HEADS, HEAD_DIM, HEAD_DIM), f32)
    _, y = lax.scan(step, state0, xs)
    y = jnp.moveaxis(y, 0, 1)
    mean = jnp.mean(y, axis=-1, keepdims=True)
    var = jnp.mean(jnp.square(y - mean), axis=-1, keepdims=True)
    y = ((y - mean) * lax.rsqrt(var + RWKV_GN_EPS)).reshape(Bsz, S, RWKV_WIDTH)
    y = y * ln_w.astype(f32) + ln_b.astype(f32)
    bonus = jnp.sum(r * k * r_k.astype(f32), axis=-1, keepdims=True) * v
    return ((y + bonus.reshape(Bsz, S, RWKV_WIDTH)) * g).astype(out_dtype)

def dsa_attention(q, k, v, q_idx, k_idx, w_idx):
    f32 = jnp.float32
    Bsz, S, H, hd = q.shape
    topk = min(DSA_TOPK, S // 4)
    nq = S // DSA_QBLOCK
    scale = hd ** -0.5
    w_scaled = w_idx.astype(f32) * (DSA_IDX_HEADS ** -0.5 * DSA_IDX_DIM ** -0.5)
    pos = jnp.arange(S, dtype=jnp.int32)

    def blocks(t):
        return jnp.moveaxis(t.reshape(Bsz, nq, DSA_QBLOCK, *t.shape[2:]), 1, 0)

    gather = jax.vmap(lambda t, i: t[i])

    def block_attn(args):
        qb, qib, wb, pb = args
        logits = jnp.einsum('bqhd,bsd->bqhs', qib, k_idx, preferred_element_type=f32)
        score = jnp.einsum('bqhs,bqh->bqs', jax.nn.relu(logits), wb)
        causal = pos[None, :] <= pb[:, None]
        score = jnp.where(causal[None], score, -jnp.inf)
        _, sel = lax.top_k(score, topk)
        kg = gather(k, sel)
        vg = gather(v, sel)
        s = jnp.einsum('bqhd,bqkd->bqhk', qb, kg, preferred_element_type=f32) * scale
        ok = (sel <= pb[None, :, None])[:, :, None, :]
        p = jax.nn.softmax(jnp.where(ok, s, -jnp.inf), axis=-1)
        return jnp.einsum('bqhk,bqkd->bqhd', p, vg.astype(f32)).astype(q.dtype)

    out = lax.map(block_attn, (blocks(q), blocks(q_idx), blocks(w_scaled),
                               pos.reshape(nq, DSA_QBLOCK)))
    return jnp.moveaxis(out, 0, 1).reshape(Bsz, S, H * hd)

def moe_swiglu(x, router, w_gate, w_up, w_down):
    f32 = jnp.float32
    Bsz, S, D = x.shape
    T = Bsz * S
    xt = x.reshape(T, D)
    logits = xt.astype(f32) @ router.astype(f32)
    top_val, top_exp = lax.top_k(logits, TOP_K)
    gates = jax.nn.softmax(top_val, axis=-1)
    flat_exp = top_exp.reshape(-1).astype(jnp.int32)
    flat_tok = jnp.repeat(jnp.arange(T, dtype=jnp.int32), TOP_K)
    flat_gate = gates.reshape(-1)
    order = jnp.argsort(flat_exp)
    sorted_exp = flat_exp[order]
    counts = jnp.bincount(flat_exp, length=N_EXPERTS).astype(jnp.int32)
    padded = (counts + MOE_BLOCK - 1) // MOE_BLOCK * MOE_BLOCK
    pad_end = jnp.cumsum(padded)
    pad_start = pad_end - padded
    grp_start = jnp.cumsum(counts) - counts
    rank = jnp.arange(T * TOP_K, dtype=jnp.int32) - grp_start[sorted_exp]
    dest = pad_start[sorted_exp] + rank
    n_blocks = -(-(T * TOP_K + N_EXPERTS * (MOE_BLOCK - 1)) // MOE_BLOCK)
    n_slots = n_blocks * MOE_BLOCK
    slot_tok = jnp.full((n_slots,), T, jnp.int32).at[dest].set(flat_tok[order])
    slot_gate = jnp.zeros((n_slots,), f32).at[dest].set(flat_gate[order])
    block_start = jnp.arange(n_blocks, dtype=jnp.int32) * MOE_BLOCK
    block_exp = jnp.minimum(jnp.searchsorted(pad_end, block_start, side='right'), N_EXPERTS - 1)
    x_pad = jnp.concatenate([xt, jnp.zeros((1, D), xt.dtype)], axis=0)

    def run_block(args):
        tok, e = args
        xb = x_pad[tok]
        return swiglu(xb, w_gate[e], w_up[e], w_down[e])

    yb = lax.map(run_block, (slot_tok.reshape(n_blocks, MOE_BLOCK), block_exp))
    y = jnp.zeros((T + 1, D), f32).at[slot_tok].add(
        yb.reshape(n_slots, D).astype(f32) * slot_gate[:, None])
    return y[:T].reshape(Bsz, S, D).astype(x.dtype)

def even_layer(h, pos, norm_mix, w_in, a_re, a_im, log_dt, b_re, b_im, c_re, c_im, d,
               glu_w, glu_b, w_out, norm_ffn, w_gate, w_up, w_down):
    Bsz, S, _ = h.shape
    proj = rms_norm(h, norm_mix) @ w_in
    u, q, k, v = split_cols(proj, EVEN_SPLITS)
    y_a = s5_mixer(u, a_re, a_im, log_dt, b_re, b_im, c_re, c_im, d, glu_w, glu_b)

    def heads(t):
        return t.reshape(Bsz, S, MOBA_HEADS, HEAD_DIM)

    y_b = moba_attention(partial_rope(heads(q), pos), partial_rope(heads(k), pos), heads(v))
    h = h + jnp.concatenate([y_a, y_b.reshape(Bsz, S, MOBA_WIDTH)], axis=-1) @ w_out
    return h + swiglu(rms_norm(h, norm_ffn), w_gate, w_up, w_down)

def odd_layer(h, pos, norm_mix, w_in, mu, w0, w_up_w, a0, a_up, g_up, k_k, k_a, r_k, ln_w, ln_b,
              w_out, norm_ffn, router, e_gate, e_up, e_down):
    Bsz, S, _ = h.shape
    proj = rms_norm(h, norm_mix) @ w_in
    proj_c, proj_d = jnp.split(proj, [RWKV_PROJ], axis=-1)
    y_c = rwkv7_time_mix(proj_c, mu, w0, w_up_w, a0, a_up, g_up, k_k, k_a, r_k, ln_w, ln_b)
    q, k, v, qi, ki, wi = split_cols(proj_d, DSA_SPLITS)
    q = partial_rope(q.reshape(Bsz, S, DSA_HEADS, HEAD_DIM), pos)
    k = partial_rope(k[:, :, None, :], pos)[:, :, 0]
    qi = partial_rope(qi.reshape(Bsz, S, DSA_IDX_HEADS, DSA_IDX_DIM), pos)
    ki = partial_rope(ki[:, :, None, :], pos)[:, :, 0]
    y_d = dsa_attention(q, k, v, qi, ki, wi)
    h = h + jnp.concatenate([y_c, y_d], axis=-1) @ w_out
    return h + moe_swiglu(rms_norm(h, norm_ffn), router, e_gate, e_up, e_down)

def setup_inputs(seed: int = 0) -> dict:
    key = jax.random.key(seed)
    ks = iter(jax.random.split(key, 48))
    f32 = jnp.float32

    def nrm(shape, scale):
        return scale * jax.random.normal(next(ks), shape, f32)

    D = D_MODEL
    NE, NO = N_EVEN, N_ODD
    n = jnp.arange(S5_STATE, dtype=f32)
    inp = {}
    inp['x'] = nrm((BATCH, SEQ, D), 1.0)
    inp['e_norm_mix'] = 1.0 + nrm((NE, D), 0.02)
    inp['e_w_in'] = nrm((NE, D, EVEN_PROJ), D ** -0.5)
    inp['s5_a_re'] = -0.5 + nrm((NE, S5_GROUPS, S5_STATE), 0.01)
    inp['s5_a_im'] = math.pi * n + nrm((NE, S5_GROUPS, S5_STATE), 0.01)
    inp['s5_log_dt'] = jax.random.uniform(next(ks), (NE, S5_GROUPS), f32,
                                          minval=math.log(1e-3), maxval=math.log(1e-1))
    inp['s5_b_re'] = nrm((NE, S5_GROUPS, S5_STATE, S5_GROUP), (2 * S5_GROUP) ** -0.5)
    inp['s5_b_im'] = nrm((NE, S5_GROUPS, S5_STATE, S5_GROUP), (2 * S5_GROUP) ** -0.5)
    inp['s5_c_re'] = nrm((NE, S5_GROUPS, S5_GROUP, S5_STATE), (2 * S5_STATE) ** -0.5)
    inp['s5_c_im'] = nrm((NE, S5_GROUPS, S5_GROUP, S5_STATE), (2 * S5_STATE) ** -0.5)
    inp['s5_d'] = nrm((NE, S5_WIDTH), 1.0)
    inp['s5_glu_w'] = nrm((NE, S5_WIDTH, S5_WIDTH), S5_WIDTH ** -0.5)
    inp['s5_glu_b'] = nrm((NE, S5_WIDTH), 0.01)
    inp['e_w_out'] = nrm((NE, MIX_WIDTH, D), MIX_WIDTH ** -0.5)
    inp['e_norm_ffn'] = 1.0 + nrm((NE, D), 0.02)
    inp['ffn_w_gate'] = nrm((NE, D, FFN_DENSE), D ** -0.5)
    inp['ffn_w_up'] = nrm((NE, D, FFN_DENSE), D ** -0.5)
    inp['ffn_w_down'] = nrm((NE, FFN_DENSE, D), FFN_DENSE ** -0.5)
    inp['o_norm_mix'] = 1.0 + nrm((NO, D), 0.02)
    inp['o_w_in'] = nrm((NO, D, ODD_PROJ), D ** -0.5)
    inp['rwkv_mu'] = jax.random.uniform(next(ks), (NO, RWKV_PROJ), f32)
    inp['rwkv_w0'] = -2.0 + nrm((NO, RWKV_WIDTH), 1.0)
    inp['rwkv_w_up'] = nrm((NO, RWKV_W_LORA, RWKV_WIDTH), 0.1)
    inp['rwkv_a0'] = nrm((NO, RWKV_WIDTH), 0.5)
    inp['rwkv_a_up'] = nrm((NO, RWKV_A_LORA, RWKV_WIDTH), 0.1)
    inp['rwkv_g_up'] = nrm((NO, RWKV_G_LORA, RWKV_WIDTH), RWKV_G_LORA ** -0.5)
    inp['rwkv_k_k'] = 0.85 + nrm((NO, RWKV_WIDTH), 0.02)
    inp['rwkv_k_a'] = 1.0 + nrm((NO, RWKV_WIDTH), 0.02)
    inp['rwkv_r_k'] = nrm((NO, RWKV_HEADS, HEAD_DIM), 0.1)
    inp['rwkv_ln_w'] = 1.0 + nrm((NO, RWKV_WIDTH), 0.02)
    inp['rwkv_ln_b'] = nrm((NO, RWKV_WIDTH), 0.01)
    inp['o_w_out'] = nrm((NO, MIX_WIDTH, D), MIX_WIDTH ** -0.5)
    inp['o_norm_ffn'] = 1.0 + nrm((NO, D), 0.02)
    inp['moe_router'] = nrm((NO, D, N_EXPERTS), D ** -0.5)
    inp['moe_w_gate'] = nrm((NO, N_EXPERTS, D, FFN_EXPERT), D ** -0.5)
    inp['moe_w_up'] = nrm((NO, N_EXPERTS, D, FFN_EXPERT), D ** -0.5)
    inp['moe_w_down'] = nrm((NO, N_EXPERTS, FFN_EXPERT, D), FFN_EXPERT ** -0.5)
    inp['final_norm'] = 1.0 + nrm((D,), 0.02)
    return inp

def reference(x, e_norm_mix, e_w_in, s5_a_re, s5_a_im, s5_log_dt, s5_b_re, s5_b_im, s5_c_re,
              s5_c_im, s5_d, s5_glu_w, s5_glu_b, e_w_out, e_norm_ffn, ffn_w_gate, ffn_w_up,
              ffn_w_down, o_norm_mix, o_w_in, rwkv_mu, rwkv_w0, rwkv_w_up, rwkv_a0, rwkv_a_up,
              rwkv_g_up, rwkv_k_k, rwkv_k_a, rwkv_r_k, rwkv_ln_w, rwkv_ln_b, o_w_out, o_norm_ffn,
              moe_router, moe_w_gate, moe_w_up, moe_w_down, final_norm):
    pos = jnp.arange(x.shape[1], dtype=jnp.int32)
    h = x
    for layer in range(DEPTH):
        j = layer // 2
        if layer % 2 == 0:
            h = even_layer(h, pos, e_norm_mix[j], e_w_in[j], s5_a_re[j], s5_a_im[j], s5_log_dt[j],
                           s5_b_re[j], s5_b_im[j], s5_c_re[j], s5_c_im[j], s5_d[j], s5_glu_w[j],
                           s5_glu_b[j], e_w_out[j], e_norm_ffn[j], ffn_w_gate[j], ffn_w_up[j],
                           ffn_w_down[j])
        else:
            h = odd_layer(h, pos, o_norm_mix[j], o_w_in[j], rwkv_mu[j], rwkv_w0[j], rwkv_w_up[j],
                          rwkv_a0[j], rwkv_a_up[j], rwkv_g_up[j], rwkv_k_k[j], rwkv_k_a[j],
                          rwkv_r_k[j], rwkv_ln_w[j], rwkv_ln_b[j], o_w_out[j], o_norm_ffn[j],
                          moe_router[j], moe_w_gate[j], moe_w_up[j], moe_w_down[j])
    return rms_norm(h, final_norm)


_drawn_inputs = setup_inputs


def setup_inputs(seed=0):
    import zlib

    import numpy as np

    out = dict(_drawn_inputs(seed))
    spreads = {}
    factors = {'s5_a_re': 64.0,
     's5_glu_b': 15.544,
     'rwkv_k_k': 38.899,
     'rwkv_k_a': 5.074,
     'rwkv_ln_w': 4.235,
     'rwkv_ln_b': 8.0,
     'final_norm': 7.445,
     's5_a_im': 3.055,
     's5_log_dt': 2.736,
     's5_b_re': 3.854,
     's5_b_im': 4.158,
     's5_c_re': 5.068,
     's5_c_im': 3.199,
     'o_norm_ffn': 2.875}
    for name, (base, spread) in spreads.items():
        noise = np.random.default_rng([zlib.crc32(name.encode()), seed]).standard_normal(out[name].shape)
        drawn = base * np.exp(spread * noise) if base else spread * noise
        out[name] = jnp.asarray(drawn.astype(out[name].dtype))
    for name, factor in factors.items():
        out[name] = (out[name] * factor).astype(out[name].dtype)
    return out
```

```python
import math
from contextlib import ExitStack

import numpy as np

import concourse.bass as bass
from concourse import mybir

D, T, P = 1024, 256, 128
KD, NT = D // P, T // P
HD, HEADS = 64, 8
MW = HEADS * HD
KM = MW // P
G5, C5, N5 = 32, 16, 64
FFN, FFE, NE = 2816, 3584, 8
FB = 512
RWKV_COLS = 3 * MW + 64 + 64 + 128
ODD_COLS = RWKV_COLS + MW + HD + HD + 4 * HD + HD + 4
CHUNK = 64
NCH = T // CHUNK
CAP = 128
ITEMS = NE + (2 * T) // (CAP + 1)
TOPK = 64
SLOTS = 7
EPS, GN_EPS = 1e-6, 64e-5
NEG = -1.0e30
ROUND = 12582912.0
DECAY = -math.exp(-0.5)

VECS = [("e_norm_mix", 8), ("e_norm_ffn", 8), ("o_norm_mix", 8), ("o_norm_ffn", 8), ("s5_d", 4),
        ("s5_glu_b", 4), ("rwkv_mu", 14), ("rwkv_w0", 4), ("rwkv_a0", 4), ("rwkv_k_k", 4),
        ("rwkv_k_a", 4), ("rwkv_r_k", 4)]
VOFF = {}
NVEC = 0
for _n, _k in VECS:
    VOFF[_n] = NVEC
    NVEC += _k

LEVELS = [1, 2, 4, 8, 16, 32]


def constants():
    f = np.float32
    i = np.arange(P)
    r, c = i[:, None], i[None, :]
    out = {}
    out["ident"] = (r == c).astype(f)
    def rope_perm(k_of):
        p = np.zeros((P, P), f)
        for m in range(P):
            j = m % HD
            if j < 8:
                p[k_of(m) + 8, m] = -1.0
            elif j < 16:
                p[k_of(m) - 8, m] = 1.0
        return p
    out["perm"] = rope_perm(lambda m: m)
    out["dup"] = (r == c % HD).astype(f)
    out["dup_perm"] = rope_perm(lambda m: m % HD)
    out["ones"] = np.ones((P, P), f)
    out["block_ones"] = (r // HD == c // HD).astype(f)
    out["earlier"] = (r < c).astype(f)
    half = 8
    inv = (np.float32(500000.0) ** (-np.arange(half, dtype=f) / half)).astype(f)
    ang = (np.arange(T, dtype=f)[:, None] * inv[None, :]).astype(f)
    cos, sin = np.ones((P, T), f), np.zeros((P, T), f)
    for m in range(P):
        j = m % HD
        if j < 16:
            cos[m], sin[m] = np.cos(ang[:, j % 8]), np.sin(ang[:, j % 8])
    out["cos"], out["sin"] = cos, sin
    k = np.arange(T)[None, :]
    for t in range(NT):
        out[f"causal{t}"] = np.where(k <= r + t * P, 0.0, NEG).astype(f)
    out["time"] = np.broadcast_to(np.arange(T, dtype=f), (P, T)).copy()
    same = r // CHUNK == c // CHUNK
    for m in LEVELS:
        out[f"level{m}"] = ((r // (2 * m) == c // (2 * m)) & (r // m > c // m)).astype(f)
    out["level1T"] = out["level1"].T.copy()
    out["before"] = ((r < c) & same).astype(f)
    out["upto"] = ((r <= c) & same).astype(f)
    out["restart"] = np.broadcast_to((np.arange(T) % CHUNK != 0).astype(f), (P, T)).copy()
    out["group"] = (r // C5 == np.arange(P // C5)[None, :]).astype(f)
    out["pair"] = (r // HD == np.arange(2)[None, :]).astype(f)
    out["item"] = np.broadcast_to(np.repeat(np.arange(ITEMS, dtype=f), NE), (P, ITEMS * NE)).copy()
    out["first"] = np.broadcast_to(np.eye(ITEMS, NE, dtype=f).reshape(-1), (P, ITEMS * NE)).copy()
    out["expert"] = np.broadcast_to(np.arange(NE, dtype=f), (P, NE)).copy()
    out["restart8"] = np.broadcast_to((np.arange(NT * NE) % NE != 0).astype(f), (P, NT * NE)).copy()
    out["half_sign"] = np.where(r < HD, -1.0, 1.0).astype(f)
    out["eps"] = np.full((P, 1), EPS, f)
    out["gn_eps"] = np.full((P, 1), GN_EPS, f)
    out["half_pi"] = np.full((P, 1), math.pi / 2, f)
    return out


def const_layout():
    off, n = {}, 0
    for name, a in constants().items():
        off[name] = (n, a.shape[1])
        n += a.shape[1]
    return off, n


def block_list():
    out = [("e_w_in", c, FB) for c in range(0, 4 * MW, FB)]
    out += [("s5_glu_w", 0, MW), ("e_w_out", 0, FB), ("e_w_out", FB, FB)]
    ffn = [(c, min(FB, FFN - c)) for c in range(0, FFN, FB)]
    for n, (c, w) in enumerate(ffn):
        out += [("ffn_w_gate", c, w), ("ffn_w_up", c, w)]
        if n:
            out.append(("ffn_w_down", *ffn[n - 1]))
    out.append(("ffn_w_down", *ffn[-1]))
    out += [("o_w_in", c, min(FB, ODD_COLS - c)) for c in range(0, ODD_COLS, FB)]
    out += [("o_w_out", 0, FB), ("o_w_out", FB, FB)]
    return out


def trunk(nc, a, consts_dram, out):
    f32, i32 = mybir.dt.float32, mybir.dt.int32
    ALU, ACT, AX = mybir.AluOpType, mybir.ActivationFunctionType, mybir.AxisListType.X
    ADD, SUB, MUL = ALU.add, ALU.subtract, ALU.mult
    v, act_, pe_ = nc.vector, nc.scalar, nc.tensor
    ctx = ExitStack()

    def sb(name, cols, dt=f32, rows=P):
        return ctx.enter_context(nc.sbuf_tensor(name, [rows, cols], dt))

    sems = {}

    def sem(name):
        if name not in sems:
            sems[name] = ctx.enter_context(nc.semaphore(name))
        return sems[name]

    ring = sb("ring", SLOTS * KD * FB)
    coff, ncon = const_layout()
    con = sb("con", ncon)
    hT = sb("hT", KD * T)[:, :].rearrange("p (k t) -> p k t", k=KD)
    xnT = sb("xnT", KD * T)[:, :].rearrange("p (k t) -> p k t", k=KD)
    yT = sb("yT", KD * T)[:, :].rearrange("p (k t) -> p k t", k=KD)
    pcol = sb("pcol", NVEC)
    ARENA = 14120
    arena = sb("arena", ARENA)
    bank = [ctx.enter_context(nc.psum_tensor(f"bank{i}", [P, 512], f32)) for i in range(8)]

    def C(name):
        o, n = coff[name]
        return con[:, o:o + n]

    def col(name, i):
        return pcol[:, VOFF[name] + i:VOFF[name] + i + 1]

    def carve(base, start, sizes):
        got, at = {}, start
        for name, n in sizes:
            got[name] = base[:, at:at + n]
            at += n
        return got, at

    def slot(n, w=KD * FB):
        return ring[:, (n % SLOTS) * KD * FB:(n % SLOTS) * KD * FB + w]

    L0, end = carve(arena, 0, [("uT", KM * T), ("qT", KM * T), ("kT", KM * T), ("V", NT * MW),
                               ("BT", 8 * P), ("CT", 8 * P), ("s5p", 4 * G5),
                               ("CW", 4 * 8 * (P + C5)), ("um", 4 * T), ("fr", 4 * T), ("pT", 512)])
    assert end <= ARENA, end
    free_slots = 5 * KD * FB
    pre, end = carve(ring, free_slots, [("xtok", NT * D), ("vecs", P), ("Bx", 512), ("Bs", 512),
                                        ("Cx", 512), ("Cs", 512), ("M1", 512), ("M2", 512),
                                        ("mt", 512), ("small", 16 * P)])
    assert end <= SLOTS * KD * FB
    s5w, end = carve(ring, free_slots, [("rn", 2 * T), ("sn", 4 * T), ("cs", 4 * T), ("ta", 2 * T),
                                        ("tb", 2 * T), ("scan", 4 * T), ("oc", 4 * T), ("os", 4 * T)])
    assert end <= SLOTS * KD * FB
    att, _ = carve(xnT.rearrange("p k t -> p (k t)"), 0, [("rope", 1024), ("p", 1024)])
    stat = sb("stat", 64)
    uT, qT, kT = (L0[n].rearrange("p (k t) -> p k t", k=KM) for n in ("uT", "qT", "kT"))
    V0 = L0["V"].rearrange("p (t c) -> p t c", t=NT)
    BT = L0["BT"].rearrange("p (m k c) -> p m k c", m=2, k=4)
    CT = L0["CT"].rearrange("p (m k c) -> p m k c", m=2, k=4)
    s5p = L0["s5p"].rearrange("p (q g) -> p q g", q=4)
    CW = L0["CW"].rearrange("p (b m x) -> p b m x", b=2, m=2)
    um = L0["um"].rearrange("p (b j t) -> p b j t", b=2, j=2)
    frac = L0["fr"].rearrange("p (b j t) -> p b j t", b=2, j=2)
    rn = s5w["rn"].rearrange("p (j t) -> p j t", j=2)
    sn, cs, scan, oc, os_ = (s5w[n].rearrange("p (b j t) -> p b j t", b=2, j=2)
                             for n in ("sn", "cs", "scan", "oc", "os"))
    ta, tb = (s5w[n].rearrange("p (j t) -> p j t", j=2) for n in ("ta", "tb"))
    xtok = pre["xtok"].rearrange("p (t d) -> p t d", t=NT)
    small = [pre["small"][0:G5, P * i:P * i + P] for i in range(16)]

    rstd = sb("rstd", T)
    hc = arena[:, 0:2 * 4 * T].rearrange("p (b j t) -> p b j t", b=2, j=4)
    gate_s = arena[:, 2048:2048 + 4 * T]

    nblocks = block_list()
    NB0 = len(nblocks)
    slot_sem = [sem(f"slot{i}_loaded") for i in range(SLOTS)]
    used_when = [(sem("u_done"), 2)] + [(sem("proj_done"), 2 * n) for n in (1, 2, 3)]
    used_when += [(sem("z_done"), 2), (sem("into_h"), 2), (sem("into_h"), 4)]
    for n in range(7, NB0):
        name, c, w = nblocks[n]
        if name.startswith("ffn"):
            done = {"ffn_w_gate": "ffn_gate", "ffn_w_up": "ffn_up", "ffn_w_down": "ffn_down"}[name]
            last_down = name == "ffn_w_down" and c + w == FFN
            used_when.append((sem("into_h"), 8) if last_down else (sem(done), c // FB + 1))
        elif name == "o_w_in":
            used_when.append((sem("odd_proj"), min(2 * (c // FB) + 2, 11)))
        else:
            used_when.append((sem("into_h"), 10 + 2 * (c // FB)))

    def src_of(name, c, w):
        m = a[name][0]
        if "down" in name:
            return m[c:c + w, :].rearrange("(j p) n -> p j n", p=P)
        return m[:, c:c + w].rearrange("(k p) n -> p k n", p=P)

    def view(n):
        name, c, w = nblocks[n]
        k = src_of(name, c, w).shape[1]
        wid = src_of(name, c, w).shape[2]
        return slot(n, k * wid).rearrange("p (k n) -> p k n", k=k)

    def flat(ap):
        return ap.rearrange("p a b -> p (a b)")
    L1, end = carve(arena, 0, [("shift", 14 * T), ("draw", 8 * T), ("kd", T), ("kid", T), ("Vd", NT * HD),
                               ("wi", NT * 4), ("md", NT * T), ("acc", T), ("work", T), ("relu", 4 * T),
                               ("pT", 512), ("raw", 4 * (T + 1)), ("diff", 2 * T), ("top", 8),
                               ("WA", MW), ("GU", MW), ("lnw", MW), ("lnb", MW), ("rk", KM * T),
                               ("lam", KM * NCH), ("st8", 32)])
    assert end <= ARENA, end
    sc, end = carve(ring, 0, [("lw", KM * T), ("L", KM * T), ("Em", KM * T), ("KK", KM * T), ("A", KM * T),
                              ("AR", 2 * KM * T), ("tmp", KM * T), ("Vt", MW), ("Kt", MW), ("Bt", MW),
                              ("TT", HEADS * P), ("T", HEADS * P), ("G", MW)])
    assert end <= 3 * KD * FB
    sc6, end = carve(ring, 6 * KD * FB, [("Z", HEADS * P), ("U", MW), ("S", MW), ("ya", MW), ("yb", MW),
                                         ("ds", MW)])
    assert end <= 7 * KD * FB
    sc.update(sc6)
    shf = L1["shift"].rearrange("p (k t) -> p k t", k=14)
    draw = L1["draw"].rearrange("p (k t) -> p k t", k=8)
    raw = L1["raw"].rearrange("p (b k t) -> p b k t", b=2, k=2)
    Vd = L1["Vd"].rearrange("p (t c) -> p t c", t=NT)
    wi = L1["wi"].rearrange("p (t c) -> p t c", t=NT)
    md = L1["md"].rearrange("p (t c) -> p t c", t=NT)
    relu = L1["relu"].rearrange("p (h c) -> p h c", h=4)
    st8 = L1["st8"].rearrange("p (a h) -> p a h", a=4)
    lw, Lc, Em, KK, Ag, tmp4, rk = (x.rearrange("p (k t) -> p k t", k=KM) for x in (
        sc["lw"], sc["L"], sc["Em"], sc["KK"], sc["A"], sc["tmp"], L1["rk"]))
    AR = sc["AR"].rearrange("p (k m t) -> p k m t", k=KM, m=2)
    lam = L1["lam"].rearrange("p (k c) -> p k c", k=KM)
    MB = ring[:, 0:HEADS * 2 * P].rearrange("p (h m n) -> p h m n", h=HEADS, m=2)
    MK = ring[:, HEADS * 2 * P:2 * HEADS * 2 * P].rearrange("p (h m n) -> p h m n", h=HEADS, m=2)
    TT, Tm, Zm = (sc[n].rearrange("p (h n) -> p h n", h=HEADS) for n in ("TT", "T", "Z"))
    Sbd = sc["S"].rearrange("p (k n) -> p k n", k=KM)

    MO, end = carve(arena, 0, [("xtok", NT * D), ("htok", NT * D), ("XgT", KD * CAP), ("onehot", NT * CAP),
                               ("gated", NT * CAP), ("gatedT", T), ("silu", FB), ("H", 2 * FB),
                               ("HT", 2 * FB), ("Y", D), ("gfin", D), ("router", KD * NE),
                               ("lg", NT * NE), ("e1", NT * NE), ("e2", NT * NE), ("t16", NT * NE),
                               ("sel", NT * NE), ("gate", NT * NE), ("rank", NT * NE), ("m12", 16),
                               ("cnt", 4 * NE), ("oh", ITEMS * NE), ("ohx", ITEMS * NE),
                               ("off", ITEMS * NE), ("offi", ITEMS), ("slotp", NT * ITEMS), ("gatep", NT * ITEMS), ("ef", ITEMS + 1)])
    assert end <= ARENA, end
    work_list = sb("work_list", ITEMS + 1, i32)
    mtok = MO["xtok"].rearrange("p (t d) -> p t d", t=NT)
    htok = MO["htok"].rearrange("p (t d) -> p t d", t=NT)
    XgT = MO["XgT"].rearrange("p (k s) -> p k s", k=KD)
    onehot = MO["onehot"].rearrange("p (t s) -> p t s", t=NT)
    gated = MO["gated"].rearrange("p (t s) -> p t s", t=NT)
    Hs = MO["H"].rearrange("p (b n) -> p b n", b=2)
    HT = MO["HT"].rearrange("p (b j s) -> p b j s", b=2, j=4)
    router = MO["router"].rearrange("p (k e) -> p k e", k=KD)
    lg, e1, e2, t16, sel, gate, rank = (MO[n].rearrange("p (t e) -> p t e", t=NT) for n in (
        "lg", "e1", "e2", "t16", "sel", "gate", "rank"))
    slotp, gatep = (MO[n].rearrange("p (t i) -> p t i", t=NT) for n in ("slotp", "gatep"))
    NFC = FFE // FB
    expert_blocks = []
    for c_ in range(NFC):
        expert_blocks += [("moe_w_gate", c_), ("moe_w_up", c_)]
        if c_:
            expert_blocks.append(("moe_w_down", c_ - 1))
    expert_blocks.append(("moe_w_down", NFC - 1))
    NEB = len(expert_blocks)
    assert NEB % SLOTS == 0
    GATE_UP_DOWN = {"moe_w_gate": "moe_gate", "moe_w_up": "moe_up", "moe_w_down": "moe_down"}

    NB5 = G5 // 2
    fillers = [("proj", i) for i in range(6)] + [("rope", i) for i in range(4)] \
        + [("attn", u) for u in range(KM * NT + 2)]
    plan = []
    for b in range(NB5 + 1):
        plan.append(("s5", b))
        lo, hi = b * len(fillers) // NB5, min((b + 1) * len(fillers) // NB5, len(fillers))
        plan += fillers[lo:hi]
    UNITS = KM * NT
    SCALE = HD ** -0.5
    TWO_PI = 6.283185

    block = ctx.enter_context(nc.Block())

    @block.sync
    def _(sp):
        sp.dma_start(xtok, a["x"][0].rearrange("(t p) d -> p t d", p=P)).then_inc(sem("x_loaded"), 16)
        sp.dma_start(con[:, :], consts_dram).then_inc(sem("consts_loaded"), 16)
        for n, (name, c, w) in enumerate(nblocks):
            if n == 1:
                sp.wait_ge(sem("vecs_loaded"), 16 * len(VECS))
                sp.wait_ge(sem("s5_loaded"), 16 * 13)
            if n in (5, 6):
                sp.wait_ge(sem("s5_out"), NB5)
                sp.wait_ge(sem("y_used"), NB5)
            if n >= SLOTS:
                sp.wait_ge(*used_when[n - SLOTS])
            sp.dma_start(view(n), src_of(name, c, w)).then_inc(slot_sem[n % SLOTS], 16)
        def load_expert(it, e):
            for j, (name, c) in enumerate(expert_blocks):
                s = (NB0 + j) % SLOTS
                before, cb = expert_blocks[(j - SLOTS) % NEB]
                if j < SLOTS:
                    if s in (0, 1, 2, 6):
                        sp.wait_ge(sem("yc_copied"), NT)
                        sp.wait_ge(sem("bonus_used"), NT)
                    sp.wait_ge(*used_when[NB0 + j - SLOTS])
                    sp.wait_ge(sem(GATE_UP_DOWN[before]), NFC * it + cb + 1)
                else:
                    sp.wait_ge(sem(GATE_UP_DOWN[before]), NFC * it + NFC + cb + 1)
                m = a[name][0]
                if name == "moe_w_down":
                    src = m[bass.ds(e, 1), c * FB:c * FB + FB, :].rearrange("o (j p) n -> p (o j) n", p=P)
                else:
                    src = m[bass.ds(e, 1), :, c * FB:c * FB + FB].rearrange("o (k p) n -> p (o k) n", p=P)
                k = src.shape[1]
                sp.dma_start(slot(s).rearrange("p (k n) -> p k n", k=k), src).then_inc(slot_sem[s], 16)

        with sp.Fori(0, NE) as it:
            load_expert(it, it)
        sp.wait_ge(sem("work_ready"), 1)
        n_items = sp.value_load(work_list[0:1, ITEMS:ITEMS + 1], min_val=NE, max_val=ITEMS)
        with sp.If(n_items > NE):
            with sp.Fori(NE, n_items) as it:
                load_expert(it, sp.value_load(work_list[0:1, bass.ds(it, 1)], min_val=0, max_val=NE - 1))
        sp.wait_ge(sem("y_final"), NT)
        sp.dma_start(out[0].rearrange("(t p) d -> p t d", p=P), htok).then_inc(sem("out_stored"), 16)
        sp.wait_ge(sem("out_stored"), 16)

    @block.gpsimd
    def _(pool):
        pl = nc.gpsimd
        pl.memset(L0["CW"], 0.0).then_inc(sem("cw_zero"), 1)
        pool.wait_ge(sem("consts_loaded"), 16)
        pool.wait_ge(sem("u_copied"), 2)
        for b in range(NB5):
            if b >= 2:
                pool.wait_ge(sem("ab_done"), b - 1)
            for j in range(2):
                g = 2 * b + j
                last = pl.tensor_scalar(um[:, b % 2, j, :], uT[:, g // 8, :],
                                        C("group")[:, g % 8:g % 8 + 1], 1.0, MUL, MUL)
            last.then_inc(sem("um_ready"), 1)

    @block.scalar
    def _(act):
        nv = 0
        for name, k in VECS:
            m = a[name][0]
            if len(m.shape) == 2:
                m = m.rearrange("h d -> (h d)")
            act.dma_start(pre["vecs"][nv:nv + k, :], m.rearrange("(n p) -> n p", p=P)).then_inc(
                sem("vecs_loaded"), 16)
            nv += k
        s5_in = sem("s5_loaded")
        for i, name in enumerate(["s5_a_re", "s5_a_im"]):
            for half in range(2):
                act.dma_start(small[i][:, N5 * half:N5 * half + N5], a[name][0]).then_inc(s5_in, 16)
        act.dma_start(small[2][:, 0:1], a["s5_log_dt"][0].rearrange("(g o) -> g o", o=1)).then_inc(s5_in, 16)
        for half, (nx, ns) in enumerate([("s5_b_re", "s5_b_im"), ("s5_b_im", "s5_b_re")]):
            rows = slice(N5 * half, N5 * half + N5)
            for dst, name in ((pre["Bx"], nx), (pre["Bs"], ns)):
                act.dma_start(dst[rows, :].rearrange("p (g c) -> p g c", c=C5),
                              a[name][0].rearrange("g p c -> p g c")).then_inc(s5_in, 16)
        for half, (nx, ns) in enumerate([("s5_c_re", "s5_c_im"), ("s5_c_im", "s5_c_re")]):
            for dst, name in ((pre["Cx"], nx), (pre["Cs"], ns)):
                act.dma_start(dst.rearrange("p (k n) -> p k n", k=4)[:, :, N5 * half:N5 * half + N5],
                              a[name][0].rearrange("(k g) c p -> (g c) k p", k=4)).then_inc(s5_in, 16)

        chain = [0]

        def link(ins):
            chain[0] += 1
            ins.then_inc(sem("act_chain"), 1)
            act.wait_ge(sem("act_chain"), chain[0])

        for i in range(2):
            act.wait_ge(sem("x_T"), 3 + i)
            act_.activation(flat(hT[:, 4 + 2 * i:6 + 2 * i, :]), bank[3 + i][:, :], ACT.Copy).then_inc(
                sem("x_copied_act"), 1)

        def norm(n, h_ready):
            h_ready()
            act_.activation(flat(yT), flat(hT), ACT.Square).then_inc(sem("sq_done"), 1)
            act.wait_ge(sem("ss_done"), n + 1)
            act_.activation(rstd[:, :], bank[5][:, 0:T], ACT.Sqrt, scale=1.0 / D, bias=C("eps")).then_inc(
                sem("rms_done"), 1)

        def h0():
            act.wait_ge(sem("x_copied_act"), 2)
            act.wait_ge(sem("x_copied"), 2)
        norm(0, h0)
        for i in range(2):
            act.wait_ge(sem("u_done"), i + 1)
            act_.activation(flat(uT[:, 2 * i:2 * i + 2, :]), bank[i][:, :], ACT.Copy).then_inc(
                sem("u_copied"), 1)
        act.wait_ge(sem("s5_angle"), 1)
        act_.activation(small[6], small[5], ACT.Sin, scale=TWO_PI)
        act_.activation(small[7], small[5], ACT.Sin, scale=TWO_PI / 2).then_inc(sem("s5_sin"), 1)

        def tables(b):
            act.wait_ge(sem("frac_ready"), b + 1)
            if b >= 2:
                act.wait_ge(sem("s5_out"), b - 1)
            act_.activation(flat(sn[:, b % 2]), flat(frac[:, b % 2]), ACT.Sin, scale=TWO_PI)
            link(act_.activation(flat(frac[:, b % 2]), flat(frac[:, b % 2]), ACT.Abs))
            act_.activation(flat(cs[:, b % 2]), flat(frac[:, b % 2]), ACT.Sin, scale=-TWO_PI,
                            bias=C("half_pi")).then_inc(sem("table_ready"), 1)

        def attention(u, base, p, pT, o_dst):
            if u >= 2:
                act.wait_ge(sem("pv_done"), base + u - 1)
                act_.activation(o_dst(u - 2), bank[7][:, 0:P], ACT.Copy).then_inc(sem("o_copied"), 1)
            if u < UNITS:
                nk = P * (u % NT + 1)
                act.wait_ge(sem("nb_ready"), base + u + 1)
                for j in range(2):
                    s = 2 * (u % 2) + j
                    last = act_.activation(p[:, u % 2, j, 0:nk], p[:, u % 2, j, 0:nk], ACT.Exp, scale=SCALE,
                                           bias=stat[:, 8 + s:9 + s], accum_out=stat[:, 16 + s:17 + s])
                last.then_inc(sem("exp_done"), 1)
            if 1 <= u <= UNITS:
                act.wait_ge(sem("pt_done"), base + u)
                n = 2 * P * ((u - 1) % NT + 1)
                act_.activation(pT[:, 0:n], bank[7][:, 0:n], ACT.Copy).then_inc(sem("pt_copied"), 1)

        p0 = att["p"].rearrange("p (b j n) -> p b j n", b=2, j=2)
        tables(0)
        for what, i in plan:
            if what == "s5" and i + 1 < NB5:
                tables(i + 1)
            elif what == "proj":
                act.wait_ge(sem("proj_done"), i + 1)
                dst = [flat(qT[:, 0:2]), flat(qT[:, 2:4]), flat(kT[:, 0:2]), flat(kT[:, 2:4]),
                       V0[:, 0, :], V0[:, 1, :]][i]
                act_.activation(dst, bank[5 + i % 3][:, :], ACT.Copy).then_inc(sem("proj_copied"), 1)
            elif what == "attn":
                attention(i, 0, p0, L0["pT"], lambda w: yT[:, KM + w // NT, w % NT * P:w % NT * P + P])
        act.wait_ge(sem("y_added"), 4)
        act_.activation(flat(yT[:, 0:KM]), flat(yT[:, 0:KM]), ACT.Gelu_apprx_tanh).then_inc(sem("gelu_done"), 1)
        for m in range(KM):
            if m % 2 == 0:
                act.wait_ge(sem("z_done"), m // 2 + 1)
            last = act_.activation(L0["um"][:, T * m:T * m + T], bank[m // 2][:, (m % 2) * T:(m % 2) * T + T],
                                   ACT.Sigmoid, bias=col("s5_glu_b", m))
        last.then_inc(sem("glu_gate"), 1)
        norm(1, lambda: act.wait_ge(sem("h_added"), 4))
        nf = len(range(0, FFN, FB))
        for c in range(nf):
            w = min(FB, FFN - c * FB) // P
            act.wait_ge(sem("ffn_gate"), c + 1)
            if c:
                act.wait_ge(sem("hc_done"), c)
            for i in range(w // 2):
                last = act_.activation(gate_s[:, 512 * i:512 * i + 512], bank[i][:, :], ACT.Silu)
            last.then_inc(sem("silu_done"), 1)

        for dst, name in ((L1["WA"][0:64, :], "rwkv_w_up"), (L1["WA"][64:128, :], "rwkv_a_up"),
                          (L1["GU"], "rwkv_g_up")):
            act.dma_start(dst, a[name][0]).then_inc(sem("lora_loaded"), 16)
        for dst, name in ((L1["lnw"], "rwkv_ln_w"), (L1["lnb"], "rwkv_ln_b")):
            act.dma_start(dst, a[name][0:1, :].to_broadcast([P, MW])).then_inc(sem("lora_loaded"), 16)
        norm(2, lambda: act.wait_ge(sem("h_added"), 8))
        for i in range(11):
            act.wait_ge(sem("odd_proj"), i + 1)
            b = bank[i % 8]
            if i < 7:
                if i >= 2:
                    act.wait_ge(sem("shifted"), i - 1)
                else:
                    act.wait_ge(sem("raw_zero"), 1)
                ins = act_.activation(raw[:, i % 2, :, 1:T + 1], b[:, :].rearrange("p (k t) -> p k t", k=2), ACT.Copy)
            elif i < 10:
                ins = act_.activation(flat(draw[:, 2 * i - 14:2 * i - 12, :]), b[:, :], ACT.Copy)
            else:
                act_.activation(draw[:, 6, :], b[:, 0:T], ACT.Copy)
                ins = act_.activation(draw[0:HD + 4, 7, :], b[0:HD + 4, T:2 * T], ACT.Copy)
            ins.then_inc(sem("odd_copied"), 1)
        act.wait_ge(sem("shifted"), 7)
        act_.activation(shf[0:64, 12, :], shf[0:64, 12, :], ACT.Tanh).then_inc(sem("lora_in"), 1)
        act_.activation(shf[:, 13, :], shf[:, 13, :], ACT.Sigmoid).then_inc(sem("lora_in"), 1)
        for t in range(NT):
            act.wait_ge(sem("kv_T"), t + 1)
            act_.activation(Vd[:, t, :], bank[2 + t][:, HD:2 * HD], ACT.Copy)
            act_.activation(wi[:, t, :], bank[2 + t][:, P + HD:P + HD + 4], ACT.Copy,
                            scale=4 ** -0.5 * HD ** -0.5).then_inc(sem("kv_copied"), 1)
        for t in range(NT):
            nk = P * (t + 1)
            act.wait_ge(sem("idx_done"), t + 1)
            if t:
                act.wait_ge(sem("acc_done"), t)
            for j in range(2):
                last = act_.activation(relu[:, j::2, 0:nk], bank[4 + j][:, :].rearrange(
                    "p (h n) -> p h n", h=2)[:, :, 0:nk], ACT.Relu)
            last.then_inc(sem("relu_done"), 1)
        for u in range(UNITS + 2):
            attention(u, UNITS, p0, L1["pT"], lambda w: yT[:, KM + w // NT, w % NT * P:w % NT * P + P])
        act.wait_ge(sem("lora_done"), 1)
        for k in range(KM):
            act_.activation(lw[:, k, :], bank[k // 2][:, (k % 2) * T:(k % 2) * T + T], ACT.Sigmoid,
                            bias=col("rwkv_w0", k))
            last = act_.activation(Ag[:, k, :], bank[2 + k // 2][:, (k % 2) * T:(k % 2) * T + T], ACT.Sigmoid,
                                   bias=col("rwkv_a0", k))
        last.then_inc(sem("gates_done"), 1)
        act.wait_ge(sem("kk_raw"), 1)
        act_.activation(flat(tmp4), flat(KK), ACT.Square).then_inc(sem("kk_sq"), 1)
        act.wait_ge(sem("kk_ss"), 1)
        for i in range(2):
            last = act_.activation(sc["tmp"][:, 512 * i:512 * i + 512], bank[4 + i][:, :], ACT.Sqrt)
        last.then_inc(sem("kk_norm"), 1)
        act.wait_ge(sem("L_done"), 1)
        act_.activation(flat(Em), flat(Lc), ACT.Exp, scale=-DECAY)
        act_.activation(flat(Lc), flat(Lc), ACT.Exp, scale=DECAY)
        act_.activation(flat(lw), flat(lw), ACT.Exp, scale=DECAY).then_inc(sem("exps_done"), 1)
        for t in range(NT):
            act.wait_ge(sem("tok_T"), t + 1)
            if t:
                act.wait_ge(sem("bonus_used"), t)
            for i, n in enumerate(("Vt", "Kt", "Bt")):
                last = act_.activation(sc[n], bank[i][:, :], ACT.Copy)
            last.then_inc(sem("tok_copied"), 1)
            for ci in range(2):
                c, R = 2 * t + ci, slice(CHUNK * ci, CHUNK * ci + CHUNK)
                act.wait_ge(sem("G_done"), c + 1)
                act_.activation(sc["G"][R, :], bank[6][R, :], ACT.Copy).then_inc(sem("G_copied"), 1)
                act.wait_ge(sem("U_done"), c + 1)
                act_.activation(sc["U"][R, :], bank[7][R, :], ACT.Copy).then_inc(sem("U_copied"), 1)
            act.wait_ge(sem("gn_var"), t + 1)
            act_.activation(st8[:, 2, :], st8[:, 1, :], ACT.Sqrt, scale=1.0 / HD, bias=C("gn_eps")).then_inc(
                sem("gn_std"), 1)
            act.wait_ge(sem("yc_T"), t + 1)
            act_.activation(yT[:, 0:KM, t * P:t * P + P], bank[2][:, :].rearrange("p (k n) -> p k n", k=KM),
                            ACT.Copy).then_inc(sem("yc_copied"), 1)

        act.dma_start(router, a["moe_router"][0].rearrange("(k p) e -> p k e", p=P)).then_inc(
            sem("router_loaded"), 16)
        act.dma_start(MO["gfin"], a["final_norm"].rearrange("(o d) -> o d", o=1).to_broadcast([P, D])).then_inc(
            sem("gfin_loaded"), 16)
        norm(3, lambda: act.wait_ge(sem("h_added"), 12))
        act.wait_ge(sem("m12_done"), 1)
        act_.activation(MO["m12"][:, 4:6], MO["m12"][:, 2:4], ACT.Exp).then_inc(sem("m12_exp"), 1)
        for t in range(NT):
            for i in range(2):
                act.wait_ge(sem("xtok_T"), 2 * t + i + 1)
                act_.activation(mtok[:, t, 512 * i:512 * i + 512], bank[i][:, :], ACT.Copy).then_inc(
                    sem("xtok_copied"), 1)
        act.wait_ge(sem("work_ready"), 1)
        n_items = act.value_load(work_list[0:1, ITEMS:ITEMS + 1], min_val=NE, max_val=ITEMS)
        with act.Fori(0, n_items) as it:
            act.wait_ge(sem("gather_done"), it + 1)
            for i in range(2):
                last = act_.activation(MO["XgT"][:, 512 * i:512 * i + 512], bank[6 + i][:, :], ACT.Copy)
            last.then_inc(sem("gather_copied"), 1)
            for c in range(NFC):
                act.wait_ge(sem("moe_gate"), NFC * it + NFC + c + 1)
                if c == 0:
                    act.wait_ge(sem("H_done"), NFC * it + NFC)
                else:
                    act.wait_ge(sem("H_done"), NFC * it + NFC + c)
                act_.activation(MO["silu"], bank[0][:, :], ACT.Silu).then_inc(sem("moe_silu"), 1)
                if c:
                    act.wait_ge(sem("HT_done"), NFC * it + c)
                    act_.activation(flat(HT[:, (c - 1) % 2]), bank[2][:, :], ACT.Copy).then_inc(
                        sem("HT_copied"), 1)
            act.wait_ge(sem("HT_done"), NFC * it + NFC)
            act_.activation(flat(HT[:, (NFC - 1) % 2]), bank[2][:, :], ACT.Copy).then_inc(sem("HT_copied"), 1)
            act.wait_ge(sem("gatedT_done"), it + 1)
            act_.activation(MO["gatedT"], bank[3][:, 0:T], ACT.Copy).then_inc(sem("gatedT_copied"), 1)
            act.wait_ge(sem("moe_down"), NFC * it + 2 * NFC)
            for i in range(2):
                last = act_.activation(MO["Y"][:, 512 * i:512 * i + 512], bank[4 + i][:, :], ACT.Copy)
            last.then_inc(sem("Y_copied"), 1)
        act.wait_ge(sem("acc_final"), 1)
        for t in range(NT):
            last = act_.activation(MO["xtok"][:, t * D:t * D + D], htok[:, t, :], ACT.Square,
                                   accum_out=MO["m12"][:, 8 + t:9 + t])
        link(last)
        act_.activation(MO["m12"][:, 10:12], MO["m12"][:, 8:10], ACT.Sqrt, scale=1.0 / D, bias=C("eps")).then_inc(
            sem("final_rms"), 1)

    @block.vector
    def _(dve):
        chain = [0]

        def link(ins):
            chain[0] += 1
            ins.then_inc(sem("dve_chain"), 1)
            dve.wait_ge(sem("dve_chain"), chain[0])

        dve.wait_ge(sem("vecs_T"), 1)
        v.tensor_copy(pcol[:, :], bank[0][:, 0:NVEC])
        for i in range(2):
            dve.wait_ge(sem("x_T"), i + 1)
            v.tensor_copy(flat(hT[:, 2 * i:2 * i + 2, :]), bank[1 + i][:, :]).then_inc(sem("x_copied"), 1)

        def norm(n, gname):
            dve.wait_ge(sem("rms_done"), n + 1)
            link(v.reciprocal(rstd[:, :], rstd[:, :]))
            for k in range(KD):
                last = v.scalar_tensor_tensor(xnT[:, k, :], hT[:, k, :], col(gname, k), rstd[:, :], MUL, MUL)
            last.then_inc(sem("xn_done"), 1)

        norm(0, "e_norm_mix")

        dve.wait_ge(sem("s5_loaded"), 16 * 13)
        dve.wait_ge(sem("consts_loaded"), 16)

        def exp_parts(x, pm1, s, k, r):
            link(v.tensor_scalar(k, x, 1.0 / math.log(2), ROUND, MUL, ADD))
            link(v.tensor_scalar(k, k, ROUND, -126.0, SUB, ALU.max))
            link(v.tensor_scalar(k, k, 127.0, None, ALU.min))
            link(v.scalar_tensor_tensor(r, k, -0.693359375, x, MUL, ADD))
            link(v.scalar_tensor_tensor(r, k, 2.12194440e-4, r, MUL, ADD))
            link(v.tensor_scalar(pm1, r, 1.0 / math.factorial(8), None, MUL))
            for n in range(7, 0, -1):
                link(v.scalar_tensor_tensor(pm1, pm1, 1.0 / math.factorial(n), r, ADD, MUL))
            link(v.tensor_scalar(k, k, 127.0, float(2 ** 23), ADD, MUL))
            link(v.tensor_copy(s.bitcast(i32), k))

        ar, ai, dts, em, mag, fr_, sn_, hs, cs_, xi, den, tmp, fre, fim, t14, t15 = small
        dt = dts[:, 1:2]
        exp_parts(dts[:, 0:1], dt, dts[:, 2:3], dts[:, 3:4], dts[:, 4:5])
        link(v.scalar_tensor_tensor(dt, dt, 1.0, dts[:, 2:3], ADD, MUL))
        link(v.tensor_scalar(t14, ar, dt, None, MUL))
        exp_parts(t14, em, mag, tmp, t15)
        link(v.tensor_tensor(em, em, mag, MUL))
        link(v.scalar_tensor_tensor(em, mag, -1.0, em, ADD, ADD))
        link(v.tensor_scalar(mag, em, 1.0, None, ADD))
        link(v.tensor_scalar(t14, ai, dt, 1.0 / (2 * math.pi), MUL, MUL))
        link(v.tensor_scalar(t15, t14, ROUND, ROUND, ADD, SUB))
        v.tensor_tensor(fr_, t14, t15, SUB).then_inc(sem("s5_angle"), 1)
        v.tensor_tensor(den, ar, ar, MUL)
        link(v.tensor_tensor(tmp, ai, ai, MUL))
        link(v.tensor_tensor(den, den, tmp, ADD))
        link(v.reciprocal(den, den))
        dve.wait_ge(sem("s5_sin"), 1)
        link(v.scalar_tensor_tensor(hs, hs, -2.0, hs, MUL, MUL))
        link(v.tensor_scalar(cs_, hs, 1.0, None, ADD))
        v.tensor_tensor(xi, mag, sn_, MUL)
        link(v.tensor_tensor(tmp, em, cs_, MUL))
        link(v.tensor_tensor(cs_, tmp, hs, ADD))
        v.tensor_tensor(t14, cs_, ar, MUL)
        v.tensor_tensor(t15, xi, ai, MUL)
        v.tensor_tensor(fre, xi, ar, MUL)
        link(v.tensor_tensor(fim, cs_, ai, MUL))
        link(v.tensor_tensor(t14, t14, t15, ADD))
        link(v.tensor_tensor(t15, fre, fim, SUB))
        v.tensor_tensor(fre, t14, den, MUL)
        v.tensor_tensor(fim, t15, den, MUL).then_inc(sem("s5_params"), 1)
        dve.wait_ge(sem("s5_params_T"), 1)
        link(v.tensor_copy(flat(s5p), bank[7][:, 0:4 * G5]))
        def gc(x):
            return x.rearrange("p (g c) -> p g c", c=C5)
        F_re = s5p[:, 2, :][:, :, None].to_broadcast([P, G5, C5])
        F_im = s5p[:, 3, :][:, :, None].to_broadcast([P, G5, C5])
        link(v.tensor_scalar(pre["Bs"], pre["Bs"], C("half_sign"), None, MUL))
        v.tensor_tensor(gc(pre["M1"]), gc(pre["Bx"]), F_re, MUL)
        v.tensor_tensor(gc(pre["M2"]), gc(pre["Bx"]), F_im, MUL)
        link(v.tensor_tensor(gc(pre["mt"]), gc(pre["Bs"]), F_im, MUL))
        link(v.tensor_tensor(gc(pre["Bs"]), gc(pre["Bs"]), F_re, MUL))
        v.tensor_tensor(pre["M1"], pre["M1"], pre["mt"], ADD)
        v.tensor_tensor(pre["M2"], pre["M2"], pre["Bs"], SUB).then_inc(sem("bbar_done"), 1)
        dve.wait_ge(sem("c_T"), 1)
        v.tensor_scalar(flat(CT[:, 0]), bank[2][:, :], C("half_sign"), -1.0, MUL, MUL)
        v.tensor_scalar(flat(CT[:, 1]), bank[3][:, :], -1.0, None, MUL).then_inc(sem("c_copied"), 1)
        dve.wait_ge(sem("bbar_T"), 1)
        v.tensor_copy(flat(BT[:, 0]), bank[5][:, :])
        v.tensor_copy(flat(BT[:, 1]), bank[6][:, :]).then_inc(sem("prep_done"), 1)

        def c_weights(k):
            if k == 0:
                dve.wait_ge(sem("cw_zero"), 1)
                dve.wait_ge(sem("c_copied"), 1)
            if k >= 2:
                dve.wait_ge(sem("y_used"), 4 * (k - 1))
            for m in range(2):
                last = v.tensor_copy(CW[:, k % 2, m, :].rearrange("p (g x) -> p g x", x=P + C5)[:, :, 0:C5],
                                     CT[:, m, k, :].rearrange("p (g c) -> p g c", c=C5))
            last.then_inc(sem("cw_ready"), 1)

        def less_whole(b):
            for j in range(2):
                last = v.scalar_tensor_tensor(frac[:, b % 2, j, :], C("time"), s5p[:, 1, 2 * b + j:2 * b + j + 1],
                                              rn[:, j, :], MUL, SUB)
            last.then_inc(sem("frac_ready"), 1)

        def all_angles(b):
            if b >= 2:
                dve.wait_ge(sem("table_ready"), b - 1)
            if b:
                dve.wait_ge(sem("frac_ready"), b)
            v.tensor_scalar(rn[:, 0, :], C("time"), s5p[:, 1, 2 * b:2 * b + 1], ROUND, MUL, ADD)
            link(v.tensor_scalar(rn[:, 1, :], C("time"), s5p[:, 1, 2 * b + 1:2 * b + 2], ROUND, MUL, ADD))
            link(v.tensor_scalar(flat(rn), flat(rn), ROUND, None, SUB))
            less_whole(b)

        def scans(b):
            A, B = bank[2 * (b % 2)], bank[2 * (b % 2) + 1]
            dve.wait_ge(sem("ab_done"), b + 1)
            dve.wait_ge(sem("table_ready"), b + 1)
            v.tensor_tensor(flat(ta), A[:, :], flat(cs[:, b % 2]), MUL)
            v.tensor_tensor(flat(tb), B[:, :], flat(sn[:, b % 2]), MUL).then_inc(sem("ab_read"), 1)
            dve.wait_ge(sem("ab_read"), b + 1)
            link(v.tensor_tensor(flat(ta), flat(ta), flat(tb), ADD))
            for j in range(2):
                g = 2 * b + j
                last = v.tensor_tensor_scan(scan[:, b % 2, j, :], s5p[:, 0, g:g + 1].to_broadcast([P, T]),
                                            ta[:, j, :], 0.0, MUL, ADD)
            link(last)
            if b >= 2:
                dve.wait_ge(sem("y_used"), b - 1)
            v.tensor_tensor(flat(oc[:, b % 2]), flat(scan[:, b % 2]), flat(cs[:, b % 2]), MUL)
            v.tensor_tensor(flat(os_[:, b % 2]), flat(scan[:, b % 2]), flat(sn[:, b % 2]), MUL).then_inc(
                sem("s5_out"), 1)

        def softmax(u, base, p, mask, first):
            if 1 <= u <= UNITS:
                w, nk = u - 1, P * ((u - 1) % NT + 1)
                s = 2 * (w % 2)
                dve.wait_ge(sem("exp_done"), base + w + 1)
                link(v.reciprocal(stat[:, 24 + s:26 + s], stat[:, 16 + s:18 + s]))
                for j in range(2):
                    last = v.tensor_scalar(p[:, w % 2, j, 0:nk], p[:, w % 2, j, 0:nk],
                                           stat[:, 24 + s + j:25 + s + j], None, MUL)
                last.then_inc(sem("p_ready"), 1)
            if u < UNITS:
                nk, s = P * (u % NT + 1), 2 * (u % 2)
                dve.wait_ge(sem("sc_done"), base + u + 1)
                if u >= 2:
                    dve.wait_ge(sem("pt_done"), base + u - 1)
                for j in range(2):
                    last = v.tensor_tensor(p[:, u % 2, j, 0:nk], bank[5 + j][:, 0:nk], mask(u)[:, 0:nk], ADD)
                last.then_inc(sem("sc_read"), 1)
                dve.wait_ge(sem("sc_read"), base + u + 1)
                link(v.tensor_reduce(stat[:, s:s + 2], p[:, u % 2, :, 0:nk], AX, ALU.max))
                v.tensor_scalar(stat[:, 8 + s:10 + s], stat[:, s:s + 2], -SCALE, None, MUL).then_inc(
                    sem("nb_ready"), 1)

        def rope(x, pb, tmp, done):
            n = x.shape[1]
            cosb = C("cos")[:, None, :].to_broadcast([P, n, T])
            sinb = C("sin")[:, None, :].to_broadcast([P, n, T])
            v.tensor_tensor(tmp.rearrange("p (k t) -> p k t", k=n),
                            pb.rearrange("p (k t) -> p k t", k=n), sinb, MUL)
            link(v.tensor_tensor(x, x, cosb, MUL))
            v.tensor_tensor(x, x, tmp.rearrange("p (k t) -> p k t", k=n), ADD).then_inc(done, 1)

        p0 = att["p"].rearrange("p (b j n) -> p b j n", b=2, j=2)
        c_weights(0)
        c_weights(1)
        all_angles(0)
        for what, i in plan:
            if what == "s5":
                if i + 1 < NB5:
                    all_angles(i + 1)
                if i < NB5:
                    scans(i)
                if i % 4 == 0 and i:
                    k = i // 4 - 1
                    dve.wait_ge(sem("y_used"), i)
                    v.scalar_tensor_tensor(yT[:, k, :], uT[:, k, :], col("s5_d", k), bank[4][:, 0:T],
                                           MUL, ADD).then_inc(sem("y_added"), 1)
                if i in (7, 11):
                    c_weights((i + 1) // 4)
            elif what == "rope":
                x = (qT, kT)[i // 2][:, 2 * (i % 2):2 * (i % 2) + 2, :]
                dve.wait_ge(sem("rope_P"), i + 1)
                rope(x, bank[5 + i % 3][:, :], att["rope"][:, 512 * (i % 2):512 * (i % 2) + 512], sem("rope_done"))
            elif what == "attn":
                softmax(i, 0, p0, lambda u: C(f"causal{u % NT}"), None)
        dve.wait_ge(sem("glu_gate"), 1)
        v.tensor_tensor(flat(yT[:, 0:KM]), flat(yT[:, 0:KM]), L0["um"], MUL).then_inc(sem("glu_done"), 1)

        def add_h(i, b, n):
            dve.wait_ge(sem("into_h"), n)
            v.tensor_tensor(flat(hT[:, 2 * i:2 * i + 2, :]), flat(hT[:, 2 * i:2 * i + 2, :]), b[:, :],
                            ADD).then_inc(sem("h_added"), 1)

        for i in range(4):
            add_h(i, bank[2 + i], i + 1)
        norm(1, "e_norm_ffn")
        nf = len(range(0, FFN, FB))
        for c in range(nf):
            w = min(FB, FFN - c * FB) // P
            dve.wait_ge(sem("silu_done"), c + 1)
            dve.wait_ge(sem("ffn_up"), c + 1)
            if c >= 2:
                dve.wait_ge(sem("ffn_down"), c - 1)
            for i in range(w // 2):
                last = v.tensor_tensor(flat(hc[:, c % 2, 2 * i:2 * i + 2, :]), gate_s[:, 512 * i:512 * i + 512],
                                       bank[2 + i][:, :], MUL)
            last.then_inc(sem("hc_done"), 1)
        for i in range(4):
            add_h(i, bank[4 + i], 5 + i)

        norm(2, "o_norm_mix")
        v.memset(raw[:, :, :, 0:1].rearrange("p b k o -> p (b k o)"), 0.0).then_inc(sem("raw_zero"), 1)
        dve.wait_ge(sem("raw_zero"), 1)
        for i in range(7):
            dve.wait_ge(sem("odd_copied"), i + 1)
            x = raw[:, i % 2]
            if i:
                dve.wait_ge(sem("shifted"), i)
            link(v.tensor_tensor(L1["diff"].rearrange("p (k t) -> p k t", k=2), x[:, :, 0:T], x[:, :, 1:T + 1], SUB))
            for k in range(2):
                last = v.scalar_tensor_tensor(shf[:, 2 * i + k, :], L1["diff"][:, k * T:k * T + T],
                                              col("rwkv_mu", 2 * i + k), x[:, k, 1:T + 1], MUL, ADD)
            last.then_inc(sem("shifted"), 1)
        for i, x in enumerate((draw[:, 0:2], draw[:, 2:4], draw[:, 5:7])):
            dve.wait_ge(sem("odd_rope_P"), i + 1)
            rope(x, bank[5 + i % 3][:, :], att["rope"][:, 512 * (i % 2):512 * (i % 2) + 512], sem("odd_rope"))
        for i, x in enumerate((L1["kd"], L1["kid"])):
            dve.wait_ge(sem("odd_rope_P"), 4 + i)
            dve.wait_ge(sem("odd_rope"), 3 + i)
            link(v.tensor_tensor(x, bank[i][:, 0:T], C("cos"), MUL))
            link(v.tensor_tensor(att["rope"][:, 0:T], bank[i][:, T:2 * T], C("sin"), MUL))
            v.tensor_tensor(x, x, att["rope"][:, 0:T], ADD).then_inc(sem("odd_rope"), 1)
        for t in range(NT):
            nk = P * (t + 1)
            acc, work = L1["acc"][:, 0:nk], L1["work"][:, 0:nk]
            dve.wait_ge(sem("relu_done"), t + 1)
            dve.wait_ge(sem("kv_copied"), NT)
            link(v.tensor_scalar(acc, relu[:, 0, 0:nk], wi[:, t, 0:1], None, MUL))
            for h in range(1, 4):
                ins = v.scalar_tensor_tensor(acc, relu[:, h, 0:nk], wi[:, t, h:h + 1], acc, MUL, ADD)
                if h < 3:
                    link(ins)
                else:
                    ins.then_inc(sem("acc_done"), 1)
            dve.wait_ge(sem("acc_done"), t + 1)
            link(v.tensor_tensor(work, acc, C(f"causal{t}")[:, 0:nk], ADD))
            for r in range(TOPK // 8):
                link(v.max(L1["top"], work))
                link(v.match_replace(work, L1["top"], work, -3.0e38))
            link(v.tensor_scalar(work, work, -2.0e38, NEG, ALU.is_gt, MUL))
            v.tensor_tensor(md[:, t, 0:nk], work, C(f"causal{t}")[:, 0:nk], ADD).then_inc(sem("md_done"), 1)
            dve.wait_ge(sem("md_done"), t + 1)
        for u in range(UNITS + 2):
            softmax(u, UNITS, p0, lambda u: md[:, u % NT, :], None)
        dve.wait_ge(sem("gates_done"), 1)
        for k in range(KM):
            last = v.tensor_scalar(KK[:, k, :], shf[:, 4 + k, :], col("rwkv_k_k", k), None, MUL)
        last.then_inc(sem("kk_raw"), 1)
        for k in range(KM):
            last = v.tensor_tensor_scan(Lc[:, k, :], C("restart"), lw[:, k, :], 0.0, MUL, ADD)
        link(last)
        v.tensor_tensor(flat(lw), flat(Lc), flat(lw), SUB).then_inc(sem("L_done"), 1)
        for k in range(KM):
            last = v.tensor_scalar(rk[:, k, :], Ag[:, k, :], -1.0, col("rwkv_k_a", k), ADD, MUL)
        link(last)
        link(v.scalar_tensor_tensor(flat(shf[:, 4:8]), flat(rk), 1.0, flat(shf[:, 4:8]), ADD, MUL))
        for k in range(KM):
            last = v.scalar_tensor_tensor(rk[:, k, :], shf[:, k, :], col("rwkv_r_k", k), shf[:, 4 + k, :], MUL, MUL)
        last.then_inc(sem("rk_done"), 1)
        dve.wait_ge(sem("kk_norm"), 1)
        link(v.tensor_scalar(flat(tmp4), flat(tmp4), 1e-12, None, ALU.max))
        link(v.reciprocal(flat(tmp4), flat(tmp4)))
        link(v.tensor_tensor(flat(KK), flat(KK), flat(tmp4), MUL))
        dve.wait_ge(sem("exps_done"), 1)
        link(v.tensor_tensor(flat(Ag), flat(Ag), flat(KK), MUL))
        v.tensor_tensor(flat(Ag), flat(Ag), flat(Em), MUL)
        v.scalar_tensor_tensor(AR[:, :, 0, :], KK[:, :, :], -1.0, lw[:, :, :], MUL, MUL)
        v.tensor_tensor(AR[:, :, 1, :], shf[:, 0:4, :], Lc, MUL)
        v.tensor_tensor(flat(shf[:, 4:8]), flat(shf[:, 4:8]), flat(Em), MUL)
        v.tensor_copy(lam, Lc[:, :, CHUNK - 1::CHUNK])
        v.memset(sc["S"], 0.0)
        v.memset(sc["G"], 0.0)
        v.memset(sc["U"], 0.0).then_inc(sem("tilde_done"), 1)
        dve.wait_ge(sem("tilde_done"), 1)
        MB5 = ring[:, 0:HEADS * 2 * P].rearrange("p (f j x) -> p f j x", f=KM, j=2)
        MK5 = ring[:, HEADS * 2 * P:2 * HEADS * 2 * P].rearrange("p (f j x) -> p f j x", f=KM, j=2)
        T4 = sc["T"].rearrange("p (f j n) -> p f j n", f=KM, j=2)
        pair_mask = con[:, coff["before"][0]:coff["before"][0] + 2 * P]
        for t in range(NT):
            for hh in range(2):
                dve.wait_ge(sem("A_done"), 2 * t + hh + 1)
                for j in range(2):
                    for dst, b in ((MB5, bank[j]), (MK5, bank[2 + j])):
                        v.tensor_tensor(dst[:, 2 * hh:2 * hh + 2, j, :], b[:, :].rearrange("p (f x) -> p f x", f=2),
                                        pair_mask[:, None, :].to_broadcast([P, 2, 2 * P]), MUL)
                    last = v.tensor_tensor(T4[:, 2 * hh:2 * hh + 2, j, :],
                                           bank[4 + j][:, 0:2 * P].rearrange("p (f n) -> p f n", f=2),
                                           C("level1")[:, None, :].to_broadcast([P, 2, P]), MUL)
                last.then_inc(sem("A_copied"), 1)
                dve.wait_ge(sem("A_copied"), 2 * t + hh + 1)
                hs_ = slice(4 * hh, 4 * hh + 4)
                idb = C("ident")[:, None, :].to_broadcast([P, 4, P])
                link(v.tensor_tensor(TT[:, hs_, :], MB[:, hs_, 0, :], C("level1T")[:, None, :].to_broadcast([P, 4, P]), MUL))
                v.tensor_tensor(TT[:, hs_, :], TT[:, hs_, :], idb, ADD)
                v.tensor_tensor(Tm[:, hs_, :], Tm[:, hs_, :], idb, ADD).then_inc(sem("T_ready"), 1)
            for n, m in enumerate(LEVELS[1:]):
                for hh in range(2):
                    q = (t * 5 + n) * 2 + hh
                    hs_ = slice(4 * hh, 4 * hh + 4)
                    Z4, T4_, TT4 = Zm[:, hs_, :], Tm[:, hs_, :], TT[:, hs_, :]
                    bz, bt, btt = bank[3 * hh], bank[3 * hh + 1], bank[3 * hh + 2]
                    dve.wait_ge(sem("Z_done"), q + 1)
                    v.tensor_tensor(Z4, bz[:, :].rearrange("p (h n) -> p h n", h=4),
                                    C(f"level{m}")[:, None, :].to_broadcast([P, 4, P]), MUL).then_inc(sem("Z_copied"), 1)
                for hh in range(2):
                    q = (t * 5 + n) * 2 + hh
                    hs_ = slice(4 * hh, 4 * hh + 4)
                    T4_, TT4 = Tm[:, hs_, :], TT[:, hs_, :]
                    bt, btt = bank[3 * hh + 1], bank[3 * hh + 2]
                    dve.wait_ge(sem("TZ_done"), q + 1)
                    if m < 32:
                        v.tensor_tensor(flat(T4_), flat(T4_), bt[:, :], ADD)
                    v.tensor_tensor(flat(TT4), flat(TT4), btt[:, :], ADD).then_inc(sem("TT_ready"), 1)
            for ci in range(2):
                c = 2 * t + ci
                dve.wait_ge(sem("dS_done"), c + 1)
                if c:
                    dve.wait_ge(sem("S_ready"), c)
                ds = sc["ds"].rearrange("p (k n) -> p k n", k=KM)
                link(v.tensor_tensor(ds, bank[0][:, :].rearrange("p (k n) -> p k n", k=KM),
                                     C("block_ones")[:, None, :].to_broadcast([P, KM, P]), MUL))
                link(v.tensor_tensor(ds, ds, Sbd, ADD))
                v.tensor_tensor(Sbd, ds, lam[:, :, c:c + 1].to_broadcast([P, KM, P]), MUL).then_inc(sem("S_ready"), 1)
            dve.wait_ge(sem("y_done"), t + 1)
            dve.wait_ge(sem("lora_loaded"), 16 * 5)
            ya, yb = (sc[n].rearrange("p (h n) -> p h n", h=HEADS) for n in ("ya", "yb"))
            yp = bank[1][:, :].rearrange("p (h n) -> p h n", h=HEADS)
            link(v.tensor_reduce(st8[:, 0, :], yp, AX, ADD))
            link(v.tensor_scalar(st8[:, 0, :], st8[:, 0, :], -1.0 / HD, None, MUL))
            link(v.tensor_tensor(ya, yp, st8[:, 0, :][:, :, None].to_broadcast([P, HEADS, HD]), ADD))
            link(v.tensor_tensor(yb, ya, ya, MUL))
            v.tensor_reduce(st8[:, 1, :], yb, AX, ADD).then_inc(sem("gn_var"), 1)
            dve.wait_ge(sem("gn_var"), t + 1)
            link(v.tensor_tensor(yb, sc["Vt"].rearrange("p (h n) -> p h n", h=HEADS),
                                 bank[4][:, 0:HEADS][:, :, None].to_broadcast([P, HEADS, HD]), MUL))
            dve.wait_ge(sem("gn_std"), t + 1)
            link(v.reciprocal(st8[:, 3, :], st8[:, 2, :]))
            link(v.tensor_tensor(ya, ya, st8[:, 3, :][:, :, None].to_broadcast([P, HEADS, HD]), MUL))
            link(v.tensor_tensor(sc["ya"], sc["ya"], L1["lnw"], MUL))
            link(v.tensor_tensor(sc["ya"], sc["ya"], L1["lnb"], ADD))
            link(v.tensor_tensor(sc["ya"], sc["ya"], sc["yb"], ADD))
            v.tensor_tensor(sc["ya"], sc["ya"], bank[3][:, :], MUL).then_inc(sem("bonus_used"), 1)
            dve.wait_ge(sem("bonus_used"), t + 1)
        for i in range(4):
            add_h(i, bank[2 + i], 9 + i)

        norm(3, "o_norm_ffn")
        def cp(dst, src):
            return v.tensor_copy(dst, src)

        m12 = MO["m12"]
        dve.wait_ge(sem("logits_done"), 1)
        link(cp(flat(lg), bank[7][:, 0:NT * NE]))

        def first_max(e_out, x, m):
            link(v.tensor_reduce(m, x, AX, ALU.max))
            link(v.tensor_tensor(e_out, x, m[:, :, None].to_broadcast([P, NT, NE]), ALU.is_equal))
            link(v.tensor_tensor_scan(flat(t16), C("restart8"), flat(e_out), 0.0, MUL, ADD))
            link(v.scalar_tensor_tensor(flat(e_out), flat(t16), 1.0, flat(e_out), ALU.is_le, MUL))

        first_max(e1, lg, m12[:, 0:2])
        link(v.scalar_tensor_tensor(flat(lg), flat(e1), -3.0e38, flat(lg), MUL, ADD))
        first_max(e2, lg, m12[:, 2:4])
        link(v.tensor_tensor(m12[:, 2:4], m12[:, 2:4], m12[:, 0:2], SUB))
        v.tensor_tensor(flat(sel), flat(e1), flat(e2), ADD).then_inc(sem("m12_done"), 1)
        dve.wait_ge(sem("m12_exp"), 1)
        link(v.tensor_scalar(m12[:, 6:8], m12[:, 4:6], 1.0, None, ADD))
        link(v.reciprocal(m12[:, 6:8], m12[:, 6:8]))
        link(v.tensor_tensor(m12[:, 4:6], m12[:, 4:6], m12[:, 6:8], MUL))
        link(v.tensor_tensor(gate, e1, m12[:, 6:8][:, :, None].to_broadcast([P, NT, NE]), MUL))
        link(v.tensor_tensor(e2, e2, m12[:, 4:6][:, :, None].to_broadcast([P, NT, NE]), MUL))
        link(v.tensor_tensor(flat(gate), flat(gate), flat(e2), ADD))
        cnt = MO["cnt"].rearrange("p (a e) -> p a e", a=4)
        dve.wait_ge(sem("rank_done"), 1)
        cp(flat(rank), bank[6][:, 0:NT * NE])
        link(cp(cnt[:, 0, :], bank[6][:, NT * NE:NT * NE + NE]))
        link(v.tensor_scalar(cnt[:, 1, :], cnt[:, 0, :], CAP + 0.5, None, ALU.is_gt))
        link(v.tensor_tensor_scan(cnt[:, 2, :], C("ones")[:, 0:NE], cnt[:, 1, :], float(NE), MUL, ADD))
        link(v.tensor_tensor(cnt[:, 3, :], cnt[:, 2, :], cnt[:, 1, :], SUB))
        item = C("item").rearrange("p (i e) -> p i e", e=NE)
        first = C("first").rearrange("p (i e) -> p i e", e=NE)
        oh, ohx = (MO[n].rearrange("p (i e) -> p i e", e=NE) for n in ("oh", "ohx"))
        sh3 = [P, ITEMS, NE]
        link(v.tensor_tensor(oh, item, cnt[:, 3, :][:, None, :].to_broadcast(sh3), ALU.is_ge))
        link(v.tensor_tensor(ohx, item, cnt[:, 2, :][:, None, :].to_broadcast(sh3), ALU.is_lt))
        link(v.tensor_tensor(oh, oh, ohx, MUL))
        link(v.tensor_scalar(MO["off"], MO["oh"], float(CAP), None, MUL))
        link(v.tensor_tensor(oh, oh, first, ADD))
        link(v.tensor_tensor(ohx, oh, C("expert")[:, None, :].to_broadcast(sh3), MUL))
        link(v.tensor_reduce(MO["ef"][:, 0:ITEMS], ohx, AX, ADD))
        link(cp(MO["ef"][:, ITEMS:ITEMS + 1], cnt[:, 2, NE - 1:NE]))
        v.tensor_copy(work_list[:, :], MO["ef"]).then_inc(sem("work_ready"), 1)
        link(v.tensor_scalar(flat(t16), flat(sel), -1.0, 4096.0, ADD, MUL))
        link(v.tensor_tensor(flat(rank), flat(rank), flat(t16), ADD))
        link(v.tensor_reduce(MO["offi"], MO["off"].rearrange("p (i e) -> p i e", e=NE), AX, ADD))
        for t in range(NT):
            link(v.tensor_tensor(ohx, oh, rank[:, t, :][:, None, :].to_broadcast(sh3), MUL))
            link(v.tensor_reduce(slotp[:, t, :], ohx, AX, ADD))
            link(v.tensor_tensor(slotp[:, t, :], slotp[:, t, :], MO["offi"], SUB))
            link(v.tensor_tensor(ohx, oh, gate[:, t, :][:, None, :].to_broadcast(sh3), MUL))
            link(v.tensor_reduce(gatep[:, t, :], ohx, AX, ADD))
        for t in range(NT):
            for i in range(2):
                dve.wait_ge(sem("htok_T"), 2 * t + i + 1)
                v.tensor_copy(htok[:, t, 512 * i:512 * i + 512], bank[2 + i][:, :]).then_inc(sem("htok_copied"), 1)
        dve.sem_inc(sem("H_done"), NFC)
        dve.sem_inc(sem("scattered"), NT)
        n_items = dve.value_load(work_list[0:1, ITEMS:ITEMS + 1], min_val=NE, max_val=ITEMS)
        with dve.Fori(0, n_items) as it:
            dve.wait_ge(sem("scatter_done"), NT * it + NT)
            for t in range(NT):
                v.tensor_scalar(onehot[:, t, :], C("time")[:, 0:CAP], slotp[:, t, bass.ds(it, 1)], None, ALU.is_equal)
                last = v.tensor_scalar(gated[:, t, :], C("time")[:, 0:CAP], slotp[:, t, bass.ds(it, 1)],
                                       gatep[:, t, bass.ds(it, 1)], ALU.is_equal, MUL)
            last.then_inc(sem("onehot_ready"), 1)
            for c in range(NFC):
                dve.wait_ge(sem("moe_silu"), NFC * it + c + 1)
                dve.wait_ge(sem("moe_up"), NFC * it + NFC + c + 1)
                v.tensor_tensor(Hs[:, c % 2, :], MO["silu"], bank[1][:, :], MUL).then_inc(sem("H_done"), 1)
            for t in range(NT):
                dve.wait_ge(sem("scatter_done"), NT * it + NT + t + 1)
                for i in range(2):
                    b = bank[6 + i] if t == 0 else bank[0 + i]
                    last = v.tensor_tensor(htok[:, t, 512 * i:512 * i + 512], htok[:, t, 512 * i:512 * i + 512],
                                           b[:, :], ADD)
                last.then_inc(sem("scattered"), 1)
        dve.wait_ge(sem("scattered"), NT * n_items + NT)
        dve.sem_inc(sem("acc_final"), 1)
        dve.wait_ge(sem("final_rms"), 1)
        dve.wait_ge(sem("gfin_loaded"), 16)
        link(v.reciprocal(m12[:, 12:14], m12[:, 10:12]))
        for t in range(NT):
            v.scalar_tensor_tensor(htok[:, t, :], htok[:, t, :], m12[:, 12 + t:13 + t], MO["gfin"], MUL,
                                   MUL).then_inc(sem("y_final"), 1)

    @block.tensor
    def _(pe):
        def loaded(n):
            pe.wait_ge(slot_sem[n % SLOTS], 16 * (n // SLOTS + 1))

        pe.wait_ge(sem("consts_loaded"), 16)
        pe.wait_ge(sem("vecs_loaded"), 16 * len(VECS))
        ident = C("ident")
        pe_.transpose(bank[0][:, 0:NVEC], pre["vecs"][0:NVEC, :], ident[0:NVEC, 0:NVEC]).then_inc(
            sem("vecs_T"), 1)
        pe.wait_ge(sem("x_loaded"), 16)
        for k in range(KD):
            for t in range(NT):
                o = (k % 2) * T + t * P
                last = pe_.transpose(bank[1 + k // 2][:, o:o + P], xtok[:, t, k * P:k * P + P], ident)
            if k % 2:
                last.then_inc(sem("x_T"), 1)

        def norm(n):
            pe.wait_ge(sem("sq_done"), n + 1)
            for k in range(KD):
                last = pe_.matmul(bank[5][:, 0:T], C("ones"), yT[:, k, :], start=(k == 0), stop=(k == KD - 1))
            last.then_inc(sem("ss_done"), 1)

        def project(n, tiles, dst):
            w = view(n)
            for i in tiles:
                width = min(P, w.shape[2] - i * P)
                for k in range(KD):
                    last = pe_.matmul(dst(i)[0:width, :], w[:, k, i * P:i * P + width], xnT[:, k, :],
                                      start=(k == 0), stop=(k == KD - 1))
            return last

        def half(b, i):
            return b[:, (i % 2) * T:(i % 2) * T + T]

        norm(0)
        pe.wait_ge(sem("xn_done"), 1)
        loaded(0)
        for i in range(2):
            last = project(0, (2 * i, 2 * i + 1), lambda j: half(bank[j // 2], j))
            last.then_inc(sem("u_done"), 1)
        pe.wait_ge(sem("s5_loaded"), 16 * 13)
        for m, src in enumerate((pre["Cx"], pre["Cs"])):
            for k in range(4):
                last = pe_.transpose(bank[2 + m][:, k * P:k * P + P], src[:, k * P:k * P + P], ident)
        last.then_inc(sem("c_T"), 1)
        pe.wait_ge(sem("s5_params"), 1)
        for i, x in enumerate((small[4], small[5], small[12], small[13])):
            last = pe_.transpose(bank[7][:, G5 * i:G5 * i + G5], x, ident[0:G5, 0:G5])
        last.then_inc(sem("s5_params_T"), 1)
        pe.wait_ge(sem("bbar_done"), 1)
        for m, src in enumerate((pre["M1"], pre["M2"])):
            for k in range(4):
                last = pe_.transpose(bank[5 + m][:, k * P:k * P + P], src[:, k * P:k * P + P], ident)
        last.then_inc(sem("bbar_T"), 1)

        def bu(b):
            pe.wait_ge(sem("um_ready"), b + 1)
            if b < 2:
                pe.wait_ge(sem("prep_done"), 1)
            else:
                pe.wait_ge(sem("ab_read"), b - 1)
            for m in range(2):
                for j in range(2):
                    last = pe_.matmul(half(bank[2 * (b % 2) + m], j), BT[:, m, b // 4, :], um[:, b % 2, j, :],
                                      start=True, stop=True)
            last.then_inc(sem("ab_done"), 1)

        def cx(b):
            k = b // 4
            pe.wait_ge(sem("s5_out"), b + 1)
            if b % 4 == 0:
                pe.wait_ge(sem("cw_ready"), k + 1)
                if k:
                    pe.wait_ge(sem("y_added"), k)
            for j in range(2):
                g = (2 * b + j) % 8
                for m, x in enumerate((oc, os_)):
                    last = pe_.matmul(bank[4][:, 0:T], CW[:, k % 2, m, g * P:g * P + P], x[:, b % 2, j, :],
                                      start=(g == 0 and m == 0), stop=(g == 7 and m == 1))
            last.then_inc(sem("y_used"), 1)

        def attention(u, base, q, k, vals, pT, first):
            if u >= 2:
                w = u - 2
                t, nt = w % NT, w % NT + 1
                pe.wait_ge(sem("pt_copied"), base + w + 1)
                for j in range(2):
                    for kt in range(nt):
                        last = pe_.matmul(bank[7][HD * j:HD * j + HD, 0:P], vals(kt, 2 * (w // NT) + j),
                                          pT[:, P * (nt * j + kt):P * (nt * j + kt) + P],
                                          start=(kt == 0), stop=(kt == nt - 1))
                last.then_inc(sem("pv_done"), 1)
            if u < UNITS:
                t, nk = u % NT, P * (u % NT + 1)
                if u == 0:
                    first()
                else:
                    pe.wait_ge(sem("sc_read"), base + u)
                for j in range(2):
                    last = pe_.matmul(bank[5 + j][:, 0:nk], q(u // NT, j)[:, t * P:t * P + P],
                                      k(u // NT, j)[:, 0:nk], start=True, stop=True)
                last.then_inc(sem("sc_done"), 1)
            if 1 <= u <= UNITS:
                w = u - 1
                nt = w % NT + 1
                pe.wait_ge(sem("p_ready"), base + w + 1)
                if w:
                    pe.wait_ge(sem("o_copied"), base + w)
                p = att["p"].rearrange("p (b j n) -> p b j n", b=2, j=2)
                for j in range(2):
                    for kt in range(nt):
                        o = P * (nt * j + kt)
                        last = pe_.transpose(bank[7][:, o:o + P], p[:, w % 2, j, kt * P:kt * P + P], ident)
                last.then_inc(sem("pt_done"), 1)

        for what, i in plan:
            if what == "s5":
                if i < NB5:
                    bu(i)
                if i:
                    cx(i - 1)
            elif what == "proj":
                if i >= 3:
                    pe.wait_ge(sem("proj_copied"), i - 2)
                b = bank[5 + i % 3]
                if i < 4:
                    n = 1 + i // 2
                    loaded(n)
                    last = project(n, (2 * (i % 2), 2 * (i % 2) + 1), lambda j: half(b, j))
                else:
                    loaded(3)
                    t = i - 4
                    for k in range(KD):
                        last = pe_.matmul(b[:, :], xnT[:, k, t * P:t * P + P], view(3)[:, k, :],
                                          start=(k == 0), stop=(k == KD - 1))
                last.then_inc(sem("proj_done"), 1)
            elif what == "rope":
                pe.wait_ge(sem("proj_copied"), 6)
                if i >= 3:
                    pe.wait_ge(sem("rope_done"), i - 2)
                x = (qT, kT)[i // 2][:, 2 * (i % 2):2 * (i % 2) + 2, :]
                pe_.matmul(bank[5 + i % 3][:, :], C("perm"), flat(x), start=True, stop=True).then_inc(
                    sem("rope_P"), 1)
            elif what == "attn":
                attention(i, 0, lambda f, j: qT[HD * j:HD * j + HD, f, :],
                          lambda f, j: kT[HD * j:HD * j + HD, f, :],
                          lambda kt, h: V0[:, kt, h * HD:h * HD + HD], L0["pT"],
                          lambda: pe.wait_ge(sem("rope_done"), 4))
        loaded(4)
        pe.wait_ge(sem("gelu_done"), 1)
        for m in range(KM):
            for k in range(KM):
                last = pe_.matmul(half(bank[m // 2], m), view(4)[:, k, m * P:m * P + P], yT[:, k, :],
                                  start=(k == 0), stop=(k == KM - 1))
            if m % 2:
                last.then_inc(sem("z_done"), 1)

        def out_projection(n):
            for i in range(KD):
                if i % 4 == 0:
                    loaded(n + i // 4)
                for k in range(KD):
                    last = pe_.matmul(half(bank[2 + i // 2], i), view(n + i // 4)[:, k, (i % 4) * P:(i % 4) * P + P],
                                      yT[:, k, :], start=(k == 0), stop=(k == KD - 1))
                if i % 2:
                    last.then_inc(sem("into_h"), 1)

        pe.wait_ge(sem("glu_done"), 1)
        pe.wait_ge(sem("o_copied"), UNITS)
        out_projection(5)
        norm(1)
        pe.wait_ge(sem("xn_done"), 2)
        nf = len(range(0, FFN, FB))
        n = 7

        def ffn_up(c, n, b, done):
            w = min(FB, FFN - c * FB) // P
            loaded(n)
            for i in range(w):
                for k in range(KD):
                    last = pe_.matmul(half(bank[b + i // 2], i), view(n)[:, k, i * P:i * P + P], xnT[:, k, :],
                                      start=(k == 0), stop=(k == KD - 1))
            last.then_inc(done, 1)

        def ffn_down(c, n):
            w = min(FB, FFN - c * FB) // P
            loaded(n)
            pe.wait_ge(sem("hc_done"), c + 1)
            for i in range(KD):
                for j in range(w):
                    last = pe_.matmul(half(bank[4 + i // 2], i), view(n)[:, j, i * P:i * P + P],
                                      hc[:, c % 2, j, :], start=(c == 0 and j == 0 and i % 2 == 0),
                                      stop=(c == nf - 1 and j == w - 1), skip_group_check=True)
                if c == nf - 1 and i % 2 == 1:
                    last.then_inc(sem("into_h"), 1)
            return last

        ffn_up(0, n, 0, sem("ffn_gate"))
        pe.wait_ge(sem("h_added"), 4)
        ffn_up(0, n + 1, 2, sem("ffn_up"))
        n += 2
        for c in range(1, nf + 1):
            if c < nf:
                pe.wait_ge(sem("silu_done"), c)
                ffn_up(c, n, 0, sem("ffn_gate"))
                pe.wait_ge(sem("hc_done"), c)
                ffn_up(c, n + 1, 2, sem("ffn_up"))
                n += 2
            last = ffn_down(c - 1, n)
            if c < nf:
                last.then_inc(sem("ffn_down"), 1)
            n += 1

        norm(2)
        pe.wait_ge(sem("xn_done"), 3)
        n = 25
        for i in range(11):
            if i >= 8:
                pe.wait_ge(sem("odd_copied"), i - 7)
            if i % 2 == 0:
                loaded(n + i // 2)
            w = view(n + i // 2)
            for x in range(2):
                c0 = ((i % 2) * 2 + x) * P
                width = min(P, w.shape[2] - c0)
                for k in range(KD):
                    last = pe_.matmul(half(bank[i % 8], x)[0:width, :], w[:, k, c0:c0 + width], xnT[:, k, :],
                                      start=(k == 0), stop=(k == KD - 1))
            last.then_inc(sem("odd_proj"), 1)
        pe.wait_ge(sem("odd_copied"), 11)
        for i, x in enumerate((draw[:, 0:2, :], draw[:, 2:4, :], draw[:, 5:7, :])):
            pe_.matmul(bank[5 + i][:, :], C("perm"), flat(x), start=True, stop=True).then_inc(sem("odd_rope_P"), 1)
        for i, k in enumerate((4, 7)):
            for m, name in enumerate(("dup", "dup_perm")):
                last = pe_.matmul(half(bank[i], m), C(name)[0:HD, :], draw[0:HD, k, :], start=True, stop=True)
            last.then_inc(sem("odd_rope_P"), 1)
        for t in range(NT):
            pe_.transpose(bank[2 + t][:, 0:P], draw[:, 4, t * P:t * P + P], ident)
            pe_.transpose(bank[2 + t][:, P:P + HD + 4], draw[0:HD + 4, 7, t * P:t * P + P],
                          ident[0:HD + 4, 0:HD + 4]).then_inc(sem("kv_T"), 1)
        pe.wait_ge(sem("odd_rope"), 5)
        for t in range(NT):
            nk = P * (t + 1)
            if t:
                pe.wait_ge(sem("relu_done"), t)
            for h in range(4):
                j = h % 2
                last = pe_.matmul(half(bank[4 + j], h // 2)[:, 0:nk],
                                  draw[HD * j:HD * j + HD, 5 + h // 2, t * P:t * P + P],
                                  L1["kid"][HD * j:HD * j + HD, 0:nk], start=True, stop=True)
            last.then_inc(sem("idx_done"), 1)
        pe.wait_ge(sem("lora_in"), 2)
        pe.wait_ge(sem("lora_loaded"), 16 * 5)
        pe.wait_ge(sem("kv_copied"), NT)
        for g, (r0, b0) in enumerate(((0, 0), (64, 2))):
            for k in range(KM):
                last = pe_.matmul(half(bank[b0 + k // 2], k), L1["WA"][r0:r0 + 64, k * P:k * P + P],
                                  shf[r0:r0 + 64, 12, :], start=True, stop=True)
        last.then_inc(sem("lora_done"), 1)

        def dsa_first():
            pe.wait_ge(sem("relu_done"), NT)
            pe.wait_ge(sem("md_done"), NT)
        for u in range(UNITS + 2):
            attention(u, UNITS, lambda f, j: draw[HD * j:HD * j + HD, f, :],
                      lambda f, j: L1["kd"][HD * j:HD * j + HD, :],
                      lambda kt, h: Vd[:, kt, :], L1["pT"], dsa_first)
        pe.wait_ge(sem("kk_sq"), 1)
        pe.wait_ge(sem("relu_done"), NT)
        pe.wait_ge(sem("sc_read"), 2 * UNITS)
        for i in range(2):
            last = pe_.matmul(bank[4 + i][:, :], C("block_ones"), sc["tmp"][:, 512 * i:512 * i + 512],
                              start=True, stop=True)
        last.then_inc(sem("kk_ss"), 1)
        pe.wait_ge(sem("tilde_done"), 1)
        pe.wait_ge(sem("gates_done"), 1)
        for t in range(NT):
            tc = slice(t * P, t * P + P)
            if t:
                pe.wait_ge(sem("yc_copied"), t)
                pe.wait_ge(sem("bonus_used"), t)
                pe.wait_ge(sem("S_ready"), 2 * t)
            for i, src in enumerate((shf[:, 8:12, :], shf[:, 4:8, :], Ag)):
                for k in range(KM):
                    last = pe_.transpose(bank[i][:, k * P:k * P + P], src[:, k, tc], ident)
            last.then_inc(sem("tok_T"), 1)
            for hh in range(2):
                if hh == 0:
                    pe.wait_ge(sem("tok_copied"), t + 1)
                else:
                    pe.wait_ge(sem("A_copied"), 2 * t + hh)
                for f in (2 * hh, 2 * hh + 1):
                    for j in range(2):
                        rows = slice(HD * j, HD * j + HD)
                        ar_ = AR[rows, f, :, tc]
                        o = (f % 2) * 2 * P
                        pe_.matmul(bank[j][:, o:o + 2 * P], Ag[rows, f, tc], ar_, start=True, stop=True)
                        pe_.matmul(bank[2 + j][:, o:o + 2 * P], shf[rows, 4 + f, tc], ar_, start=True, stop=True)
                        last = pe_.matmul(bank[4 + j][:, (f % 2) * P:(f % 2) * P + P], AR[rows, f, 0, tc],
                                          Ag[rows, f, tc], start=True, stop=True)
                last.then_inc(sem("A_done"), 1)
            pe.wait_ge(sem("A_copied"), 2 * t + 2)
            for n_, m in enumerate(LEVELS[1:]):
                for hh in range(2):
                    q = (t * 5 + n_) * 2 + hh
                    if n_ == 0:
                        pe.wait_ge(sem("T_ready"), 2 * t + hh + 1)
                    else:
                        pe.wait_ge(sem("TT_ready"), q - 1)
                    for x in range(4):
                        h = 4 * hh + x
                        last = pe_.matmul(bank[3 * hh][:, x * P:x * P + P], MB[:, h, 0, :], Tm[:, h, :],
                                          start=True, stop=True)
                    last.then_inc(sem("Z_done"), 1)
                for hh in range(2):
                    q = (t * 5 + n_) * 2 + hh
                    pe.wait_ge(sem("Z_copied"), q + 1)
                    for x in range(4):
                        h = 4 * hh + x
                        if m < 32:
                            pe_.matmul(bank[3 * hh + 1][:, x * P:x * P + P], TT[:, h, :], Zm[:, h, :],
                                       start=True, stop=True)
                        last = pe_.matmul(bank[3 * hh + 2][:, x * P:x * P + P], Zm[:, h, :], TT[:, h, :],
                                          start=True, stop=True)
                    last.then_inc(sem("TZ_done"), 1)
            pe.wait_ge(sem("TT_ready"), (t + 1) * 10)
            pe_.matmul(bank[3][:, :], shf[:, 13, tc], L1["GU"], start=True, stop=True)
            pe.wait_ge(sem("rk_done"), 1)
            for k in range(KM):
                pe_.matmul(bank[4][:, 2 * k:2 * k + 2], rk[:, k, tc], C("pair"), start=True, stop=True)
            for ci in range(2):
                c = 2 * t + ci
                R = slice(CHUNK * ci, CHUNK * ci + CHUNK)
                tR = slice(t * P + CHUNK * ci, t * P + CHUNK * ci + CHUNK)
                if c:
                    pe.wait_ge(sem("S_ready"), c)
                for k in range(KM):
                    pe_.matmul(bank[6][R, k * P:k * P + P], AR[:, k, 0, tR], Sbd[:, k, :], start=(k == 0),
                               stop=False, skip_group_check=True)
                for h in range(HEADS):
                    last = pe_.matmul(bank[6][R, h * HD:h * HD + HD], MK[:, h, 0, R], sc["Vt"][:, h * HD:h * HD + HD],
                                      start=False, stop=(h == HEADS - 1), skip_group_check=True)
                last.then_inc(sem("G_done"), 1)
                for k in range(KM):
                    pe_.matmul(bank[1][R, k * P:k * P + P], AR[:, k, 1, tR], Sbd[:, k, :], start=(k == 0),
                               stop=False, skip_group_check=True)
                pe.wait_ge(sem("G_copied"), c + 1)
                for h in range(HEADS):
                    last = pe_.matmul(bank[7][R, h * HD:h * HD + HD], TT[:, h, R], sc["G"][:, h * HD:h * HD + HD],
                                      start=True, stop=True)
                last.then_inc(sem("U_done"), 1)
                pe.wait_ge(sem("U_copied"), c + 1)
                for k in range(KM):
                    kc = slice(k * P, k * P + P)
                    pe_.matmul(bank[0][:, kc], sc["Kt"][R, kc], sc["Vt"][R, kc], start=True, stop=False)
                    last = pe_.matmul(bank[0][:, kc], sc["Bt"][R, kc], sc["U"][R, kc], start=False, stop=True)
                last.then_inc(sem("dS_done"), 1)
                for h in range(HEADS):
                    hc_ = slice(h * HD, h * HD + HD)
                    pe_.matmul(bank[1][R, hc_], MB[:, h, 1, R], sc["U"][:, hc_], start=False, stop=False,
                               skip_group_check=True)
                    last = pe_.matmul(bank[1][R, hc_], MK[:, h, 1, R], sc["Vt"][:, hc_], start=False,
                                      stop=(h == HEADS - 1), skip_group_check=True)
            last.then_inc(sem("y_done"), 1)
            pe.wait_ge(sem("bonus_used"), t + 1)
            for k in range(KM):
                last = pe_.transpose(bank[2][:, k * P:k * P + P], sc["ya"][:, k * P:k * P + P], ident)
            last.then_inc(sem("yc_T"), 1)
        pe.wait_ge(sem("yc_copied"), NT)
        pe.wait_ge(sem("o_copied"), 2 * UNITS)
        out_projection(31)

        pe.sem_inc(sem("scatter_done"), NT)
        pe.sem_inc(sem("moe_gate"), NFC)
        pe.sem_inc(sem("moe_up"), NFC)
        pe.sem_inc(sem("moe_down"), NFC)
        norm(3)
        pe.wait_ge(sem("xn_done"), 4)
        pe.wait_ge(sem("router_loaded"), 16)
        for t in range(NT):
            for k in range(KD):
                last = pe_.matmul(bank[7][:, t * NE:t * NE + NE], xnT[:, k, t * P:t * P + P], router[:, k, :],
                                  start=(k == 0), stop=(k == KD - 1))
        last.then_inc(sem("logits_done"), 1)

        def to_tokens(src, b0, done, copied):
            for t in range(NT):
                if t:
                    pe.wait_ge(sem(copied), 2)
                for k in range(KD):
                    last = pe_.transpose(bank[b0 + k // 4][:, (k % 4) * P:(k % 4) * P + P],
                                         src[:, k, t * P:t * P + P], ident)
                    if k % 4 == 3:
                        last.then_inc(sem(done), 1)

        pe.wait_ge(sem("h_added"), 12)
        to_tokens(xnT, 0, "xtok_T", "xtok_copied")
        pe.wait_ge(sem("m12_done"), 1)
        pe_.matmul(bank[6][:, 0:NE], C("earlier"), sel[:, 0, :], start=True, stop=True)
        pe_.matmul(bank[6][:, NE:2 * NE], C("ones"), sel[:, 0, :], start=True, stop=False)
        pe_.matmul(bank[6][:, NE:2 * NE], C("earlier"), sel[:, 1, :], start=False, stop=True)
        pe_.matmul(bank[6][:, 2 * NE:3 * NE], C("ones"), sel[:, 0, :], start=True, stop=False)
        pe_.matmul(bank[6][:, 2 * NE:3 * NE], C("ones"), sel[:, 1, :], start=False, stop=True).then_inc(
            sem("rank_done"), 1)
        to_tokens(hT, 2, "htok_T", "htok_copied")
        pe.wait_ge(sem("work_ready"), 1)
        pe.wait_ge(sem("xtok_copied"), 4)
        pe.wait_ge(sem("htok_copied"), 4)
        n_items = pe.value_load(work_list[0:1, ITEMS:ITEMS + 1], min_val=NE, max_val=ITEMS)
        with pe.Fori(0, n_items) as it:
            def expert_block(j):
                s, turn = (NB0 + j) % SLOTS, (NB0 + j) // SLOTS
                pe.wait_ge(slot_sem[s], (NEB // SLOTS) * 16 * it + 16 * (turn + 1))
                name = expert_blocks[j][0]
                return slot(s).rearrange("p (k n) -> p k n", k=4 if name == "moe_w_down" else KD)

            def up(j, b, done):
                w = expert_block(j)
                for k in range(KD):
                    last = pe_.matmul(bank[b][:, :], XgT[:, k, :], w[:, k, :], start=(k == 0), stop=(k == KD - 1))
                last.then_inc(sem(done), 1)

            def transposes(c):
                pe.wait_ge(sem("H_done"), NFC * it + NFC + c + 1)
                for j in range(4):
                    last = pe_.transpose(bank[2][:, j * CAP:j * CAP + CAP], Hs[:, c % 2, j * P:j * P + P], ident)
                last.then_inc(sem("HT_done"), 1)

            def down(c, j):
                w = expert_block(j)
                pe.wait_ge(sem("HT_copied"), NFC * it + c + 1)
                for i in range(2):
                    for x in range(4):
                        last = pe_.matmul(bank[4 + i][:, :], HT[:, c % 2, x, :], w[:, x, 512 * i:512 * i + 512],
                                          start=(c == 0 and x == 0), stop=(c == NFC - 1 and x == 3))
                last.then_inc(sem("moe_down"), 1)

            pe.wait_ge(sem("onehot_ready"), it + 1)
            pe.wait_ge(sem("scattered"), NT * it + NT)
            for k in range(KD):
                for t in range(NT):
                    last = pe_.matmul(bank[6 + k // 4][:, (k % 4) * CAP:(k % 4) * CAP + CAP],
                                      mtok[:, t, k * P:k * P + P], onehot[:, t, :], start=(t == 0), stop=(t == 1))
            last.then_inc(sem("gather_done"), 1)
            pe.wait_ge(sem("gather_copied"), it + 1)
            j = 0
            for c in range(NFC):
                if c:
                    pe.wait_ge(sem("moe_silu"), NFC * it + c)
                up(j, 0, "moe_gate")
                if c:
                    transposes(c - 1)
                up(j + 1, 1, "moe_up")
                j += 2
                if c:
                    down(c - 1, j)
                    j += 1
            for t in range(NT):
                last = pe_.transpose(bank[3][:, t * P:t * P + P], gated[:, t, :], ident)
            last.then_inc(sem("gatedT_done"), 1)
            transposes(NFC - 1)
            down(NFC - 1, j)
            pe.wait_ge(sem("gatedT_copied"), it + 1)
            pe.wait_ge(sem("Y_copied"), it + 1)
            for t in range(NT):
                for i in range(2):
                    b = bank[6 + i] if t == 0 else bank[i]
                    last = pe_.matmul(b[:, :], MO["gatedT"][:, t * P:t * P + P], MO["Y"][:, 512 * i:512 * i + 512],
                                      start=True, stop=True)
                last.then_inc(sem("scatter_done"), 1)

    ctx.close()


def kernel(**inputs):
    import numpy as _np
    import concourse.bacc as _bacc
    from concourse import mybir as _mybir
    from concourse.bass_utils import run_bass_kernel_spmd as _run

    nc = _bacc.Bacc("TRN2", target_bir_lowering=False, num_devices=1)
    arrays, aps = {}, {}
    for name in inputs:
        x = _np.ascontiguousarray(inputs[name])
        arrays[f"in_{name}"] = x
        aps[name] = nc.dram_tensor(f"in_{name}", x.shape, _mybir.dt.from_np(x.dtype), kind="ExternalInput").ap()
    packed = _np.ascontiguousarray(_np.concatenate(list(constants().values()), axis=1))
    arrays["shape_constants"] = packed
    con = nc.dram_tensor("shape_constants", packed.shape, _mybir.dt.float32, kind="ExternalInput").ap()
    out = nc.dram_tensor("out_0_dram", (1, T, D), _mybir.dt.float32, kind="ExternalOutput").ap()
    trunk(nc, aps, con, out)
    r = _run(nc, [arrays], core_ids=[0])
    return r.results[0]["out_0_dram"]
```

```python
import math
from contextlib import ExitStack

import numpy as np

import concourse.bass as bass
from concourse import mybir

D, T, P = 1024, 256, 128
KD, NT = D // P, T // P
HD, HEADS = 64, 8
MW = HEADS * HD
KM = MW // P
G5, C5, N5 = 32, 16, 64
FFN, FFE, NE = 2816, 3584, 8
FB = 512
RWKV_COLS = 3 * MW + 64 + 64 + 128
ODD_COLS = RWKV_COLS + MW + HD + HD + 4 * HD + HD + 4
CHUNK = 64
NCH = T // CHUNK
CAP = 128
ITEMS = NE + (2 * T) // (CAP + 1)
TOPK = 64
SLOTS = 7
WARM = {"norm_in": [0, 5, 5, 5], "norm_out": [8, 12, 14, 10], "tilde": 3, "A": [3, 5, 8], "group_norm": 14,
        "routing": 3}
PAIR_SLOTS = 3
ARENA = 14120
EPS, GN_EPS = 1e-6, 64e-5
NEG = -1.0e30
ROUND = 12582912.0
DECAY = -math.exp(-0.5)

VECS = [("e_norm_mix", 8), ("e_norm_ffn", 8), ("o_norm_mix", 8), ("o_norm_ffn", 8), ("s5_d", 4),
        ("s5_glu_b", 4), ("rwkv_mu", 14), ("rwkv_w0", 4), ("rwkv_a0", 4), ("rwkv_k_k", 4),
        ("rwkv_k_a", 4), ("rwkv_r_k", 4)]
VOFF = {}
NVEC = 0
for _n, _k in VECS:
    VOFF[_n] = NVEC
    NVEC += _k

LEVELS = [1, 2, 4, 8, 16, 32]


def constants():
    f = np.float32
    i = np.arange(P)
    r, c = i[:, None], i[None, :]
    out = {}
    out["ident"] = (r == c).astype(f)
    out["ones"] = np.ones((P, P), f)
    out["half_sign"] = np.where(r < HD, -1.0, 1.0).astype(f)
    out["eps"] = np.full((P, 1), EPS, f)
    out["gn_eps"] = np.full((P, 1), GN_EPS, f)
    out["half_pi"] = np.full((P, 1), math.pi / 2, f)
    def rope_perm(k_of):
        p = np.zeros((P, P), f)
        for m in range(P):
            j = m % HD
            if j < 8:
                p[k_of(m) + 8, m] = -1.0
            elif j < 16:
                p[k_of(m) - 8, m] = 1.0
        return p
    out["perm"] = rope_perm(lambda m: m)
    out["dup"] = (r == c % HD).astype(f)
    out["dup_perm"] = rope_perm(lambda m: m % HD)
    out["block_ones"] = (r // HD == c // HD).astype(f)
    out["earlier"] = (r < c).astype(f)
    half = 8
    inv = (np.float32(500000.0) ** (-np.arange(half, dtype=f) / half)).astype(f)
    ang = (np.arange(T, dtype=f)[:, None] * inv[None, :]).astype(f)
    cos, sin = np.ones((P, T), f), np.zeros((P, T), f)
    for m in range(P):
        j = m % HD
        if j < 16:
            cos[m], sin[m] = np.cos(ang[:, j % 8]), np.sin(ang[:, j % 8])
    out["cos"], out["sin"] = cos, sin
    k = np.arange(T)[None, :]
    for t in range(NT):
        out[f"causal{t}"] = np.where(k <= r + t * P, 0.0, NEG).astype(f)
    out["time"] = np.broadcast_to(np.arange(T, dtype=f), (P, T)).copy()
    same = r // CHUNK == c // CHUNK
    for m in LEVELS:
        out[f"level{m}"] = ((r // (2 * m) == c // (2 * m)) & (r // m > c // m)).astype(f)
    out["level1T"] = out["level1"].T.copy()
    out["before"] = ((r < c) & same).astype(f)
    out["upto"] = ((r <= c) & same).astype(f)
    out["restart"] = np.broadcast_to((np.arange(T) % CHUNK != 0).astype(f), (P, T)).copy()
    out["group"] = (r // C5 == np.arange(P // C5)[None, :]).astype(f)
    out["pair"] = (r // HD == np.arange(2)[None, :]).astype(f)
    out["item"] = np.broadcast_to(np.repeat(np.arange(ITEMS, dtype=f), NE), (P, ITEMS * NE)).copy()
    out["first"] = np.broadcast_to(np.eye(ITEMS, NE, dtype=f).reshape(-1), (P, ITEMS * NE)).copy()
    out["expert"] = np.broadcast_to(np.arange(NE, dtype=f), (P, NE)).copy()
    out["restart8"] = np.broadcast_to((np.arange(NT * NE) % NE != 0).astype(f), (P, NT * NE)).copy()
    return out


def const_layout():
    off, n = {}, 0
    for name, a in constants().items():
        off[name] = (n, a.shape[1])
        n += a.shape[1]
    return off, n


def block_list():
    out = [("e_w_in", c, FB) for c in range(0, 4 * MW, FB)]
    out += [("s5_glu_w", 0, MW), ("e_w_out", 0, FB), ("e_w_out", FB, FB)]
    ffn = [(c, min(FB, FFN - c)) for c in range(0, FFN, FB)]
    for n, (c, w) in enumerate(ffn):
        out += [("ffn_w_gate", c, w), ("ffn_w_up", c, w)]
        if n:
            out.append(("ffn_w_down", *ffn[n - 1]))
    out.append(("ffn_w_down", *ffn[-1]))
    out += [("o_w_in", c, min(FB, ODD_COLS - c)) for c in range(0, ODD_COLS, FB)]
    out += [("o_w_out", 0, FB), ("o_w_out", FB, FB)]
    return out


def trunk(nc, a, consts_dram, out):
    f32, i32 = mybir.dt.float32, mybir.dt.int32
    ALU, ACT, AX = mybir.AluOpType, mybir.ActivationFunctionType, mybir.AxisListType.X
    ADD, SUB, MUL = ALU.add, ALU.subtract, ALU.mult
    v, act_, pe_ = nc.vector, nc.scalar, nc.tensor
    ctx = ExitStack()

    def sb(name, cols, dt=f32, rows=P):
        return ctx.enter_context(nc.sbuf_tensor(name, [rows, cols], dt))

    sems = {}

    def sem(name):
        if name not in sems:
            sems[name] = ctx.enter_context(nc.semaphore(name))
        return sems[name]

    f32r = mybir.dt.float32r
    spans = [("ring", PAIR_SLOTS * KD * FB), ("ring2", (SLOTS - PAIR_SLOTS) * KD * FB), ("arena", ARENA), ("yT", KD * T)]
    with ExitStack() as views:
        ring_r, ring2_r, arena_r, yT_r = (views.enter_context(nc.sbuf_tensor(n + "_r", [P, w], f32r)) for n, w in spans)
    ring, ring2, arena, yT_flat = (sb(n, w) for n, w in spans)
    coff, ncon = const_layout()
    NFIRST = coff["perm"][0]
    con = sb("con", ncon)
    hT = sb("hT", KD * T)[:, :].rearrange("p (k t) -> p k t", k=KD)
    xnT = sb("xnT", KD * T)[:, :].rearrange("p (k t) -> p k t", k=KD)
    yT = yT_flat[:, :].rearrange("p (k t) -> p k t", k=KD)
    pcol = sb("pcol", NVEC)
    bank = [ctx.enter_context(nc.psum_tensor(f"bank{i}", [P, 512], f32)) for i in range(8)]

    def C(name):
        o, n = coff[name]
        return con[:, o:o + n]

    def col(name, i):
        return pcol[:, VOFF[name] + i:VOFF[name] + i + 1]

    def carve(base, start, sizes):
        got, at = {}, start
        for name, n in sizes:
            got[name] = base[:, at:at + n]
            at += n
        return got, at

    def slot(s, w=KD * FB):
        buf, at = (ring, s) if s < PAIR_SLOTS else (ring2, s - PAIR_SLOTS)
        return buf[:, at * KD * FB:at * KD * FB + w]

    L0, end = carve(arena, 0, [("uT", KM * T), ("qT", KM * T), ("kT", KM * T), ("V", NT * MW),
                               ("BT", 8 * P), ("CT", 8 * P), ("s5p", 4 * G5),
                               ("CW", 4 * 8 * (P + C5)), ("um", 4 * T), ("fr", 4 * T), ("pT", 512)])
    assert end <= ARENA, end
    free_slots = (5 - PAIR_SLOTS) * KD * FB
    pre, end = carve(ring2, free_slots, [("xtok", NT * D), ("vecs", P), ("Bx", 512), ("Bs", 512),
                                        ("Cx", 512), ("Cs", 512), ("M1", 512), ("M2", 512),
                                        ("mt", 512), ("small", 16 * P)])
    assert end <= (SLOTS - PAIR_SLOTS) * KD * FB
    s5w, end = carve(ring2, free_slots, [("rn", 2 * T), ("sn", 4 * T), ("cs", 4 * T), ("ta", 2 * T),
                                        ("tb", 2 * T), ("scan", 4 * T), ("oc", 4 * T), ("os", 4 * T)])
    assert end <= (SLOTS - PAIR_SLOTS) * KD * FB
    att, _ = carve(xnT.rearrange("p k t -> p (k t)"), 0, [("rope", 1024), ("p", 1024)])
    stat = sb("stat", 64)
    uT, qT, kT = (L0[n].rearrange("p (k t) -> p k t", k=KM) for n in ("uT", "qT", "kT"))
    V0 = L0["V"].rearrange("p (t c) -> p t c", t=NT)
    BT = L0["BT"].rearrange("p (m k c) -> p m k c", m=2, k=4)
    CT = L0["CT"].rearrange("p (m k c) -> p m k c", m=2, k=4)
    s5p = L0["s5p"].rearrange("p (q g) -> p q g", q=4)
    CW = L0["CW"].rearrange("p (b m x) -> p b m x", b=2, m=2)
    um = L0["um"].rearrange("p (b j t) -> p b j t", b=2, j=2)
    frac = L0["fr"].rearrange("p (b j t) -> p b j t", b=2, j=2)
    rn = s5w["rn"].rearrange("p (j t) -> p j t", j=2)
    sn, cs, scan, oc, os_ = (s5w[n].rearrange("p (b j t) -> p b j t", b=2, j=2)
                             for n in ("sn", "cs", "scan", "oc", "os"))
    ta, tb = (s5w[n].rearrange("p (j t) -> p j t", j=2) for n in ("ta", "tb"))
    xtok = pre["xtok"].rearrange("p (t d) -> p t d", t=NT)
    small = [pre["small"][0:G5, P * i:P * i + P] for i in range(16)]

    rstd = sb("rstd", T)
    gate_s, hprod = (arena[:, 2048 + 4 * T * i:2048 + 4 * T * i + 4 * T] for i in range(2))
    XLO = 14 * T + 8 * T + 2 * T + NT * HD + NT * 4
    xhi = yT_r[:, :].rearrange("p (k t) -> p k t", k=KD)
    xlo = arena_r[:, XLO:XLO + KD * T].rearrange("p (k t) -> p k t", k=KD)
    hhi, hlo = (arena_r[:, XLO + 2048 * i:XLO + 2048 * i + 2048].rearrange("p (b j t) -> p b j t", b=2, j=4)
                for i in (1, 2))
    assert XLO + 3 * 2048 <= ARENA

    nblocks = block_list()
    NB0 = len(nblocks)
    NFFN = 7
    NRAW = [n for n in range(NB0) if nblocks[n][0] == "o_w_in"][-1]
    NH0 = 2 * (NRAW - NFFN)
    slot_sem = [sem(f"slot{i}_loaded") for i in range(SLOTS)]
    slot_of = [n if n < NFFN else 3 + (n - NFFN) % 4 for n in range(NB0)]
    loads_of = [slot_of[:n + 1].count(slot_of[n]) for n in range(NB0)]
    used_when = [(sem("u_done"), 2)] + [(sem("proj_done"), 2 * n) for n in (1, 2, 3)]
    used_when += [(sem("z_done"), 2), (sem("into_h"), 2), (sem("into_h"), 4)]
    used_when += [(sem("lo_done"), 2 * (n - NFFN) + 2) for n in range(NFFN, NRAW)]
    used_when += [(sem("odd_proj"), 6), (sem("into_h"), 10), (sem("into_h"), 12)]

    def ss_bank(n):
        return bank[1 if n else 5][:, 0:T]

    H_ODD = NH0 - 10

    def odd_ready(i):
        if i == 10 or i % 2 == 0:
            return sem("odd_proj"), i // 2 + 1
        return sem("pair_used"), H_ODD + i + 1

    def pair(h, w=2048):
        o = (h % 3) * KD * FB
        return ring_r[:, o:o + w], ring_r[:, o + 2048:o + 2048 + w]

    def src_of(name, c, w):
        m = a[name][0]
        if "down" in name:
            return m[c:c + w, :].rearrange("(j p) n -> p j n", p=P)
        return m[:, c:c + w].rearrange("(k p) n -> p k n", p=P)

    def view(n):
        name, c, w = nblocks[n]
        k = src_of(name, c, w).shape[1]
        wid = src_of(name, c, w).shape[2]
        return slot(slot_of[n], k * wid).rearrange("p (k n) -> p k n", k=k)

    def raw_half(n, x):
        w = view(n)
        hk = w.shape[1] // 2
        return flat(w[:, x * hk:x * hk + hk, :])

    def half_parts(n, x):
        w = view(n)
        hk = w.shape[1] // 2
        return [p.rearrange("p (k n) -> p k n", k=hk) for p in pair(2 * (n - NFFN) + x, hk * w.shape[2])]

    def flat(ap):
        return ap.rearrange("p a b -> p (a b)")
    L1, end = carve(arena, 0, [("shift", 14 * T), ("draw", 8 * T), ("kd", T), ("kid", T), ("Vd", NT * HD),
                               ("wi", NT * 4), ("md", NT * T), ("acc", T), ("work", T), ("relu", 4 * T),
                               ("pT", 512), ("raw", 4 * (T + 1)), ("diff", 2 * T), ("top", 8),
                               ("WA", MW), ("GU", MW), ("lnw", MW), ("lnb", MW), ("rk", KM * T),
                               ("lam", KM * NCH), ("st8", 32)])
    assert end <= ARENA, end
    sc, end = carve(ring, 0, [("lw", KM * T), ("L", KM * T), ("Em", KM * T), ("KK", KM * T), ("A", KM * T),
                              ("AR", 2 * KM * T), ("tmp", KM * T), ("Vt", MW), ("Kt", MW), ("Bt", MW),
                              ("TT", HEADS * P), ("T", HEADS * P), ("G", MW)])
    assert end <= 3 * KD * FB
    sc6, end = carve(ring2, (6 - PAIR_SLOTS) * KD * FB, [("Z", HEADS * P), ("U", MW), ("S", MW), ("ya", MW), ("yb", MW),
                                         ("ds", MW)])
    assert end <= (SLOTS - PAIR_SLOTS) * KD * FB
    sc.update(sc6)
    shf = L1["shift"].rearrange("p (k t) -> p k t", k=14)
    draw = L1["draw"].rearrange("p (k t) -> p k t", k=8)
    raw = L1["raw"].rearrange("p (b k t) -> p b k t", b=2, k=2)
    Vd = L1["Vd"].rearrange("p (t c) -> p t c", t=NT)
    wi = L1["wi"].rearrange("p (t c) -> p t c", t=NT)
    md = L1["md"].rearrange("p (t c) -> p t c", t=NT)
    relu = L1["relu"].rearrange("p (h c) -> p h c", h=4)
    st8 = L1["st8"].rearrange("p (a h) -> p a h", a=4)
    lw, Lc, Em, KK, Ag, tmp4, rk = (x.rearrange("p (k t) -> p k t", k=KM) for x in (
        sc["lw"], sc["L"], sc["Em"], sc["KK"], sc["A"], sc["tmp"], L1["rk"]))
    AR = sc["AR"].rearrange("p (k m t) -> p k m t", k=KM, m=2)
    lam = L1["lam"].rearrange("p (k c) -> p k c", k=KM)
    MB = ring[:, 0:HEADS * 2 * P].rearrange("p (h m n) -> p h m n", h=HEADS, m=2)
    MK = ring[:, HEADS * 2 * P:2 * HEADS * 2 * P].rearrange("p (h m n) -> p h m n", h=HEADS, m=2)
    TT, Tm, Zm = (sc[n].rearrange("p (h n) -> p h n", h=HEADS) for n in ("TT", "T", "Z"))
    Sbd = sc["S"].rearrange("p (k n) -> p k n", k=KM)

    MO, end = carve(arena, 0, [("xtok", NT * D), ("htok", NT * D), ("onehot", NT * CAP),
                               ("gated", NT * CAP), ("gatedT", T), ("silu", FB), ("H", FB),
                               ("Y", D), ("gfin", D), ("router", KD * NE),
                               ("lg", NT * NE), ("e1", NT * NE), ("e2", NT * NE), ("t16", NT * NE),
                               ("sel", NT * NE), ("gate", NT * NE), ("rank", NT * NE), ("m12", 16),
                               ("cnt", 4 * NE), ("oh", ITEMS * NE), ("ohx", ITEMS * NE),
                               ("off", ITEMS * NE), ("offi", ITEMS), ("slotp", NT * (ITEMS + 1)), ("gatep", NT * ITEMS), ("ef", ITEMS + 1)])
    assert end <= ARENA, end
    work_list = sb("work_list", ITEMS + 1, i32)
    mtok = MO["xtok"].rearrange("p (t d) -> p t d", t=NT)
    htok = MO["htok"].rearrange("p (t d) -> p t d", t=NT)
    onehot = MO["onehot"].rearrange("p (t s) -> p t s", t=NT)
    gated = MO["gated"].rearrange("p (t s) -> p t s", t=NT)
    in6 = (6 - PAIR_SLOTS) * KD * FB
    xg = [ring2_r[:, in6 + KD * CAP * i:in6 + KD * CAP * i + KD * CAP].rearrange("p (k s) -> p k s", k=KD)
          for i in range(2)]
    in6 += 2 * KD * CAP
    ht = [ring2_r[:, in6 + FB * 2 * i:in6 + FB * 2 * i + FB * 2].rearrange("p (b j s) -> p b j s", b=2, j=4)
          for i in range(2)]
    router = MO["router"].rearrange("p (k e) -> p k e", k=KD)
    lg, e1, e2, t16, sel, gate, rank = (MO[n].rearrange("p (t e) -> p t e", t=NT) for n in (
        "lg", "e1", "e2", "t16", "sel", "gate", "rank"))
    slotp, gatep = (MO[n].rearrange("p (t i) -> p t i", t=NT) for n in ("slotp", "gatep"))
    NFC = FFE // FB
    expert_blocks = []
    for c_ in range(NFC):
        expert_blocks += [("moe_w_gate", c_), ("moe_w_up", c_)]
        if c_:
            expert_blocks.append(("moe_w_down", c_ - 1))
    expert_blocks.append(("moe_w_down", NFC - 1))
    NEB = len(expert_blocks)
    NHE = 2 * NEB
    EXPERT_SLOTS = [5, 3, 4]
    assert NEB % 3 == 0
    extra = arena[:, ARENA - KD * FB:]
    assert end <= ARENA - KD * FB

    def expert_place(j, peeled):
        if peeled and j == 3:
            return [extra[:, 0:2048], extra[:, 2048:4096]], sem("extra_loaded"), 1
        if peeled and j == 4:
            return [flat(hT), flat(xnT)], sem("extra2_loaded"), 2
        turn = j if peeled and j < 3 else j - 2
        s = EXPERT_SLOTS[turn % 3]
        return [slot(s)[:, 0:2048], slot(s)[:, 2048:4096]], slot_sem[s], slot_of.count(s) + turn // 3 + 1
    expert_steps = [({"moe_w_gate": "gate", "moe_w_up": "up", "moe_w_down": "down"}[n_], c_)
                    for n_, c_ in expert_blocks]

    def step_before(h):
        return expert_steps[h // 2 - 2] if h % 2 == 0 and h >= 4 else ("", 0)

    NB5 = G5 // 2
    fillers = [("proj", i) for i in range(6)] + [("rope", i) for i in range(4)] \
        + [("attn", u) for u in range(KM * NT + 2)]
    plan = []
    for b in range(NB5 + 1):
        plan.append(("s5", b))
        lo, hi = b * len(fillers) // NB5, min((b + 1) * len(fillers) // NB5, len(fillers))
        plan += fillers[lo:hi]
    ffn_steps = [({"ffn_w_gate": "gate", "ffn_w_up": "up", "ffn_w_down": "down"}[n_], c_ // FB)
                 for n_, c_, w_ in nblocks if n_.startswith("ffn")]
    UNITS = KM * NT

    def unit(u, base):
        return (u // NT, u % NT) if base == 0 else (u % KM, u // KM)

    SCALE = HD ** -0.5
    TWO_PI = 6.283185

    block = ctx.enter_context(nc.Block())

    @block.sync
    def _(sp):
        def s5_loads():
            s5_in = sem("s5_loaded")
            for i, name in enumerate(["s5_a_re", "s5_a_im"]):
                for half in range(2):
                    sp.dma_start(small[i][:, N5 * half:N5 * half + N5], a[name][0]).then_inc(s5_in, 16)
            sp.dma_start(small[2][:, 0:1], a["s5_log_dt"][0].rearrange("(g o) -> g o", o=1)).then_inc(s5_in, 16)
            for half, (nx, ns) in enumerate([("s5_b_re", "s5_b_im"), ("s5_b_im", "s5_b_re")]):
                rows = slice(N5 * half, N5 * half + N5)
                for dst, name in ((pre["Bx"], nx), (pre["Bs"], ns)):
                    sp.dma_start(dst[rows, :].rearrange("p (g c) -> p g c", c=C5),
                                  a[name][0].rearrange("g p c -> p g c")).then_inc(s5_in, 16)
            for half, (nx, ns) in enumerate([("s5_c_re", "s5_c_im"), ("s5_c_im", "s5_c_re")]):
                for dst, name in ((pre["Cx"], nx), (pre["Cs"], ns)):
                    sp.dma_start(dst.rearrange("p (k n) -> p k n", k=4)[:, :, N5 * half:N5 * half + N5],
                                  a[name][0].rearrange("(k g) c p -> (g c) k p", k=4)).then_inc(s5_in, 16)
            sp.dma_start(con[:, NFIRST:], consts_dram[:, NFIRST:]).then_inc(sem("all_consts_loaded"), 16)

        sp.dma_start(xtok, a["x"][0].rearrange("(t p) d -> p t d", p=P)).then_inc(sem("x_loaded"), 16)
        sp.dma_start(con[:, 0:NFIRST], consts_dram[:, 0:NFIRST]).then_inc(sem("consts_loaded"), 16)
        for n, (name, c, w) in enumerate(nblocks):
            if n == 0:
                sp.wait_ge(sem("vecs_loaded"), 16 * len(VECS))
            if n == 1:
                s5_loads()
            if n in (5, 6):
                sp.wait_ge(sem("s5_out"), NB5)
                sp.wait_ge(sem("y_used"), NB5)
            if loads_of[n] > 1:
                sp.wait_ge(*used_when[max(m for m in range(n) if slot_of[m] == slot_of[n])])
            sp.dma_start(view(n), src_of(name, c, w)).then_inc(slot_sem[slot_of[n]], 16)
        def load_block(e, j, peeled=False):
            name, c = expert_blocks[j]
            m = a[name][0]
            if name == "moe_w_down":
                src = m[bass.ds(e, 1), c * FB:c * FB + FB, :].rearrange("o (j p) n -> p (o j) n", p=P)
            else:
                src = m[bass.ds(e, 1), :, c * FB:c * FB + FB].rearrange("o (k p) n -> p (o k) n", p=P)
            k = src.shape[1]
            halves, loaded, count = expert_place(j, peeled)
            if peeled and j == 4:
                for x in range(2):
                    sp.dma_start(halves[x].rearrange("p (k n) -> p k n", k=k // 2),
                                 src[:, x * k // 2:(x + 1) * k // 2, :]).then_inc(loaded, 16)
            else:
                s = EXPERT_SLOTS[(j if peeled and j < 3 else j - 2) % 3]
                dst = extra if peeled and j == 3 else slot(s)
                sp.dma_start(dst.rearrange("p (k n) -> p k n", k=k), src).then_inc(loaded, 16)

        def load_expert(it, e):
            for j in range(NEB):
                sp.wait_ge(sem("lo_done"), NHE * it + NH0 + 2 * j - 4)
                load_block(e, j)

        sp.wait_ge(sem("lo_done"), NH0)
        load_block(0, 0, peeled=True)
        sp.wait_ge(sem("bonus_used"), NT)
        sp.wait_ge(sem("yc_copied"), NT)
        load_block(0, 3, peeled=True)
        for j in (1, 2):
            sp.wait_ge(*used_when[NRAW + j])
            load_block(0, j, peeled=True)
        sp.wait_ge(sem("htok_T"), 2 * NT)
        load_block(0, 4, peeled=True)
        for j in range(5, NEB):
            sp.wait_ge(sem("lo_done"), NH0 + 2 * (j - 5 if j < 8 else j - 3) + 2)
            load_block(0, j, peeled=True)
        with sp.Fori(1, NE) as it:
            load_expert(it, it)
        sp.wait_ge(sem("work_ready"), 1)
        n_items = sp.value_load(work_list[0:1, ITEMS:ITEMS + 1], min_val=NE, max_val=ITEMS)
        with sp.If(n_items > NE):
            with sp.Fori(NE, n_items) as it:
                load_expert(it, sp.value_load(work_list[0:1, bass.ds(it, 1)], min_val=0, max_val=NE - 1))
        sp.wait_ge(sem("y_final"), NT)
        sp.dma_start(out[0].rearrange("(t p) d -> p t d", p=P), htok).then_inc(sem("out_stored"), 16)
        sp.wait_ge(sem("out_stored"), 16)

    @block.gpsimd
    def _(pool):
        pl = nc.gpsimd
        pl.memset(L0["CW"], 0.0).then_inc(sem("cw_zero"), 1)
        pool.wait_ge(sem("all_consts_loaded"), 16)
        pool.wait_ge(sem("u_copied"), 2)
        chain = [0]

        def link(ins):
            chain[0] += 1
            ins.then_inc(sem("pool_chain"), 1)
            pool.wait_ge(sem("pool_chain"), chain[0])

        for b in range(NB5):
            if b >= 2:
                pool.wait_ge(sem("ab_done"), b - 1)
            for j in range(2):
                g = 2 * b + j
                last = pl.tensor_scalar(um[:, b % 2, j, :], uT[:, g // 8, :],
                                        C("group")[:, g % 8:g % 8 + 1], 1.0, MUL, MUL)
            last.then_inc(sem("um_ready"), 1)
            if b == 0:
                pool.wait_ge(sem("s5p_ready"), 1)
            if b >= 2:
                pool.wait_ge(sem("table_ready"), b - 1)
            for j in range(2):
                turns = s5p[:, 1, 2 * b + j:2 * b + j + 1]
                pl.tensor_scalar(frac[:, b % 2, j, :], C("time"), turns, 1.0, MUL, MUL)
                last = pl.tensor_scalar(rn[:, j, :], C("time"), turns, ROUND, MUL, ADD)
            link(last)
            link(pl.tensor_scalar(flat(rn), flat(rn), ROUND, 0.0, SUB, ADD))
            ins = pl.tensor_tensor(flat(frac[:, b % 2]), flat(frac[:, b % 2]), flat(rn), SUB)
            ins.then_inc(sem("frac_ready"), 1)
            pool.wait_ge(sem("frac_ready"), b + 1)

    @block.scalar
    def _(act):
        nv = 0
        for name, k in VECS:
            m = a[name][0]
            if len(m.shape) == 2:
                m = m.rearrange("h d -> (h d)")
            act.dma_start(pre["vecs"][nv:nv + k, :], m.rearrange("(n p) -> n p", p=P)).then_inc(
                sem("vecs_loaded"), 16)
            nv += k

        chain = [0]

        def link(ins):
            chain[0] += 1
            ins.then_inc(sem("act_chain"), 1)
            act.wait_ge(sem("act_chain"), chain[0])

        def norm(n, h_ready):
            for i in range(4):
                h_ready(i)
                act_.activation(flat(xnT[:, 2 * i:2 * i + 2, :]), flat(hT[:, 2 * i:2 * i + 2, :]),
                                ACT.Square).then_inc(sem("sq_done"), 1)
            act.wait_ge(sem("ss_done"), n + 1)
            act_.activation(rstd[:, :], ss_bank(n), ACT.Sqrt, scale=1.0 / D, bias=C("eps")).then_inc(
                sem("rms_done"), 1)

        def h0(i):
            if i >= 2:
                act.wait_ge(sem("x_T"), 1 + i)
                act_.activation(flat(hT[:, 2 * i:2 * i + 2, :]), bank[1 + i][:, :], ACT.Copy).then_inc(
                    sem("x_copied_act"), 1)
                act.wait_ge(sem("x_copied_act"), i - 1)
            else:
                act.wait_ge(sem("x_copied"), i + 1)
        act.wait_ge(sem("consts_loaded"), 16)
        norm(0, h0)
        for i in range(2):
            act.wait_ge(sem("u_done"), i + 1)
            act_.activation(flat(uT[:, 2 * i:2 * i + 2, :]), bank[i][:, :], ACT.Copy).then_inc(
                sem("u_copied"), 1)
        act.wait_ge(sem("all_consts_loaded"), 16)
        act.wait_ge(sem("s5_angle"), 1)
        act_.activation(small[6], small[5], ACT.Sin, scale=TWO_PI)
        act_.activation(small[7], small[5], ACT.Sin, scale=TWO_PI / 2).then_inc(sem("s5_sin"), 1)

        def tables(b):
            act.wait_ge(sem("frac_ready"), b + 1)
            if b == 0:
                act.wait_ge(sem("bbar_done"), 1)
            if b >= 2:
                act.wait_ge(sem("s5_out"), b - 1)
            act_.activation(flat(sn[:, b % 2]), flat(frac[:, b % 2]), ACT.Sin, scale=TWO_PI)
            link(act_.activation(flat(frac[:, b % 2]), flat(frac[:, b % 2]), ACT.Abs))
            act_.activation(flat(cs[:, b % 2]), flat(frac[:, b % 2]), ACT.Sin, scale=-TWO_PI,
                            bias=C("half_pi")).then_inc(sem("table_ready"), 1)

        def attention(u, base, p, pT, o_dst):
            if u >= 2:
                act.wait_ge(sem("pv_done"), base + u - 1)
                act_.activation(o_dst(u - 2), bank[7][:, 0:P], ACT.Copy).then_inc(sem("o_copied"), 1)
            if u < UNITS:
                nk = P * (unit(u, base)[1] + 1)
                act.wait_ge(sem("nb_ready"), base + u + 1)
                for j in range(2):
                    s = 2 * (u % 2) + j
                    last = act_.activation(p[:, u % 2, j, 0:nk], p[:, u % 2, j, 0:nk], ACT.Exp, scale=SCALE,
                                           bias=stat[:, 8 + s:9 + s], accum_out=stat[:, 16 + s:17 + s])
                last.then_inc(sem("exp_done"), 1)
            if 1 <= u <= UNITS:
                act.wait_ge(sem("pt_done"), base + u)
                n = 2 * P * (unit(u - 1, base)[1] + 1)
                act_.activation(pT[:, 0:n], bank[7][:, 0:n], ACT.Copy).then_inc(sem("pt_copied"), 1)

        p0 = att["p"].rearrange("p (b j n) -> p b j n", b=2, j=2)
        tables(0)
        for what, i in plan:
            if what == "s5" and i + 1 < NB5:
                tables(i + 1)
            elif what == "proj":
                act.wait_ge(sem("proj_done"), i + 1)
                dst = [flat(qT[:, 0:2]), flat(qT[:, 2:4]), flat(kT[:, 0:2]), flat(kT[:, 2:4]),
                       V0[:, 0, :], V0[:, 1, :]][i]
                act_.activation(dst, bank[5 + i % 3][:, :], ACT.Copy).then_inc(sem("proj_copied"), 1)
            elif what == "attn":
                attention(i, 0, p0, L0["pT"], lambda w: yT[:, KM + w // NT, w % NT * P:w % NT * P + P])
        act.wait_ge(sem("y_added"), 4)
        act_.activation(flat(yT[:, 0:KM]), flat(yT[:, 0:KM]), ACT.Gelu_apprx_tanh).then_inc(sem("gelu_done"), 1)
        for m in range(KM):
            if m % 2 == 0:
                act.wait_ge(sem("z_done"), m // 2 + 1)
            last = act_.activation(L0["um"][:, T * m:T * m + T], bank[m // 2][:, (m % 2) * T:(m % 2) * T + T],
                                   ACT.Sigmoid, bias=col("s5_glu_b", m))
        last.then_inc(sem("glu_gate"), 1)

        def split_hi(n, x):
            h = 2 * (n - NFFN) + x
            act.wait_ge(slot_sem[slot_of[n]], 16 * loads_of[n])
            if h >= 3:
                act.wait_ge(sem("pair_used"), h - 2)
            src = raw_half(n, x)
            act_.activation(pair(h, src.shape[1])[0], src, ACT.Copy).then_inc(sem("hi_done"), 1)

        def split_xn(m):
            for i in range(2):
                act.wait_ge(sem("xn_done"), 2 * m + i + 1)
                act_.activation(flat(xhi[:, 4 * i:4 * i + 4, :]), flat(xnT[:, 4 * i:4 * i + 4, :]), ACT.Copy).then_inc(
                    sem("xhi_done"), 1)

        act.wait_ge(sem("proj_done"), 6)
        for h in range(3):
            split_hi(NFFN + h // 2, h % 2)
        norm(1, lambda i: act.wait_ge(sem("h_added"), i + 1))
        split_xn(1)
        for h in range(3, 2 * len(ffn_steps) + 3):
            kind, c = ffn_steps[(h - 4) // 2] if h >= 4 and h % 2 == 0 else ("", 0)
            if kind == "gate":
                w = min(FB, FFN - c * FB) // P
                act.wait_ge(sem("pair_used"), h - 2)
                if c:
                    act.wait_ge(sem("hprod_done"), c)
                for i in range(w // 2):
                    last = act_.activation(gate_s[:, 512 * i:512 * i + 512], bank[i][:, :], ACT.Silu)
                last.then_inc(sem("silu_done"), 1)
            kind, c = ffn_steps[(h - 5) // 2] if h >= 5 and h % 2 == 1 else ("", 0)
            if kind == "up":
                w = min(FB, FFN - c * FB) // P
                act.wait_ge(sem("hprod_done"), c + 1)
                if c >= 2:
                    act.wait_ge(sem("pair_used"), 2 * ffn_steps.index(("down", c - 2)) + 2)
                act_.activation(flat(hhi[:, c % 2, 0:w]), hprod[:, 0:w * T], ACT.Copy).then_inc(sem("hhi_done"), 1)
            if h < 2 * len(ffn_steps) + 2:
                split_hi(NFFN + h // 2, h % 2)

        norm(2, lambda i: act.wait_ge(sem("h_added"), 5 + i))
        for dst, name in ((L1["WA"][0:64, :], "rwkv_w_up"), (L1["WA"][64:128, :], "rwkv_a_up"),
                          (L1["GU"], "rwkv_g_up")):
            act.dma_start(dst, a[name][0]).then_inc(sem("lora_loaded"), 16)
        for dst, name in ((L1["lnw"], "rwkv_ln_w"), (L1["lnb"], "rwkv_ln_b")):
            act.dma_start(dst, a[name][0:1, :].to_broadcast([P, MW])).then_inc(sem("lora_loaded"), 16)
        split_hi(NRAW - 4, 0)
        split_xn(2)

        def odd_copy(i):
            act.wait_ge(*odd_ready(i))
            b = bank[i % 8]
            if i < 7:
                if i >= 2:
                    act.wait_ge(sem("shifted"), i - 1)
                else:
                    act.wait_ge(sem("raw_zero"), 1)
                ins = act_.activation(raw[:, i % 2, :, 1:T + 1], b[:, :].rearrange("p (k t) -> p k t", k=2), ACT.Copy)
            elif i < 10:
                ins = act_.activation(flat(draw[:, 2 * i - 14:2 * i - 12, :]), b[:, :], ACT.Copy)
            else:
                act_.activation(draw[:, 6, :], b[:, 0:T], ACT.Copy)
                ins = act_.activation(draw[0:HD + 4, 7, :], b[0:HD + 4, T:2 * T], ACT.Copy)
            ins.then_inc(sem("odd_copied"), 1)

        for m in range(5):
            if m < 4:
                split_hi(NFFN + (H_ODD + 2 * m + 3) // 2, (H_ODD + 2 * m + 3) % 2)
            odd_copy(2 * m)
            odd_copy(2 * m + 1)
            if m < 3:
                split_hi(NFFN + (H_ODD + 2 * m + 4) // 2, (H_ODD + 2 * m + 4) % 2)
        odd_copy(10)
        act.wait_ge(sem("shifted"), 7)
        act_.activation(shf[0:64, 12, :], shf[0:64, 12, :], ACT.Tanh).then_inc(sem("lora_in"), 1)
        act_.activation(shf[:, 13, :], shf[:, 13, :], ACT.Sigmoid).then_inc(sem("lora_in"), 1)
        for t in range(NT):
            act.wait_ge(sem("kv_T"), t + 1)
            act_.activation(Vd[:, t, :], bank[2 + t][:, HD:2 * HD], ACT.Copy)
            act_.activation(wi[:, t, :], bank[2 + t][:, P + HD:P + HD + 4], ACT.Copy,
                            scale=4 ** -0.5 * HD ** -0.5).then_inc(sem("kv_copied"), 1)
        for t in range(NT):
            nk = P * (t + 1)
            act.wait_ge(sem("idx_done"), t + 1)
            if t:
                act.wait_ge(sem("acc_done"), t)
            for j in range(2):
                last = act_.activation(relu[:, j::2, 0:nk], bank[4 + j][:, :].rearrange(
                    "p (h n) -> p h n", h=2)[:, :, 0:nk], ACT.Relu)
            last.then_inc(sem("relu_done"), 1)
        act.wait_ge(sem("lora_done"), 1)
        for k in range(KM):
            act_.activation(lw[:, k, :], bank[k // 2][:, (k % 2) * T:(k % 2) * T + T], ACT.Sigmoid,
                            bias=col("rwkv_w0", k))
            last = act_.activation(Ag[:, k, :], bank[2 + k // 2][:, (k % 2) * T:(k % 2) * T + T], ACT.Sigmoid,
                                   bias=col("rwkv_a0", k))
        last.then_inc(sem("gates_done"), 1)

        def rwkv_step(u):
            if u == 1:
                act.wait_ge(sem("kk_raw"), 1)
                act_.activation(flat(tmp4), flat(KK), ACT.Square).then_inc(sem("kk_sq"), 1)
            elif u == 2:
                act.wait_ge(sem("L_done"), 1)
                act_.activation(flat(Em), flat(Lc), ACT.Exp, scale=-DECAY)
                act_.activation(flat(Lc), flat(Lc), ACT.Exp, scale=DECAY)
                act_.activation(flat(lw), flat(lw), ACT.Exp, scale=DECAY).then_inc(sem("exps_done"), 1)
            elif u == 3:
                act.wait_ge(sem("kk_ss"), 1)
                act_.activation(L1["st8"][:, 0:16], bank[0][:, 0:16], ACT.Sqrt).then_inc(sem("kk_norm"), 1)
            elif u == 4:
                act.wait_ge(sem("kk_inv"), 1)
                act_.activation(sc["tmp"].rearrange("p (i d) -> p i d", d=HD),
                                L1["st8"][:, 0:16][:, :, None].to_broadcast([P, 16, HD]), ACT.Copy).then_inc(
                    sem("kk_wide"), 1)

        for u in range(UNITS + 2):
            attention(u, UNITS, p0, L1["pT"], lambda w: yT[:, KM + w % KM, w // KM * P:w // KM * P + P])
            rwkv_step(u)
        for t in range(NT):
            act.wait_ge(sem("tok_T"), t + 1)
            if t:
                act.wait_ge(sem("bonus_used"), t)
            for i, n in enumerate(("Vt", "Kt", "Bt")):
                last = act_.activation(sc[n], bank[i][:, :], ACT.Copy)
            last.then_inc(sem("tok_copied"), 1)
            for ci in range(2):
                c, R = 2 * t + ci, slice(CHUNK * ci, CHUNK * ci + CHUNK)
                act.wait_ge(sem("G_done"), c + 1)
                act_.activation(sc["G"][R, :], bank[6][R, :], ACT.Copy).then_inc(sem("G_copied"), 1)
                act.wait_ge(sem("U_done"), c + 1)
                act_.activation(sc["U"][R, :], bank[7][R, :], ACT.Copy).then_inc(sem("U_copied"), 1)
            act.wait_ge(sem("gn_var"), t + 1)
            act_.activation(st8[:, 2, :], st8[:, 1, :], ACT.Sqrt, scale=1.0 / HD, bias=C("gn_eps")).then_inc(
                sem("gn_std"), 1)
            act.wait_ge(sem("yc_T"), t + 1)
            act_.activation(yT[:, 0:KM, t * P:t * P + P], bank[2][:, :].rearrange("p (k n) -> p k n", k=KM),
                            ACT.Copy).then_inc(sem("yc_copied"), 1)

        def expert_hi(it, h):
            halves, loaded, count = expert_place(h // 2, type(it) is int)
            act.wait_ge(loaded, 16 * (NEB // 3) * it + 16 * count)
            act.wait_ge(sem("pair_used"), NHE * it + NH0 + h - 2)
            act_.activation(pair(NH0 + h)[0], halves[h % 2], ACT.Copy).then_inc(sem("hi_done"), 1)

        act.dma_start(router, a["moe_router"][0].rearrange("(k p) e -> p k e", p=P)).then_inc(
            sem("router_loaded"), 16)
        act.dma_start(MO["gfin"], a["final_norm"].rearrange("(o d) -> o d", o=1).to_broadcast([P, D])).then_inc(
            sem("gfin_loaded"), 16)
        expert_hi(0, 0)
        expert_hi(0, 1)
        norm(3, lambda i: act.wait_ge(sem("h_added"), 9 + i))
        expert_hi(0, 2)
        act.wait_ge(sem("m12_done"), 1)
        act_.activation(MO["m12"][:, 4:6], MO["m12"][:, 2:4], ACT.Exp).then_inc(sem("m12_exp"), 1)
        for t in range(NT):
            for i in range(2):
                act.wait_ge(sem("xtok_T"), 2 * t + i + 1)
                act_.activation(mtok[:, t, 512 * i:512 * i + 512], bank[i][:, :], ACT.Copy).then_inc(
                    sem("xtok_copied"), 1)
        for t in range(NT):
            for i in range(2):
                act.wait_ge(sem("htok_T"), 2 * t + i + 1)
                act_.activation(htok[:, t, 512 * i:512 * i + 512], bank[2 + i][:, :], ACT.Copy).then_inc(
                    sem("htok_copied"), 1)
        def gather_hi():
            for i in range(2):
                last = act_.activation(flat(xg[0][:, 4 * i:4 * i + 4, :]), bank[6 + i][:, :], ACT.Copy)
            last.then_inc(sem("xg_hi"), 1)

        act.wait_ge(sem("work_ready"), 1)
        act.wait_ge(sem("gather_done"), 1)
        gather_hi()

        def run_item(it, peeled=False):
            for h in range(NHE):
                if h == 3 and not peeled:
                    act.wait_ge(sem("pair_used"), NHE * it + NH0)
                    for i in range(2):
                        last = act_.activation(MO["Y"][:, 512 * i:512 * i + 512], bank[4 + i][:, :], ACT.Copy)
                    last.then_inc(sem("Y_copied"), 1)
                kind, c = step_before(h)
                if kind == "gate":
                    act.wait_ge(sem("pair_used"), NHE * it + NH0 + h - 2)
                    act.wait_ge(sem("H_done"), NFC * it + NFC + c)
                    act_.activation(MO["silu"], bank[0][:, :], ACT.Silu).then_inc(sem("moe_silu"), 1)
                if (kind == "gate" and c) or h == NHE - 2:
                    c = c if kind == "gate" else NFC
                    act.wait_ge(sem("HT_done"), NFC * it + c)
                    act_.activation(flat(ht[0][:, (c - 1) % 2]), bank[2][:, :], ACT.Copy).then_inc(sem("ht_hi"), 1)
                if h >= 3 or not peeled:
                    expert_hi(it, h)
                if h == NHE - 2:
                    act.wait_ge(sem("gather_done"), it + 2)
                    gather_hi()
                    act.wait_ge(sem("gatedT_done"), it + 1)
                    act_.activation(MO["gatedT"], bank[3][:, 0:T], ACT.Copy).then_inc(sem("gatedT_copied"), 1)

        act.sem_inc(sem("Y_copied"), 1)
        run_item(0, peeled=True)
        n_items = act.value_load(work_list[0:1, ITEMS:ITEMS + 1], min_val=NE, max_val=ITEMS)
        with act.Fori(1, n_items) as it:
            run_item(it)
        act.wait_ge(sem("pair_used"), NHE * n_items + NH0)
        for i in range(2):
            last = act_.activation(MO["Y"][:, 512 * i:512 * i + 512], bank[4 + i][:, :], ACT.Copy)
        last.then_inc(sem("Y_copied"), 1)
        act.wait_ge(sem("acc_final"), 1)
        for t in range(NT):
            last = act_.activation(MO["xtok"][:, t * D:t * D + D], htok[:, t, :], ACT.Square,
                                   accum_out=MO["m12"][:, 8 + t:9 + t])
        link(last)
        act_.activation(MO["m12"][:, 10:12], MO["m12"][:, 8:10], ACT.Sqrt, scale=1.0 / D, bias=C("eps")).then_inc(
            sem("final_rms"), 1)

    @block.vector
    def _(dve):
        chain = [0]

        def link(ins):
            chain[0] += 1
            ins.then_inc(sem("dve_chain"), 1)
            dve.wait_ge(sem("dve_chain"), chain[0])

        for i in range(2):
            dve.wait_ge(sem("x_T"), i + 1)
            v.tensor_copy(flat(hT[:, 2 * i:2 * i + 2, :]), bank[1 + i][:, :]).then_inc(sem("x_copied"), 1)
        dve.wait_ge(sem("vecs_T"), 1)
        link(v.tensor_copy(pcol[:, :], bank[0][:, 0:NVEC]))

        def norm(n, gname):
            dve.wait_ge(sem("rms_done"), n + 1)
            link(v.reciprocal(rstd[:, :], rstd[:, :]))
            for k in range(KD):
                last = v.scalar_tensor_tensor(xnT[:, k, :], hT[:, k, :], col(gname, k), rstd[:, :], MUL, MUL)
                if k % 4 == 3:
                    last.then_inc(sem("xn_done"), 1)

        norm(0, "e_norm_mix")

        dve.wait_ge(sem("s5_loaded"), 16 * 13)
        dve.wait_ge(sem("all_consts_loaded"), 16)

        def exp_parts(x, pm1, s, k, r):
            link(v.tensor_scalar(k, x, 1.0 / math.log(2), ROUND, MUL, ADD))
            link(v.tensor_scalar(k, k, ROUND, -126.0, SUB, ALU.max))
            link(v.tensor_scalar(k, k, 127.0, None, ALU.min))
            link(v.scalar_tensor_tensor(r, k, -0.693359375, x, MUL, ADD))
            link(v.scalar_tensor_tensor(r, k, 2.12194440e-4, r, MUL, ADD))
            link(v.tensor_scalar(pm1, r, 1.0 / math.factorial(8), None, MUL))
            for n in range(7, 0, -1):
                link(v.scalar_tensor_tensor(pm1, pm1, 1.0 / math.factorial(n), r, ADD, MUL))
            link(v.tensor_scalar(k, k, 127.0, float(2 ** 23), ADD, MUL))
            link(v.tensor_copy(s.bitcast(i32), k))

        ar, ai, dts, em, mag, fr_, sn_, hs, cs_, xi, den, tmp, fre, fim, t14, t15 = small
        dt = dts[:, 1:2]
        exp_parts(dts[:, 0:1], dt, dts[:, 2:3], dts[:, 3:4], dts[:, 4:5])
        link(v.scalar_tensor_tensor(dt, dt, 1.0, dts[:, 2:3], ADD, MUL))
        link(v.tensor_scalar(t14, ar, dt, None, MUL))
        exp_parts(t14, em, mag, tmp, t15)
        link(v.tensor_tensor(em, em, mag, MUL))
        link(v.scalar_tensor_tensor(em, mag, -1.0, em, ADD, ADD))
        link(v.tensor_scalar(mag, em, 1.0, None, ADD))
        link(v.tensor_scalar(t14, ai, dt, 1.0 / (2 * math.pi), MUL, MUL))
        link(v.tensor_scalar(t15, t14, ROUND, ROUND, ADD, SUB))
        v.tensor_tensor(fr_, t14, t15, SUB).then_inc(sem("s5_angle"), 1)
        v.tensor_tensor(den, ar, ar, MUL)
        link(v.tensor_tensor(tmp, ai, ai, MUL))
        link(v.tensor_tensor(den, den, tmp, ADD))
        link(v.reciprocal(den, den))
        dve.wait_ge(sem("s5_sin"), 1)
        link(v.scalar_tensor_tensor(hs, hs, -2.0, hs, MUL, MUL))
        link(v.tensor_scalar(cs_, hs, 1.0, None, ADD))
        v.tensor_tensor(xi, mag, sn_, MUL)
        link(v.tensor_tensor(tmp, em, cs_, MUL))
        link(v.tensor_tensor(cs_, tmp, hs, ADD))
        v.tensor_tensor(t14, cs_, ar, MUL)
        v.tensor_tensor(t15, xi, ai, MUL)
        v.tensor_tensor(fre, xi, ar, MUL)
        link(v.tensor_tensor(fim, cs_, ai, MUL))
        link(v.tensor_tensor(t14, t14, t15, ADD))
        link(v.tensor_tensor(t15, fre, fim, SUB))
        v.tensor_tensor(fre, t14, den, MUL)
        v.tensor_tensor(fim, t15, den, MUL).then_inc(sem("s5_params"), 1)
        dve.wait_ge(sem("s5_params_T"), 1)
        v.tensor_copy(flat(s5p), bank[7][:, 0:4 * G5]).then_inc(sem("s5p_ready"), 1)
        dve.wait_ge(sem("s5p_ready"), 1)
        def gc(x):
            return x.rearrange("p (g c) -> p g c", c=C5)
        F_re = s5p[:, 2, :][:, :, None].to_broadcast([P, G5, C5])
        F_im = s5p[:, 3, :][:, :, None].to_broadcast([P, G5, C5])
        link(v.tensor_scalar(pre["Bs"], pre["Bs"], C("half_sign"), None, MUL))
        v.tensor_tensor(gc(pre["M1"]), gc(pre["Bx"]), F_re, MUL)
        v.tensor_tensor(gc(pre["M2"]), gc(pre["Bx"]), F_im, MUL)
        link(v.tensor_tensor(gc(pre["mt"]), gc(pre["Bs"]), F_im, MUL))
        link(v.tensor_tensor(gc(pre["Bs"]), gc(pre["Bs"]), F_re, MUL))
        v.tensor_tensor(pre["M1"], pre["M1"], pre["mt"], ADD)
        v.tensor_tensor(pre["M2"], pre["M2"], pre["Bs"], SUB).then_inc(sem("bbar_done"), 1)
        dve.wait_ge(sem("c_T"), 1)
        v.tensor_scalar(flat(CT[:, 0]), bank[2][:, :], C("half_sign"), -1.0, MUL, MUL)
        v.tensor_scalar(flat(CT[:, 1]), bank[3][:, :], -1.0, None, MUL).then_inc(sem("c_copied"), 1)
        dve.wait_ge(sem("bbar_T"), 1)
        v.tensor_copy(flat(BT[:, 0]), bank[5][:, :])
        v.tensor_copy(flat(BT[:, 1]), bank[6][:, :]).then_inc(sem("prep_done"), 1)

        def c_weights(k):
            if k == 0:
                dve.wait_ge(sem("cw_zero"), 1)
                dve.wait_ge(sem("c_copied"), 1)
            if k >= 2:
                dve.wait_ge(sem("y_used"), 4 * (k - 1))
            for m in range(2):
                last = v.tensor_copy(CW[:, k % 2, m, :].rearrange("p (g x) -> p g x", x=P + C5)[:, :, 0:C5],
                                     CT[:, m, k, :].rearrange("p (g c) -> p g c", c=C5))
            last.then_inc(sem("cw_ready"), 1)

        def scans(b):
            A, B = bank[2 * (b % 2)], bank[2 * (b % 2) + 1]
            dve.wait_ge(sem("ab_done"), b + 1)
            dve.wait_ge(sem("table_ready"), b + 1)
            v.tensor_tensor(flat(ta), A[:, :], flat(cs[:, b % 2]), MUL)
            v.tensor_tensor(flat(tb), B[:, :], flat(sn[:, b % 2]), MUL).then_inc(sem("ab_read"), 1)
            dve.wait_ge(sem("ab_read"), b + 1)
            link(v.tensor_tensor(flat(ta), flat(ta), flat(tb), ADD))
            for j in range(2):
                g = 2 * b + j
                last = v.tensor_tensor_scan(scan[:, b % 2, j, :], s5p[:, 0, g:g + 1].to_broadcast([P, T]),
                                            ta[:, j, :], 0.0, MUL, ADD)
            link(last)
            if b >= 2:
                dve.wait_ge(sem("y_used"), b - 1)
            v.tensor_tensor(flat(oc[:, b % 2]), flat(scan[:, b % 2]), flat(cs[:, b % 2]), MUL)
            v.tensor_tensor(flat(os_[:, b % 2]), flat(scan[:, b % 2]), flat(sn[:, b % 2]), MUL).then_inc(
                sem("s5_out"), 1)

        def softmax(u, base, p, mask, first):
            if 1 <= u <= UNITS:
                w, nk = u - 1, P * (unit(u - 1, base)[1] + 1)
                s = 2 * (w % 2)
                dve.wait_ge(sem("exp_done"), base + w + 1)
                link(v.reciprocal(stat[:, 24 + s:26 + s], stat[:, 16 + s:18 + s]))
                for j in range(2):
                    last = v.tensor_scalar(p[:, w % 2, j, 0:nk], p[:, w % 2, j, 0:nk],
                                           stat[:, 24 + s + j:25 + s + j], None, MUL)
                last.then_inc(sem("p_ready"), 1)
            if u < UNITS:
                nk, s = P * (unit(u, base)[1] + 1), 2 * (u % 2)
                dve.wait_ge(sem("sc_done"), base + u + 1)
                if u >= 2:
                    dve.wait_ge(sem("pt_done"), base + u - 1)
                for j in range(2):
                    last = v.tensor_tensor(p[:, u % 2, j, 0:nk], bank[5 + j][:, 0:nk], mask(u)[:, 0:nk], ADD)
                last.then_inc(sem("sc_read"), 1)
                dve.wait_ge(sem("sc_read"), base + u + 1)
                link(v.tensor_reduce(stat[:, s:s + 2], p[:, u % 2, :, 0:nk], AX, ALU.max))
                v.tensor_scalar(stat[:, 8 + s:10 + s], stat[:, s:s + 2], -SCALE, None, MUL).then_inc(
                    sem("nb_ready"), 1)

        def rope(x, pb, tmp, done):
            n = x.shape[1]
            cosb = C("cos")[:, None, :].to_broadcast([P, n, T])
            sinb = C("sin")[:, None, :].to_broadcast([P, n, T])
            v.tensor_tensor(tmp.rearrange("p (k t) -> p k t", k=n),
                            pb.rearrange("p (k t) -> p k t", k=n), sinb, MUL)
            link(v.tensor_tensor(x, x, cosb, MUL))
            v.tensor_tensor(x, x, tmp.rearrange("p (k t) -> p k t", k=n), ADD).then_inc(done, 1)

        p0 = att["p"].rearrange("p (b j n) -> p b j n", b=2, j=2)
        c_weights(0)
        c_weights(1)
        for what, i in plan:
            if what == "s5":
                if i < NB5:
                    scans(i)
                if i % 4 == 0 and i:
                    k = i // 4 - 1
                    dve.wait_ge(sem("y_used"), i)
                    v.scalar_tensor_tensor(yT[:, k, :], uT[:, k, :], col("s5_d", k), bank[4][:, 0:T],
                                           MUL, ADD).then_inc(sem("y_added"), 1)
                if i in (7, 11):
                    c_weights((i + 1) // 4)
            elif what == "rope":
                x = (qT, kT)[i // 2][:, 2 * (i % 2):2 * (i % 2) + 2, :]
                dve.wait_ge(sem("rope_P"), i + 1)
                rope(x, bank[5 + i % 3][:, :], att["rope"][:, 512 * (i % 2):512 * (i % 2) + 512], sem("rope_done"))
            elif what == "attn":
                softmax(i, 0, p0, lambda u: C(f"causal{u % NT}"), None)
        dve.wait_ge(sem("glu_gate"), 1)
        v.tensor_tensor(flat(yT[:, 0:KM]), flat(yT[:, 0:KM]), L0["um"], MUL).then_inc(sem("glu_done"), 1)

        def add_h(i, b, n):
            dve.wait_ge(sem("into_h"), n)
            v.tensor_tensor(flat(hT[:, 2 * i:2 * i + 2, :]), flat(hT[:, 2 * i:2 * i + 2, :]), b[:, :],
                            ADD).then_inc(sem("h_added"), 1)

        def split_lo(n, x):
            h = 2 * (n - NFFN) + x
            dve.wait_ge(sem("hi_done"), h + 1)
            src = raw_half(n, x)
            hi, lo = pair(h, src.shape[1])
            v.tensor_tensor(lo, src, hi.bitcast(f32), SUB).then_inc(sem("lo_done"), 1)

        def split_xn(m):
            for i in range(2):
                dve.wait_ge(sem("xhi_done"), 2 * m - 2 + i + 1)
                v.tensor_tensor(flat(xlo[:, 4 * i:4 * i + 4, :]), flat(xnT[:, 4 * i:4 * i + 4, :]),
                                flat(xhi[:, 4 * i:4 * i + 4, :]).bitcast(f32), SUB).then_inc(sem("xlo_done"), 1)

        for h in range(3):
            split_lo(NFFN + h // 2, h % 2)
        for i in range(4):
            add_h(i, bank[2 + i], i + 1)
        norm(1, "e_norm_ffn")
        split_xn(1)
        for h in range(3, 2 * len(ffn_steps) + 3):
            kind, c = ffn_steps[(h - 4) // 2] if h >= 4 and h % 2 == 0 else ("", 0)
            if kind == "up":
                w = min(FB, FFN - c * FB) // P
                dve.wait_ge(sem("silu_done"), c + 1)
                dve.wait_ge(sem("pair_used"), h - 2)
                if c:
                    dve.wait_ge(sem("hlo_done"), c)
                for i in range(w // 2):
                    last = v.tensor_tensor(hprod[:, 512 * i:512 * i + 512], gate_s[:, 512 * i:512 * i + 512],
                                           bank[2 + i][:, :], MUL)
                last.then_inc(sem("hprod_done"), 1)
            kind, c = ffn_steps[(h - 5) // 2] if h >= 5 and h % 2 == 1 else ("", 0)
            if kind == "up":
                w = min(FB, FFN - c * FB) // P
                dve.wait_ge(sem("hprod_done"), c + 1)
                dve.wait_ge(sem("hhi_done"), c + 1)
                v.tensor_tensor(flat(hlo[:, c % 2, 0:w]), hprod[:, 0:w * T], flat(hhi[:, c % 2, 0:w]).bitcast(f32),
                                SUB).then_inc(sem("hlo_done"), 1)
            if h < 2 * len(ffn_steps) + 2:
                split_lo(NFFN + h // 2, h % 2)
        for i in range(4):
            add_h(i, bank[4 + i], 5 + i)

        norm(2, "o_norm_mix")
        split_lo(NRAW - 4, 0)
        split_xn(2)
        v.memset(raw[:, :, :, 0:1].rearrange("p b k o -> p (b k o)"), 0.0).then_inc(sem("raw_zero"), 1)
        dve.wait_ge(sem("raw_zero"), 1)

        def shift(i):
            dve.wait_ge(sem("odd_copied"), i + 1)
            x = raw[:, i % 2]
            if i:
                dve.wait_ge(sem("shifted"), i)
            link(v.tensor_tensor(L1["diff"].rearrange("p (k t) -> p k t", k=2), x[:, :, 0:T], x[:, :, 1:T + 1], SUB))
            for k in range(2):
                last = v.scalar_tensor_tensor(shf[:, 2 * i + k, :], L1["diff"][:, k * T:k * T + T],
                                              col("rwkv_mu", 2 * i + k), x[:, k, 1:T + 1], MUL, ADD)
            last.then_inc(sem("shifted"), 1)

        for m in range(4):
            split_lo(NFFN + (H_ODD + 2 * m + 3) // 2, (H_ODD + 2 * m + 3) % 2)
            shift(2 * m)
            if m < 3:
                shift(2 * m + 1)
                split_lo(NFFN + (H_ODD + 2 * m + 4) // 2, (H_ODD + 2 * m + 4) % 2)
        for i, x in enumerate((draw[:, 0:2], draw[:, 2:4], draw[:, 5:7])):
            dve.wait_ge(sem("odd_rope_P"), i + 1)
            rope(x, bank[5 + i % 3][:, :], att["rope"][:, 512 * (i % 2):512 * (i % 2) + 512], sem("odd_rope"))
        for i, x in enumerate((L1["kd"], L1["kid"])):
            dve.wait_ge(sem("odd_rope_P"), 4 + i)
            dve.wait_ge(sem("odd_rope"), 3 + i)
            link(v.tensor_tensor(x, bank[i][:, 0:T], C("cos"), MUL))
            link(v.tensor_tensor(att["rope"][:, 0:T], bank[i][:, T:2 * T], C("sin"), MUL))
            v.tensor_tensor(x, x, att["rope"][:, 0:T], ADD).then_inc(sem("odd_rope"), 1)

        def index_scores(t):
            nk = P * (t + 1)
            acc, work = L1["acc"][:, 0:nk], L1["work"][:, 0:nk]
            dve.wait_ge(sem("relu_done"), t + 1)
            dve.wait_ge(sem("kv_copied"), NT)
            link(v.tensor_scalar(acc, relu[:, 0, 0:nk], wi[:, t, 0:1], None, MUL))
            for h in range(1, 4):
                ins = v.scalar_tensor_tensor(acc, relu[:, h, 0:nk], wi[:, t, h:h + 1], acc, MUL, ADD)
                if h < 3:
                    link(ins)
                else:
                    ins.then_inc(sem("acc_done"), 1)
            dve.wait_ge(sem("acc_done"), t + 1)
            link(v.tensor_tensor(work, acc, C(f"causal{t}")[:, 0:nk], ADD))

        def select_keys(t, rounds):
            work = L1["work"][:, 0:P * (t + 1)]
            for _ in range(rounds):
                link(v.max(L1["top"], work))
                link(v.match_replace(work, L1["top"], work, -3.0e38))

        def key_mask(t):
            nk = P * (t + 1)
            work = L1["work"][:, 0:nk]
            link(v.tensor_scalar(work, work, -2.0e38, NEG, ALU.is_gt, MUL))
            link(v.tensor_tensor(md[:, t, 0:nk], work, C(f"causal{t}")[:, 0:nk], ADD))

        index_scores(0)
        select_keys(0, TOPK // 8)
        key_mask(0)
        index_scores(1)

        def rwkv_step(u):
            if u == 0:
                dve.wait_ge(sem("gates_done"), 1)
                for k in range(KM):
                    last = v.tensor_scalar(KK[:, k, :], shf[:, 4 + k, :], col("rwkv_k_k", k), None, MUL)
                last.then_inc(sem("kk_raw"), 1)
                for k in range(KM):
                    last = v.tensor_tensor_scan(Lc[:, k, :], C("restart"), lw[:, k, :], 0.0, MUL, ADD)
                link(last)
                v.tensor_tensor(flat(lw), flat(Lc), flat(lw), SUB).then_inc(sem("L_done"), 1)
            elif u == 1:
                for k in range(KM):
                    last = v.tensor_scalar(rk[:, k, :], Ag[:, k, :], -1.0, col("rwkv_k_a", k), ADD, MUL)
                link(last)
                link(v.scalar_tensor_tensor(flat(shf[:, 4:8]), flat(rk), 1.0, flat(shf[:, 4:8]), ADD, MUL))
            elif u == 2:
                for k in range(KM):
                    last = v.scalar_tensor_tensor(rk[:, k, :], shf[:, k, :], col("rwkv_r_k", k),
                                                  shf[:, 4 + k, :], MUL, MUL)
                link(last)
                dve.sem_inc(sem("rk_done"), 1)
                dve.wait_ge(sem("exps_done"), 1)
                v.tensor_tensor(AR[:, :, 1, :], shf[:, 0:4, :], Lc, MUL)
            elif u == 3:
                link(v.tensor_tensor(flat(shf[:, 4:8]), flat(shf[:, 4:8]), flat(Em), MUL))
                v.tensor_copy(lam, Lc[:, :, CHUNK - 1::CHUNK])
                v.memset(sc["S"], 0.0)
                v.memset(sc["G"], 0.0)
                v.memset(sc["U"], 0.0)
            elif u == 4:
                dve.wait_ge(sem("kk_norm"), 1)
                kn = L1["st8"][:, 0:16]
                link(v.tensor_scalar(kn, kn, 1e-12, None, ALU.max))
                v.reciprocal(kn, kn).then_inc(sem("kk_inv"), 1)
            elif u in (6, 7):
                dve.wait_ge(sem("kk_back"), 1)
                kk2 = flat(KK[:, 2 * (u - 6):2 * (u - 6) + 2, :])
                link(v.tensor_tensor(kk2, kk2, bank[u - 6][:, :], MUL))
            elif u == 8:
                link(v.tensor_tensor(flat(Ag), flat(Ag), flat(KK), MUL))
                v.tensor_tensor(flat(Ag), flat(Ag), flat(Em), MUL)
            elif u == 9:
                v.scalar_tensor_tensor(AR[:, :, 0, :], KK[:, :, :], -1.0, lw[:, :, :], MUL, MUL).then_inc(
                    sem("tilde_done"), 1)

        for u in range(UNITS + 2):
            softmax(u, UNITS, p0, lambda u: md[:, u // KM, :], None)
            if u < KM:
                select_keys(1, TOPK // 8 // KM)
                if u == KM - 1:
                    key_mask(1)
            rwkv_step(u)
        dve.wait_ge(sem("tilde_done"), 1)
        MB5 = ring[:, 0:HEADS * 2 * P].rearrange("p (f j x) -> p f j x", f=KM, j=2)
        MK5 = ring[:, HEADS * 2 * P:2 * HEADS * 2 * P].rearrange("p (f j x) -> p f j x", f=KM, j=2)
        T4 = sc["T"].rearrange("p (f j n) -> p f j n", f=KM, j=2)
        pair_mask = con[:, coff["before"][0]:coff["before"][0] + 2 * P]
        for t in range(NT):
            for hh in range(2):
                dve.wait_ge(sem("A_done"), 2 * t + hh + 1)
                for j in range(2):
                    for dst, b in ((MB5, bank[j]), (MK5, bank[2 + j])):
                        v.tensor_tensor(dst[:, 2 * hh:2 * hh + 2, j, :], b[:, :].rearrange("p (f x) -> p f x", f=2),
                                        pair_mask[:, None, :].to_broadcast([P, 2, 2 * P]), MUL)
                    last = v.tensor_tensor(T4[:, 2 * hh:2 * hh + 2, j, :],
                                           bank[4 + j][:, 0:2 * P].rearrange("p (f n) -> p f n", f=2),
                                           C("level1")[:, None, :].to_broadcast([P, 2, P]), MUL)
                last.then_inc(sem("A_copied"), 1)
                dve.wait_ge(sem("A_copied"), 2 * t + hh + 1)
                hs_ = slice(4 * hh, 4 * hh + 4)
                idb = C("ident")[:, None, :].to_broadcast([P, 4, P])
                link(v.tensor_tensor(TT[:, hs_, :], MB[:, hs_, 0, :], C("level1T")[:, None, :].to_broadcast([P, 4, P]), MUL))
                v.tensor_tensor(TT[:, hs_, :], TT[:, hs_, :], idb, ADD)
                v.tensor_tensor(Tm[:, hs_, :], Tm[:, hs_, :], idb, ADD).then_inc(sem("T_ready"), 1)
            for n, m in enumerate(LEVELS[1:]):
                for hh in range(2):
                    q = (t * 5 + n) * 2 + hh
                    hs_ = slice(4 * hh, 4 * hh + 4)
                    Z4, T4_, TT4 = Zm[:, hs_, :], Tm[:, hs_, :], TT[:, hs_, :]
                    bz, bt, btt = bank[3 * hh], bank[3 * hh + 1], bank[3 * hh + 2]
                    dve.wait_ge(sem("Z_done"), q + 1)
                    v.tensor_tensor(Z4, bz[:, :].rearrange("p (h n) -> p h n", h=4),
                                    C(f"level{m}")[:, None, :].to_broadcast([P, 4, P]), MUL).then_inc(sem("Z_copied"), 1)
                for hh in range(2):
                    q = (t * 5 + n) * 2 + hh
                    hs_ = slice(4 * hh, 4 * hh + 4)
                    T4_, TT4 = Tm[:, hs_, :], TT[:, hs_, :]
                    bt, btt = bank[3 * hh + 1], bank[3 * hh + 2]
                    dve.wait_ge(sem("TZ_done"), q + 1)
                    if m < 32:
                        v.tensor_tensor(flat(T4_), flat(T4_), bt[:, :], ADD)
                    v.tensor_tensor(flat(TT4), flat(TT4), btt[:, :], ADD).then_inc(sem("TT_ready"), 1)
            for ci in range(2):
                c = 2 * t + ci
                dve.wait_ge(sem("dS_done"), c + 1)
                if c:
                    dve.wait_ge(sem("S_ready"), c)
                ds = sc["ds"].rearrange("p (k n) -> p k n", k=KM)
                link(v.tensor_tensor(ds, bank[0][:, :].rearrange("p (k n) -> p k n", k=KM),
                                     C("block_ones")[:, None, :].to_broadcast([P, KM, P]), MUL))
                link(v.tensor_tensor(ds, ds, Sbd, ADD))
                v.tensor_tensor(Sbd, ds, lam[:, :, c:c + 1].to_broadcast([P, KM, P]), MUL).then_inc(sem("S_ready"), 1)
            dve.wait_ge(sem("y_done"), t + 1)
            dve.wait_ge(sem("lora_loaded"), 16 * 5)
            ya, yb = (sc[n].rearrange("p (h n) -> p h n", h=HEADS) for n in ("ya", "yb"))
            yp = bank[1][:, :].rearrange("p (h n) -> p h n", h=HEADS)
            link(v.tensor_reduce(st8[:, 0, :], yp, AX, ADD))
            link(v.tensor_scalar(st8[:, 0, :], st8[:, 0, :], -1.0 / HD, None, MUL))
            link(v.tensor_tensor(ya, yp, st8[:, 0, :][:, :, None].to_broadcast([P, HEADS, HD]), ADD))
            link(v.tensor_tensor(yb, ya, ya, MUL))
            v.tensor_reduce(st8[:, 1, :], yb, AX, ADD).then_inc(sem("gn_var"), 1)
            dve.wait_ge(sem("gn_var"), t + 1)
            link(v.tensor_tensor(yb, sc["Vt"].rearrange("p (h n) -> p h n", h=HEADS),
                                 bank[4][:, 0:HEADS][:, :, None].to_broadcast([P, HEADS, HD]), MUL))
            dve.wait_ge(sem("gn_std"), t + 1)
            link(v.reciprocal(st8[:, 3, :], st8[:, 2, :]))
            link(v.tensor_tensor(ya, ya, st8[:, 3, :][:, :, None].to_broadcast([P, HEADS, HD]), MUL))
            link(v.tensor_tensor(sc["ya"], sc["ya"], L1["lnw"], MUL))
            link(v.tensor_tensor(sc["ya"], sc["ya"], L1["lnb"], ADD))
            link(v.tensor_tensor(sc["ya"], sc["ya"], sc["yb"], ADD))
            v.tensor_tensor(sc["ya"], sc["ya"], bank[3][:, :], MUL).then_inc(sem("bonus_used"), 1)
            dve.wait_ge(sem("bonus_used"), t + 1)

        def expert_lo(it, h):
            dve.wait_ge(sem("hi_done"), NHE * it + NH0 + h + 1)
            hi, lo = pair(NH0 + h)
            v.tensor_tensor(lo, expert_place(h // 2, type(it) is int)[0][h % 2], hi.bitcast(f32), SUB).then_inc(
                sem("lo_done"), 1)

        expert_lo(0, 0)
        expert_lo(0, 1)
        for i in range(4):
            add_h(i, bank[2 + i], 9 + i)

        norm(3, "o_norm_ffn")
        def cp(dst, src):
            return v.tensor_copy(dst, src)

        m12 = MO["m12"]
        dve.wait_ge(sem("logits_done"), 1)
        link(cp(flat(lg), bank[7][:, 0:NT * NE]))

        def first_max(e_out, x, m):
            link(v.tensor_reduce(m, x, AX, ALU.max))
            link(v.tensor_tensor(e_out, x, m[:, :, None].to_broadcast([P, NT, NE]), ALU.is_equal))
            link(v.tensor_tensor_scan(flat(t16), C("restart8"), flat(e_out), 0.0, MUL, ADD))
            link(v.scalar_tensor_tensor(flat(e_out), flat(t16), 1.0, flat(e_out), ALU.is_le, MUL))

        first_max(e1, lg, m12[:, 0:2])
        link(v.scalar_tensor_tensor(flat(lg), flat(e1), -3.0e38, flat(lg), MUL, ADD))
        first_max(e2, lg, m12[:, 2:4])
        link(v.tensor_tensor(m12[:, 2:4], m12[:, 2:4], m12[:, 0:2], SUB))
        v.tensor_tensor(flat(sel), flat(e1), flat(e2), ADD).then_inc(sem("m12_done"), 1)
        expert_lo(0, 2)
        dve.wait_ge(sem("m12_exp"), 1)
        link(v.tensor_scalar(m12[:, 6:8], m12[:, 4:6], 1.0, None, ADD))
        link(v.reciprocal(m12[:, 6:8], m12[:, 6:8]))
        link(v.tensor_tensor(m12[:, 4:6], m12[:, 4:6], m12[:, 6:8], MUL))
        link(v.tensor_tensor(gate, e1, m12[:, 6:8][:, :, None].to_broadcast([P, NT, NE]), MUL))
        link(v.tensor_tensor(e2, e2, m12[:, 4:6][:, :, None].to_broadcast([P, NT, NE]), MUL))
        link(v.tensor_tensor(flat(gate), flat(gate), flat(e2), ADD))
        cnt = MO["cnt"].rearrange("p (a e) -> p a e", a=4)
        dve.wait_ge(sem("rank_done"), 1)
        cp(flat(rank), bank[6][:, 0:NT * NE])
        link(cp(cnt[:, 0, :], bank[6][:, NT * NE:NT * NE + NE]))
        link(v.tensor_scalar(cnt[:, 1, :], cnt[:, 0, :], CAP + 0.5, None, ALU.is_gt))
        link(v.tensor_tensor_scan(cnt[:, 2, :], C("ones")[:, 0:NE], cnt[:, 1, :], float(NE), MUL, ADD))
        link(v.tensor_tensor(cnt[:, 3, :], cnt[:, 2, :], cnt[:, 1, :], SUB))
        item = C("item").rearrange("p (i e) -> p i e", e=NE)
        first = C("first").rearrange("p (i e) -> p i e", e=NE)
        oh, ohx = (MO[n].rearrange("p (i e) -> p i e", e=NE) for n in ("oh", "ohx"))
        sh3 = [P, ITEMS, NE]
        link(v.tensor_tensor(oh, item, cnt[:, 3, :][:, None, :].to_broadcast(sh3), ALU.is_ge))
        link(v.tensor_tensor(ohx, item, cnt[:, 2, :][:, None, :].to_broadcast(sh3), ALU.is_lt))
        link(v.tensor_tensor(oh, oh, ohx, MUL))
        link(v.tensor_scalar(MO["off"], MO["oh"], float(CAP), None, MUL))
        link(v.tensor_tensor(oh, oh, first, ADD))
        link(v.tensor_tensor(ohx, oh, C("expert")[:, None, :].to_broadcast(sh3), MUL))
        link(v.tensor_reduce(MO["ef"][:, 0:ITEMS], ohx, AX, ADD))
        link(cp(MO["ef"][:, ITEMS:ITEMS + 1], cnt[:, 2, NE - 1:NE]))
        v.tensor_copy(work_list[:, :], MO["ef"]).then_inc(sem("work_ready"), 1)
        link(v.tensor_scalar(flat(t16), flat(sel), -1.0, 4096.0, ADD, MUL))
        link(v.tensor_tensor(flat(rank), flat(rank), flat(t16), ADD))
        link(v.tensor_reduce(MO["offi"], MO["off"].rearrange("p (i e) -> p i e", e=NE), AX, ADD))
        for t in range(NT):
            link(v.tensor_tensor(ohx, oh, rank[:, t, :][:, None, :].to_broadcast(sh3), MUL))
            link(v.tensor_reduce(slotp[:, t, 0:ITEMS], ohx, AX, ADD))
            link(v.tensor_tensor(slotp[:, t, 0:ITEMS], slotp[:, t, 0:ITEMS], MO["offi"], SUB))
            link(v.tensor_tensor(ohx, oh, gate[:, t, :][:, None, :].to_broadcast(sh3), MUL))
            link(v.tensor_reduce(gatep[:, t, :], ohx, AX, ADD))
        link(v.memset(slotp[:, :, ITEMS:ITEMS + 1].rearrange("p t o -> p (t o)"), -1.0))
        dve.sem_inc(sem("H_done"), NFC)
        dve.sem_inc(sem("scattered"), 2 * NT)

        def onehots(it):
            for t in range(NT):
                last = v.tensor_scalar(onehot[:, t, :], C("time")[:, 0:CAP], slotp[:, t, bass.ds(it, 1)], None,
                                       ALU.is_equal)
            last.then_inc(sem("onehot_ready"), 1)

        def gather_lo():
            for i in range(2):
                last = v.tensor_tensor(flat(xg[1][:, 4 * i:4 * i + 4, :]), bank[6 + i][:, :],
                                       flat(xg[0][:, 4 * i:4 * i + 4, :]).bitcast(f32), SUB)
            last.then_inc(sem("xg_lo"), 1)

        def add_scattered(t):
            for i in range(2):
                last = v.tensor_tensor(htok[:, t, 512 * i:512 * i + 512], htok[:, t, 512 * i:512 * i + 512],
                                       bank[6 + i][:, :], ADD)
            last.then_inc(sem("scattered"), 1)

        for t in range(NT):
            last = v.tensor_scalar(onehot[:, t, :], C("time")[:, 0:CAP], slotp[:, t, 0:1], None, ALU.is_equal)
        last.then_inc(sem("onehot_ready"), 1)
        dve.wait_ge(sem("xg_hi"), 1)
        gather_lo()

        def run_item(it, peeled=False):
            for h in range(NHE):
                kind, c = step_before(h)
                if kind == "up":
                    dve.wait_ge(sem("moe_silu"), NFC * it + c + 1)
                    dve.wait_ge(sem("pair_used"), NHE * it + NH0 + h - 2)
                    v.tensor_tensor(MO["H"], MO["silu"], bank[1][:, :], MUL).then_inc(sem("H_done"), 1)
                if (kind == "gate" and c) or h == NHE - 2:
                    c = c if kind == "gate" else NFC
                    dve.wait_ge(sem("ht_hi"), NFC * it + c)
                    v.tensor_tensor(flat(ht[1][:, (c - 1) % 2]), bank[2][:, :], flat(ht[0][:, (c - 1) % 2]).bitcast(f32), SUB).then_inc(
                        sem("ht_lo"), 1)
                if h in (5, 7) and not peeled:
                    t = (h - 5) // 2
                    dve.wait_ge(sem("scatter_done"), NT * it + t + 1)
                    add_scattered(t)
                if h == 16:
                    dve.wait_ge(sem("pair_used"), NHE * it + NH0 + 1)
                    onehots(it + 1)
                    for t in range(NT):
                        last = v.tensor_scalar(gated[:, t, :], C("time")[:, 0:CAP], slotp[:, t, bass.ds(it, 1)],
                                               gatep[:, t, bass.ds(it, 1)], ALU.is_equal, MUL)
                    last.then_inc(sem("gated_ready"), 1)
                if h >= 3 or not peeled:
                    expert_lo(it, h)
                if h == NHE - 2:
                    dve.wait_ge(sem("xg_hi"), it + 2)
                    gather_lo()

        run_item(0, peeled=True)
        n_items = dve.value_load(work_list[0:1, ITEMS:ITEMS + 1], min_val=NE, max_val=ITEMS)
        with dve.Fori(1, n_items) as it:
            run_item(it)
        for t in range(NT):
            dve.wait_ge(sem("scatter_done"), NT * n_items + t + 1)
            add_scattered(t)
        dve.wait_ge(sem("scattered"), NT * n_items + 2 * NT)
        dve.sem_inc(sem("acc_final"), 1)
        dve.wait_ge(sem("final_rms"), 1)
        dve.wait_ge(sem("gfin_loaded"), 16)
        link(v.reciprocal(m12[:, 12:14], m12[:, 10:12]))
        for t in range(NT):
            v.scalar_tensor_tensor(htok[:, t, :], htok[:, t, :], m12[:, 12 + t:13 + t], MO["gfin"], MUL,
                                   MUL).then_inc(sem("y_final"), 1)

    @block.tensor
    def _(pe):
        def loaded(n):
            pe.wait_ge(slot_sem[slot_of[n]], 16 * loads_of[n])

        pe.wait_ge(sem("consts_loaded"), 16)
        ident = C("ident")
        pe.wait_ge(sem("x_loaded"), 16)
        for k in range(KD):
            for t in range(NT):
                o = (k % 2) * T + t * P
                last = pe_.transpose(bank[1 + k // 2][:, o:o + P], xtok[:, t, k * P:k * P + P], ident)
            if k % 2:
                last.then_inc(sem("x_T"), 1)
        pe.wait_ge(sem("vecs_loaded"), 16 * len(VECS))
        pe_.transpose(bank[0][:, 0:NVEC], pre["vecs"][0:NVEC, :], ident[0:NVEC, 0:NVEC]).then_inc(
            sem("vecs_T"), 1)

        def keep_warm(b, n):
            for _ in range(n):
                pe_.matmul(b[:, 0:2 * P], ident, con[:, 0:2 * P], start=True, stop=True)

        def norm(n):
            spare = bank[0 if n else 6]
            keep_warm(spare, WARM["norm_in"][n])
            for k in range(KD):
                if k % 2 == 0:
                    pe.wait_ge(sem("sq_done"), 4 * n + k // 2 + 1)
                last = pe_.matmul(ss_bank(n), C("ones"), xnT[:, k, :], start=(k == 0), stop=(k == KD - 1))
            last.then_inc(sem("ss_done"), 1)
            keep_warm(spare, WARM["norm_out"][n])

        def project(n, tiles, dst):
            w = view(n)
            for i in tiles:
                width = min(P, w.shape[2] - i * P)
                for k in range(KD):
                    last = pe_.matmul(dst(i)[0:width, :], w[:, k, i * P:i * P + width], xnT[:, k, :],
                                      start=(k == 0), stop=(k == KD - 1))
            return last

        def half(b, i):
            return b[:, (i % 2) * T:(i % 2) * T + T]

        norm(0)
        pe.wait_ge(sem("xn_done"), 2)
        loaded(0)
        for i in range(2):
            last = project(0, (2 * i, 2 * i + 1), lambda j: half(bank[j // 2], j))
            last.then_inc(sem("u_done"), 1)
        pe.wait_ge(sem("s5_loaded"), 16 * 13)
        for m, src in enumerate((pre["Cx"], pre["Cs"])):
            for k in range(4):
                last = pe_.transpose(bank[2 + m][:, k * P:k * P + P], src[:, k * P:k * P + P], ident)
        last.then_inc(sem("c_T"), 1)
        pe.wait_ge(sem("s5_params"), 1)
        for i, x in enumerate((small[4], small[5], small[12], small[13])):
            last = pe_.transpose(bank[7][:, G5 * i:G5 * i + G5], x, ident[0:G5, 0:G5])
        last.then_inc(sem("s5_params_T"), 1)
        pe.wait_ge(sem("bbar_done"), 1)
        for m, src in enumerate((pre["M1"], pre["M2"])):
            for k in range(4):
                last = pe_.transpose(bank[5 + m][:, k * P:k * P + P], src[:, k * P:k * P + P], ident)
        last.then_inc(sem("bbar_T"), 1)

        def bu(b):
            pe.wait_ge(sem("um_ready"), b + 1)
            if b < 2:
                pe.wait_ge(sem("prep_done"), 1)
            else:
                pe.wait_ge(sem("ab_read"), b - 1)
            for m in range(2):
                for j in range(2):
                    last = pe_.matmul(half(bank[2 * (b % 2) + m], j), BT[:, m, b // 4, :], um[:, b % 2, j, :],
                                      start=True, stop=True)
            last.then_inc(sem("ab_done"), 1)

        def cx(b):
            k = b // 4
            pe.wait_ge(sem("s5_out"), b + 1)
            if b % 4 == 0:
                pe.wait_ge(sem("cw_ready"), k + 1)
                if k:
                    pe.wait_ge(sem("y_added"), k)
            for j in range(2):
                g = (2 * b + j) % 8
                for m, x in enumerate((oc, os_)):
                    last = pe_.matmul(bank[4][:, 0:T], CW[:, k % 2, m, g * P:g * P + P], x[:, b % 2, j, :],
                                      start=(g == 0 and m == 0), stop=(g == 7 and m == 1))
            last.then_inc(sem("y_used"), 1)

        def attention(u, base, q, k, vals, pT, first):
            if u < UNITS:
                f, t = unit(u, base)
                nk = P * (t + 1)
                if u == 0:
                    first()
                else:
                    pe.wait_ge(sem("sc_read"), base + u)
                for j in range(2):
                    last = pe_.matmul(bank[5 + j][:, 0:nk], q(f, j)[:, t * P:t * P + P],
                                      k(f, j)[:, 0:nk], start=True, stop=True)
                last.then_inc(sem("sc_done"), 1)
            if u >= 2:
                w = u - 2
                f, t = unit(w, base)
                nt = t + 1
                pe.wait_ge(sem("pt_copied"), base + w + 1)
                for j in range(2):
                    for kt in range(nt):
                        last = pe_.matmul(bank[7][HD * j:HD * j + HD, 0:P], vals(kt, 2 * f + j),
                                          pT[:, P * (nt * j + kt):P * (nt * j + kt) + P],
                                          start=(kt == 0), stop=(kt == nt - 1))
                last.then_inc(sem("pv_done"), 1)
            if 1 <= u <= UNITS:
                w = u - 1
                nt = unit(w, base)[1] + 1
                pe.wait_ge(sem("p_ready"), base + w + 1)
                if w:
                    pe.wait_ge(sem("o_copied"), base + w)
                p = att["p"].rearrange("p (b j n) -> p b j n", b=2, j=2)
                for j in range(2):
                    for kt in range(nt):
                        o = P * (nt * j + kt)
                        last = pe_.transpose(bank[7][:, o:o + P], p[:, w % 2, j, kt * P:kt * P + P], ident)
                last.then_inc(sem("pt_done"), 1)

        for what, i in plan:
            if what == "s5":
                if i == 0:
                    bu(0)
                if i + 1 < NB5:
                    bu(i + 1)
                if i:
                    cx(i - 1)
            elif what == "proj":
                if i >= 3:
                    pe.wait_ge(sem("proj_copied"), i - 2)
                b = bank[5 + i % 3]
                if i < 4:
                    n = 1 + i // 2
                    loaded(n)
                    last = project(n, (2 * (i % 2), 2 * (i % 2) + 1), lambda j: half(b, j))
                else:
                    loaded(3)
                    t = i - 4
                    for k in range(KD):
                        last = pe_.matmul(b[:, :], xnT[:, k, t * P:t * P + P], view(3)[:, k, :],
                                          start=(k == 0), stop=(k == KD - 1))
                last.then_inc(sem("proj_done"), 1)
            elif what == "rope":
                pe.wait_ge(sem("proj_copied"), 6)
                if i >= 3:
                    pe.wait_ge(sem("rope_done"), i - 2)
                x = (qT, kT)[i // 2][:, 2 * (i % 2):2 * (i % 2) + 2, :]
                pe_.matmul(bank[5 + i % 3][:, :], C("perm"), flat(x), start=True, stop=True).then_inc(
                    sem("rope_P"), 1)
            elif what == "attn":
                attention(i, 0, lambda f, j: qT[HD * j:HD * j + HD, f, :],
                          lambda f, j: kT[HD * j:HD * j + HD, f, :],
                          lambda kt, h: V0[:, kt, h * HD:h * HD + HD], L0["pT"],
                          lambda: pe.wait_ge(sem("rope_done"), 4))
        loaded(4)
        pe.wait_ge(sem("gelu_done"), 1)
        for m in range(KM):
            for k in range(KM):
                last = pe_.matmul(half(bank[m // 2], m), view(4)[:, k, m * P:m * P + P], yT[:, k, :],
                                  start=(k == 0), stop=(k == KM - 1))
            if m % 2:
                last.then_inc(sem("z_done"), 1)

        def out_projection(n):
            for i in range(KD):
                if i % 4 == 0:
                    loaded(n + i // 4)
                for k in range(KD):
                    last = pe_.matmul(half(bank[2 + i // 2], i), view(n + i // 4)[:, k, (i % 4) * P:(i % 4) * P + P],
                                      yT[:, k, :], start=(k == 0), stop=(k == KD - 1))
                if i % 2:
                    last.then_inc(sem("into_h"), 1)

        pe.wait_ge(sem("glu_done"), 1)
        pe.wait_ge(sem("o_copied"), UNITS)
        out_projection(5)
        norm(1)
        def product3(dst, w, x, start, stop):
            pe_.matmul(dst, w[0], x[0], start=start, stop=False, skip_group_check=True)
            pe_.matmul(dst, w[1], x[0], start=False, stop=False, skip_group_check=True)
            return pe_.matmul(dst, w[0], x[1], start=False, stop=stop, skip_group_check=True)

        def split_projection(n, b, x_ready, first_bank_done=None):
            w = view(n).shape[2] // P
            for x in range(2):
                pe.wait_ge(sem("lo_done"), 2 * (n - NFFN) + x + 1)
                x_ready(x)
                hi, lo = half_parts(n, x)
                for i in range(w):
                    for k in range(4):
                        c_ = slice(i * P, i * P + P)
                        last = product3(half(b[i // 2], i), (hi[:, k, c_], lo[:, k, c_]),
                                        (xhi[:, 4 * x + k, :], xlo[:, 4 * x + k, :]),
                                        x == 0 and k == 0 and i % 2 == 0, x == 1 and k == 3)
                    if x == 1 and i == 1 and first_bank_done:
                        last.then_inc(first_bank_done, 1)
                last.then_inc(sem("pair_used"), 1)

        def ffn_down(c, n):
            w = view(n).shape[1]
            pe.wait_ge(sem("hlo_done"), c + 1)
            for x in range(2):
                pe.wait_ge(sem("lo_done"), 2 * (n - NFFN) + x + 1)
                hi, lo = half_parts(n, x)
                for i in range(KD):
                    for j in range(w // 2):
                        c_, jj = slice(i * P, i * P + P), x * (w // 2) + j
                        last = product3(half(bank[4 + i // 2], i), (hi[:, j, c_], lo[:, j, c_]),
                                        (hhi[:, c % 2, jj, :], hlo[:, c % 2, jj, :]),
                                        c == 0 and jj == 0 and i % 2 == 0, c == nf - 1 and jj == w - 1)
                    if c == nf - 1 and x == 1 and i % 2 == 1 and i < KD - 1:
                        last.then_inc(sem("into_h"), 1)
                last.then_inc(sem("pair_used"), 1)

        nf = len(range(0, FFN, FB))
        for s, (kind, c) in enumerate(ffn_steps):
            n = NFFN + s
            if kind == "gate":
                if c:
                    pe.wait_ge(sem("silu_done"), c)
                split_projection(n, bank[0:2], lambda x: pe.wait_ge(sem("xlo_done"), x + 1))
            elif kind == "up":
                if c:
                    pe.wait_ge(sem("hprod_done"), c)
                else:
                    pe.wait_ge(sem("h_added"), 4)
                split_projection(n, bank[2:4], lambda x: None)
            else:
                ffn_down(c, n)
        pe.wait_ge(sem("pair_used"), 2 * len(ffn_steps))
        pe.sem_inc(sem("into_h"), 1)

        norm(2)
        for m in range(5):
            if m == 4:
                pe.wait_ge(sem("odd_copied"), 2)
            b = [bank[2 * m % 8], bank[2 * m % 8 + 1]]
            split_projection(NRAW - 5 + m, b, lambda x: pe.wait_ge(sem("xlo_done"), 2 + x + 1), sem("odd_proj"))
        pe.wait_ge(sem("odd_copied"), 3)
        loaded(NRAW)
        w = view(NRAW)
        for x in range(2):
            width = min(P, w.shape[2] - x * P)
            for k in range(KD):
                last = pe_.matmul(half(bank[2], x)[0:width, :], w[:, k, x * P:x * P + width], xnT[:, k, :],
                                  start=(k == 0), stop=(k == KD - 1))
        last.then_inc(sem("odd_proj"), 1)
        pe.wait_ge(sem("odd_copied"), 11)
        for i, x in enumerate((draw[:, 0:2, :], draw[:, 2:4, :], draw[:, 5:7, :])):
            pe_.matmul(bank[5 + i][:, :], C("perm"), flat(x), start=True, stop=True).then_inc(sem("odd_rope_P"), 1)
        for i, k in enumerate((4, 7)):
            for m, name in enumerate(("dup", "dup_perm")):
                last = pe_.matmul(half(bank[i], m), C(name)[0:HD, :], draw[0:HD, k, :], start=True, stop=True)
            last.then_inc(sem("odd_rope_P"), 1)
        for t in range(NT):
            pe_.transpose(bank[2 + t][:, 0:P], draw[:, 4, t * P:t * P + P], ident)
            pe_.transpose(bank[2 + t][:, P:P + HD + 4], draw[0:HD + 4, 7, t * P:t * P + P],
                          ident[0:HD + 4, 0:HD + 4]).then_inc(sem("kv_T"), 1)
        pe.wait_ge(sem("odd_rope"), 5)
        def low_rank():
            pe.wait_ge(sem("lora_in"), 2)
            pe.wait_ge(sem("lora_loaded"), 16 * 5)
            pe.wait_ge(sem("kv_copied"), NT)
            for g, (r0, b0) in enumerate(((0, 0), (64, 2))):
                for k in range(KM):
                    last = pe_.matmul(half(bank[b0 + k // 2], k), L1["WA"][r0:r0 + 64, k * P:k * P + P],
                                      shf[r0:r0 + 64, 12, :], start=True, stop=True)
            last.then_inc(sem("lora_done"), 1)

        for t in range(NT):
            nk = P * (t + 1)
            if t:
                low_rank()
                pe.wait_ge(sem("relu_done"), t)
            for h in range(4):
                j = h % 2
                last = pe_.matmul(half(bank[4 + j], h // 2)[:, 0:nk],
                                  draw[HD * j:HD * j + HD, 5 + h // 2, t * P:t * P + P],
                                  L1["kid"][HD * j:HD * j + HD, 0:nk], start=True, stop=True)
            last.then_inc(sem("idx_done"), 1)
        def dsa_first():
            pe.wait_ge(sem("relu_done"), NT)
        for u in range(UNITS + 2):
            attention(u, UNITS, lambda f, j: draw[HD * j:HD * j + HD, f, :],
                      lambda f, j: L1["kd"][HD * j:HD * j + HD, :],
                      lambda kt, h: Vd[:, kt, :], L1["pT"], dsa_first)
            if u == 2:
                pe.wait_ge(sem("gates_done"), 1)
                pe.wait_ge(sem("kk_sq"), 1)
                for i in range(NT * KM):
                    t, k = i // KM, i % KM
                    last = pe_.matmul(bank[0][:, 2 * i:2 * i + 2], tmp4[:, k, t * P:t * P + P], C("pair"),
                                      start=True, stop=True)
                last.then_inc(sem("kk_ss"), 1)
            if u == 5:
                pe.wait_ge(sem("kk_wide"), 1)
                for k in range(KM):
                    for t in range(NT):
                        i = t * KM + k
                        last = pe_.transpose(half(bank[k // 2], k)[:, t * P:t * P + P],
                                             sc["tmp"][:, i * P:i * P + P], ident)
                last.then_inc(sem("kk_back"), 1)
        keep_warm(bank[6], WARM["tilde"])
        pe.wait_ge(sem("tilde_done"), 1)
        pe.wait_ge(sem("gates_done"), 1)
        for t in range(NT):
            tc = slice(t * P, t * P + P)
            if t:
                pe.wait_ge(sem("yc_copied"), t)
                pe.wait_ge(sem("bonus_used"), t)
                pe.wait_ge(sem("S_ready"), 2 * t)
            for i, src in enumerate((shf[:, 8:12, :], shf[:, 4:8, :], Ag)):
                for k in range(KM):
                    last = pe_.transpose(bank[i][:, k * P:k * P + P], src[:, k, tc], ident)
            last.then_inc(sem("tok_T"), 1)
            for hh in range(2):
                keep_warm(bank[6], WARM["A"][hh])
                if hh == 0:
                    pe.wait_ge(sem("tok_copied"), t + 1)
                else:
                    pe.wait_ge(sem("A_copied"), 2 * t + hh)
                for f in (2 * hh, 2 * hh + 1):
                    for j in range(2):
                        rows = slice(HD * j, HD * j + HD)
                        ar_ = AR[rows, f, :, tc]
                        o = (f % 2) * 2 * P
                        pe_.matmul(bank[j][:, o:o + 2 * P], Ag[rows, f, tc], ar_, start=True, stop=True)
                        pe_.matmul(bank[2 + j][:, o:o + 2 * P], shf[rows, 4 + f, tc], ar_, start=True, stop=True)
                        last = pe_.matmul(bank[4 + j][:, (f % 2) * P:(f % 2) * P + P], AR[rows, f, 0, tc],
                                          Ag[rows, f, tc], start=True, stop=True)
                last.then_inc(sem("A_done"), 1)
            keep_warm(bank[6], WARM["A"][2])
            pe.wait_ge(sem("A_copied"), 2 * t + 2)
            for n_, m in enumerate(LEVELS[1:]):
                for hh in range(2):
                    q = (t * 5 + n_) * 2 + hh
                    if n_ == 0:
                        pe.wait_ge(sem("T_ready"), 2 * t + hh + 1)
                    else:
                        pe.wait_ge(sem("TT_ready"), q - 1)
                    for x in range(4):
                        h = 4 * hh + x
                        last = pe_.matmul(bank[3 * hh][:, x * P:x * P + P], MB[:, h, 0, :], Tm[:, h, :],
                                          start=True, stop=True)
                    last.then_inc(sem("Z_done"), 1)
                for hh in range(2):
                    q = (t * 5 + n_) * 2 + hh
                    pe.wait_ge(sem("Z_copied"), q + 1)
                    for x in range(4):
                        h = 4 * hh + x
                        if m < 32:
                            pe_.matmul(bank[3 * hh + 1][:, x * P:x * P + P], TT[:, h, :], Zm[:, h, :],
                                       start=True, stop=True)
                        last = pe_.matmul(bank[3 * hh + 2][:, x * P:x * P + P], Zm[:, h, :], TT[:, h, :],
                                          start=True, stop=True)
                    last.then_inc(sem("TZ_done"), 1)
            pe.wait_ge(sem("TT_ready"), (t + 1) * 10)
            pe_.matmul(bank[3][:, :], shf[:, 13, tc], L1["GU"], start=True, stop=True)
            pe.wait_ge(sem("rk_done"), 1)
            for k in range(KM):
                pe_.matmul(bank[4][:, 2 * k:2 * k + 2], rk[:, k, tc], C("pair"), start=True, stop=True)
            for ci in range(2):
                c = 2 * t + ci
                R = slice(CHUNK * ci, CHUNK * ci + CHUNK)
                tR = slice(t * P + CHUNK * ci, t * P + CHUNK * ci + CHUNK)
                if c:
                    pe.wait_ge(sem("S_ready"), c)
                for k in range(KM):
                    pe_.matmul(bank[6][R, k * P:k * P + P], AR[:, k, 0, tR], Sbd[:, k, :], start=(k == 0),
                               stop=False, skip_group_check=True)
                for h in range(HEADS):
                    last = pe_.matmul(bank[6][R, h * HD:h * HD + HD], MK[:, h, 0, R], sc["Vt"][:, h * HD:h * HD + HD],
                                      start=False, stop=(h == HEADS - 1), skip_group_check=True)
                last.then_inc(sem("G_done"), 1)
                for k in range(KM):
                    pe_.matmul(bank[1][R, k * P:k * P + P], AR[:, k, 1, tR], Sbd[:, k, :], start=(k == 0),
                               stop=False, skip_group_check=True)
                pe.wait_ge(sem("G_copied"), c + 1)
                for h in range(HEADS):
                    last = pe_.matmul(bank[7][R, h * HD:h * HD + HD], TT[:, h, R], sc["G"][:, h * HD:h * HD + HD],
                                      start=True, stop=True)
                last.then_inc(sem("U_done"), 1)
                pe.wait_ge(sem("U_copied"), c + 1)
                for k in range(KM):
                    kc = slice(k * P, k * P + P)
                    pe_.matmul(bank[0][:, kc], sc["Kt"][R, kc], sc["Vt"][R, kc], start=True, stop=False)
                    last = pe_.matmul(bank[0][:, kc], sc["Bt"][R, kc], sc["U"][R, kc], start=False, stop=True)
                last.then_inc(sem("dS_done"), 1)
                for h in range(HEADS):
                    hc_ = slice(h * HD, h * HD + HD)
                    pe_.matmul(bank[1][R, hc_], MB[:, h, 1, R], sc["U"][:, hc_], start=False, stop=False,
                               skip_group_check=True)
                    last = pe_.matmul(bank[1][R, hc_], MK[:, h, 1, R], sc["Vt"][:, hc_], start=False,
                                      stop=(h == HEADS - 1), skip_group_check=True)
            last.then_inc(sem("y_done"), 1)
            keep_warm(bank[6], WARM["group_norm"])
            pe.wait_ge(sem("bonus_used"), t + 1)
            for k in range(KM):
                last = pe_.transpose(bank[2][:, k * P:k * P + P], sc["ya"][:, k * P:k * P + P], ident)
            last.then_inc(sem("yc_T"), 1)
        pe.wait_ge(sem("yc_copied"), NT)
        pe.wait_ge(sem("o_copied"), 2 * UNITS)
        out_projection(NRAW + 1)

        norm(3)
        pe.wait_ge(sem("xn_done"), 8)
        pe.wait_ge(sem("router_loaded"), 16)
        for t in range(NT):
            for k in range(KD):
                last = pe_.matmul(bank[7][:, t * NE:t * NE + NE], xnT[:, k, t * P:t * P + P], router[:, k, :],
                                  start=(k == 0), stop=(k == KD - 1))
        last.then_inc(sem("logits_done"), 1)

        def to_tokens(src, b0, done, copied):
            for t in range(NT):
                if t:
                    pe.wait_ge(sem(copied), 2)
                for k in range(KD):
                    last = pe_.transpose(bank[b0 + k // 4][:, (k % 4) * P:(k % 4) * P + P],
                                         src[:, k, t * P:t * P + P], ident)
                    if k % 4 == 3:
                        last.then_inc(sem(done), 1)

        pe.wait_ge(sem("h_added"), 12)
        to_tokens(xnT, 0, "xtok_T", "xtok_copied")
        pe.wait_ge(sem("m12_done"), 1)
        pe_.matmul(bank[6][:, 0:NE], C("earlier"), sel[:, 0, :], start=True, stop=True)
        pe_.matmul(bank[6][:, NE:2 * NE], C("ones"), sel[:, 0, :], start=True, stop=False)
        pe_.matmul(bank[6][:, NE:2 * NE], C("earlier"), sel[:, 1, :], start=False, stop=True)
        pe_.matmul(bank[6][:, 2 * NE:3 * NE], C("ones"), sel[:, 0, :], start=True, stop=False)
        pe_.matmul(bank[6][:, 2 * NE:3 * NE], C("ones"), sel[:, 1, :], start=False, stop=True).then_inc(
            sem("rank_done"), 1)
        to_tokens(hT, 2, "htok_T", "htok_copied")
        pe.wait_ge(sem("work_ready"), 1)
        pe.wait_ge(sem("xtok_copied"), 4)
        pe.wait_ge(sem("htok_copied"), 4)

        def gather():
            for k in range(KD):
                for t in range(NT):
                    last = pe_.matmul(bank[6 + k // 4][:, (k % 4) * CAP:(k % 4) * CAP + CAP],
                                      mtok[:, t, k * P:k * P + P], onehot[:, t, :], start=(t == 0), stop=(t == 1))
            last.then_inc(sem("gather_done"), 1)

        def scatter(t):
            for i in range(2):
                last = pe_.matmul(bank[6 + i][:, :], MO["gatedT"][:, t * P:t * P + P],
                                  MO["Y"][:, 512 * i:512 * i + 512], start=True, stop=True)
            last.then_inc(sem("scatter_done"), 1)

        keep_warm(bank[4], WARM["routing"])
        pe.wait_ge(sem("onehot_ready"), 1)
        gather()

        def run_item(it, peeled=False):
            def half_ready(h):
                pe.wait_ge(sem("lo_done"), NHE * it + NH0 + h + 1)
                return pair(NH0 + h)

            for s, (kind, c) in enumerate(expert_steps):
                if kind == "gate" and c == 0:
                    pe.wait_ge(sem("xg_lo"), it + 1)
                if kind == "gate" and c:
                    pe.wait_ge(sem("moe_silu"), NFC * it + c)
                if kind == "up" and c:
                    pe.wait_ge(sem("H_done"), NFC * it + NFC + c)
                if kind == "down":
                    pe.wait_ge(sem("ht_lo"), NFC * it + c + 1)
                    if c == 0:
                        pe.wait_ge(sem("Y_copied"), it + 1)
                for x in range(2):
                    hi, lo = (p.rearrange("p (k n) -> p k n", n=D if kind == "down" else FB)
                              for p in half_ready(2 * s + x))
                    if kind == "down":
                        for i in range(2):
                            cols = slice(512 * i, 512 * i + 512)
                            for j in range(2):
                                last = product3(bank[4 + i][:, :], [p[:, c % 2, 2 * x + j, :] for p in ht],
                                                (hi[:, j, cols], lo[:, j, cols]),
                                                c == 0 and x == 0 and j == 0, c == NFC - 1 and x == 1 and j == 1)
                    else:
                        for k in range(4):
                            last = product3(bank[0 if kind == "gate" else 1][:, :],
                                            (xg[0][:, 4 * x + k, :], xg[1][:, 4 * x + k, :]),
                                            (hi[:, k, :], lo[:, k, :]), x == 0 and k == 0, x == 1 and k == 3)
                    last.then_inc(sem("pair_used"), 1)
                if c == 0 and kind in ("gate", "up") and not peeled:
                    t = ("gate", "up").index(kind)
                    pe.wait_ge(sem("Y_copied"), it + 1)
                    pe.wait_ge(sem("scattered"), NT * it + NT + t)
                    scatter(t)
                if kind == "up" and c == NFC - 1:
                    pe.wait_ge(sem("onehot_ready"), it + 2)
                    pe.wait_ge(sem("scattered"), NT * it + 2 * NT)
                    gather()
                    pe.wait_ge(sem("gated_ready"), it + 1)
                    for t in range(NT):
                        last = pe_.transpose(bank[3][:, t * P:t * P + P], gated[:, t, :], ident)
                    last.then_inc(sem("gatedT_done"), 1)
                if (kind == "gate" and c) or (kind == "up" and c == NFC - 1):
                    cc = c if kind == "gate" else NFC
                    pe.wait_ge(sem("H_done"), NFC * it + NFC + cc)
                    if cc == NFC:
                        pe.wait_ge(sem("ht_lo"), NFC * it + cc - 1)
                    for j in range(4):
                        last = pe_.transpose(bank[2][:, j * CAP:j * CAP + CAP], MO["H"][:, j * P:j * P + P], ident)
                    last.then_inc(sem("HT_done"), 1)

        pe.sem_inc(sem("scatter_done"), NT)
        run_item(0, peeled=True)
        n_items = pe.value_load(work_list[0:1, ITEMS:ITEMS + 1], min_val=NE, max_val=ITEMS)
        with pe.Fori(1, n_items) as it:
            run_item(it)
        pe.wait_ge(sem("Y_copied"), n_items + 1)
        for t in range(NT):
            pe.wait_ge(sem("scattered"), NT * n_items + NT + t)
            scatter(t)

    ctx.close()


def kernel(**inputs):
    import numpy as _np
    import concourse.bacc as _bacc
    from concourse import mybir as _mybir
    from concourse.bass_utils import run_bass_kernel_spmd as _run

    nc = _bacc.Bacc("TRN2", target_bir_lowering=False, num_devices=1)
    arrays, aps = {}, {}
    for name in inputs:
        x = _np.ascontiguousarray(inputs[name])
        arrays[f"in_{name}"] = x
        aps[name] = nc.dram_tensor(f"in_{name}", x.shape, _mybir.dt.from_np(x.dtype), kind="ExternalInput").ap()
    packed = _np.ascontiguousarray(_np.concatenate(list(constants().values()), axis=1))
    arrays["shape_constants"] = packed
    con = nc.dram_tensor("shape_constants", packed.shape, _mybir.dt.float32, kind="ExternalInput").ap()
    out = nc.dram_tensor("out_0_dram", (1, T, D), _mybir.dt.float32, kind="ExternalOutput").ap()
    trunk(nc, aps, con, out)
    r = _run(nc, [arrays], core_ids=[0])
    return r.results[0]["out_0_dram"]
```
